# Optimizing a Trainium2 kernel written in Bass

```python
import math
import jax, jax.numpy as jnp
from jax import lax
import numpy as np

D_MODEL = 1024
BATCH = 1
SEQ = 512
DEPTH = 2

RMS_EPS = 1e-6
D_FF = -(-8 * D_MODEL // (3 * 256)) * 256
GDN_HEADS = 4
GDN_HEAD_DIM = 128
GDN_WIDTH = GDN_HEADS * GDN_HEAD_DIM
GDN_CONV = 4
GDN_CHUNK = 64
NSA_HEADS = 8
NSA_HEAD_DIM = 64
NSA_GROUPS = 2
NSA_HPG = NSA_HEADS // NSA_GROUPS
NSA_WIDTH = NSA_HEADS * NSA_HEAD_DIM
NSA_KV_WIDTH = NSA_GROUPS * NSA_HEAD_DIM
CMP_LEN = 32
CMP_STRIDE = 16
CMP_HIDDEN = 256
SLC_LEN = 64
N_SELECT = 8
WINDOW = 512
NSA_QBLOCK = SLC_LEN
FORCED_SCORE = 1e6
NEG_INF = -1e30
D_MIX = GDN_WIDTH + NSA_WIDTH
IN_SPLITS = (GDN_WIDTH,) * 4 + (GDN_HEADS,) * 2 + (NSA_WIDTH,) + (NSA_KV_WIDTH,) * 6 + (3 * NSA_HEADS,)
IN_COLS = sum(IN_SPLITS)
NUM_BUCKETS = 32
REL_MAX_DIST = 128
RWKV_HEAD = 64
RWKV_HEADS = D_MODEL // RWKV_HEAD
DECAY_LORA = 64
AAA_LORA = 64
GATE_LORA = 160
RWKV_GN_EPS = 64e-5

kernel_name = 'hybrid_gdn_nsa_rwkv7_trunk'

def rmsnorm(x, w):
    xf = x.astype(jnp.float32)
    return xf * lax.rsqrt(jnp.mean(xf * xf, axis=-1, keepdims=True) + RMS_EPS) * w.astype(jnp.float32)

def l2norm(x, eps=1e-6):
    xf = x.astype(jnp.float32)
    return xf * lax.rsqrt(jnp.sum(xf * xf, axis=-1, keepdims=True) + eps)

def masked_softmax(s, mask):
    s = jnp.where(mask, s.astype(jnp.float32), NEG_INF)
    p = jnp.where(mask, jnp.exp(s - jnp.max(s, axis=-1, keepdims=True)), 0.0)
    return p / jnp.maximum(jnp.sum(p, axis=-1, keepdims=True), 1e-30)

def causal_depthwise_conv(x, w):
    k = w.shape[0]
    return lax.conv_general_dilated(x, w[:, None, :].astype(x.dtype), (1,), [(k - 1, 0)],
                                    dimension_numbers=('NWC', 'WIO', 'NWC'),
                                    feature_group_count=x.shape[-1])

def swiglu(h, w_gate, w_up, w_down):
    return (jax.nn.silu(h @ w_gate) * (h @ w_up)) @ w_down

def rel_bucket(dist):
    n = jnp.maximum(dist, 0)
    exact = NUM_BUCKETS // 2
    nf = jnp.maximum(n, 1).astype(jnp.float32)
    large = exact + (jnp.log(nf / exact) / math.log(REL_MAX_DIST / exact) * (NUM_BUCKETS - exact)).astype(jnp.int32)
    return jnp.where(n < exact, n, jnp.minimum(large, NUM_BUCKETS - 1))

def chunk_gated_delta_rule(q, k, v, g, beta):
    B, S, H, DK = q.shape
    DV = v.shape[-1]
    C = GDN_CHUNK
    NCH = S // C

    def chunks(t):
        t = t.astype(jnp.float32).reshape((B, NCH, C, H) + t.shape[3:])
        return jnp.moveaxis(t, 3, 1)

    qc = chunks(q) * DK ** -0.5
    kc, vc, bc = chunks(k), chunks(v), chunks(beta)
    gc = jnp.cumsum(chunks(g), axis=-1)
    idx = jnp.arange(C)
    causal = idx[:, None] >= idx[None, :]
    decay = jnp.exp(jnp.where(causal, gc[..., :, None] - gc[..., None, :], -jnp.inf))
    kb = kc * bc[..., None]
    strict = jnp.where(idx[:, None] > idx[None, :], jnp.einsum('bhncd,bhnsd->bhncs', kb, kc) * decay, 0.0)
    tmat = strict + jnp.eye(C, dtype=jnp.float32)
    u = lax.linalg.triangular_solve(tmat, vc * bc[..., None], left_side=True, lower=True, unit_diagonal=True)
    w = lax.linalg.triangular_solve(tmat, kb * jnp.exp(gc)[..., None], left_side=True, lower=True, unit_diagonal=True)
    qk = jnp.einsum('bhncd,bhnsd->bhncs', qc, kc) * decay

    def step(state, inp):
        q_i, k_i, u_i, w_i, qk_i, g_i = inp
        v_new = u_i - jnp.einsum('bhcd,bhde->bhce', w_i, state)
        o = (jnp.einsum('bhcd,bhde->bhce', q_i * jnp.exp(g_i)[..., None], state)
             + jnp.einsum('bhcs,bhse->bhce', qk_i, v_new))
        g_last = g_i[..., -1:]
        state = (state * jnp.exp(g_last)[..., None]
                 + jnp.einsum('bhcd,bhce->bhde', k_i * jnp.exp(g_last - g_i)[..., None], v_new))
        return state, o

    xs = tuple(jnp.moveaxis(t, 2, 0) for t in (qc, kc, u, w, qk, gc))
    _, o = lax.scan(step, jnp.zeros((B, H, DK, DV), jnp.float32), xs)
    return o.transpose(1, 0, 3, 2, 4).reshape(B, S, H, DV)

def gated_deltanet(q, k, v, z, b, a, conv_w, a_log, dt_bias, norm_w):
    B, S, _ = q.shape
    qkv = jax.nn.silu(causal_depthwise_conv(jnp.concatenate([q, k, v], axis=-1), conv_w))
    q, k, v = jnp.split(qkv, 3, axis=-1)
    q = l2norm(q.reshape(B, S, GDN_HEADS, GDN_HEAD_DIM))
    k = l2norm(k.reshape(B, S, GDN_HEADS, GDN_HEAD_DIM))
    v = v.reshape(B, S, GDN_HEADS, GDN_HEAD_DIM).astype(jnp.float32)
    beta = jax.nn.sigmoid(b.astype(jnp.float32))
    g = -jnp.exp(a_log.astype(jnp.float32)) * jax.nn.softplus(a.astype(jnp.float32) + dt_bias.astype(jnp.float32))
    o = chunk_gated_delta_rule(q, k, v, g, beta)
    o = rmsnorm(o, norm_w) * jax.nn.silu(z.reshape(B, S, GDN_HEADS, GDN_HEAD_DIM).astype(jnp.float32))
    return o.reshape(B, S, GDN_WIDTH)

def compress_blocks(x, pe, w1, w2):
    B, S, G, DH = x.shape
    r = CMP_LEN // CMP_STRIDE
    ch = x.astype(jnp.float32).reshape(B, S // CMP_STRIDE, CMP_STRIDE, G, DH)
    nc = S // CMP_STRIDE - r + 1
    blocks = jnp.concatenate([ch[:, i:i + nc] for i in range(r)], axis=2)
    blocks = blocks + pe[None, None, :, None, :]
    flat = blocks.transpose(0, 1, 3, 2, 4).reshape(B, nc, G, CMP_LEN * DH)
    return jax.nn.silu(flat @ w1) @ w2

def nsa_attention(q, k_cmp, v_cmp, k_slc, v_slc, k_win, v_win, gate_logits,
                  cmpk_pe, cmpk_w1, cmpk_w2, cmpv_pe, cmpv_w1, cmpv_w2, rel_bias):
    B, S = q.shape[:2]
    G, HPG, DH, QB = NSA_GROUPS, NSA_HPG, NSA_HEAD_DIM, NSA_QBLOCK
    q = (q.astype(jnp.float32) * DH ** -0.5).reshape(B, S, G, HPG, DH)
    gates = jax.nn.sigmoid(gate_logits.astype(jnp.float32)).reshape(B, S, G, HPG, 3)
    kc = compress_blocks(k_cmp, cmpk_pe, cmpk_w1, cmpk_w2)
    vc = compress_blocks(v_cmp, cmpv_pe, cmpv_w1, cmpv_w2)
    NC = kc.shape[1]
    NS = S // SLC_LEN
    n_sel = min(N_SELECT, NS)
    k_blk = k_slc.astype(jnp.float32).reshape(B, NS, SLC_LEN, G, DH).transpose(0, 3, 1, 2, 4)
    v_blk = v_slc.astype(jnp.float32).reshape(B, NS, SLC_LEN, G, DH).transpose(0, 3, 1, 2, 4)
    k_wpad = jnp.pad(k_win.astype(jnp.float32), ((0, 0), (WINDOW, 0), (0, 0), (0, 0)))
    v_wpad = jnp.pad(v_win.astype(jnp.float32), ((0, 0), (WINDOW, 0), (0, 0), (0, 0)))
    cmp_start = jnp.arange(NC) * CMP_STRIDE
    cmp_end = cmp_start + CMP_LEN - 1
    slc_j = jnp.arange(NS)
    overlap = ((cmp_start[:, None] < (slc_j[None, :] + 1) * SLC_LEN)
               & (cmp_end[:, None] >= slc_j[None, :] * SLC_LEN)).astype(jnp.float32)
    table = rel_bias.astype(jnp.float32)
    table_grouped = table.reshape(NUM_BUCKETS, G, HPG).transpose(1, 0, 2).reshape(G * NUM_BUCKETS, HPG)
    bi = jnp.arange(B)[:, None, None, None]
    gi = jnp.arange(G)[None, None, :, None]

    def head_bias(dist):
        return table[rel_bucket(dist)].reshape(dist.shape + (G, HPG)).transpose(0, 2, 3, 1)

    def block(n):
        t0 = n * QB
        t = t0 + jnp.arange(QB)
        qb = lax.dynamic_slice_in_dim(q, t0, QB, axis=1)
        gb = lax.dynamic_slice_in_dim(gates, t0, QB, axis=1)
        dist_c = t[:, None] - cmp_end[None, :]
        s_c = jnp.einsum('btghd,bcgd->btghc', qb, kc) + head_bias(dist_c)[None]
        p_c = masked_softmax(s_c, (dist_c >= 0)[None, :, None, None, :])
        o_c = jnp.einsum('btghc,bcgd->btghd', p_c, vc)
        imp = jnp.einsum('btghc,cs->btgs', p_c, overlap)
        forced = (slc_j == 0) | (slc_j == n) | (slc_j == n - 1)
        imp = jnp.where(slc_j > n, -1.0, jnp.where(forced, FORCED_SCORE, imp))
        _, idx = lax.top_k(imp, n_sel)
        k_sel = k_blk[bi, gi, idx]
        v_sel = v_blk[bi, gi, idx]
        pos = idx[..., None] * SLC_LEN + jnp.arange(SLC_LEN)
        dist_s = t[None, :, None, None, None] - pos
        bias_s = table_grouped[gi[..., None] * NUM_BUCKETS + rel_bucket(dist_s)]
        s_s = jnp.einsum('btghd,btgnld->btghnl', qb, k_sel) + bias_s.transpose(0, 1, 2, 5, 3, 4)
        mask_s = (dist_s >= 0)[:, :, :, None].reshape(B, QB, G, 1, n_sel * SLC_LEN)
        p_s = masked_softmax(s_s.reshape(B, QB, G, HPG, n_sel * SLC_LEN), mask_s).reshape(s_s.shape)
        o_s = jnp.einsum('btghnl,btgnld->btghd', p_s, v_sel)
        k_w = lax.dynamic_slice_in_dim(k_wpad, t0, WINDOW + QB, axis=1)
        v_w = lax.dynamic_slice_in_dim(v_wpad, t0, WINDOW + QB, axis=1)
        kpos = t0 - WINDOW + jnp.arange(WINDOW + QB)
        dist_w = t[:, None] - kpos[None, :]
        mask_w = (dist_w >= 0) & (dist_w < WINDOW) & (kpos >= 0)[None, :]
        s_w = jnp.einsum('btghd,bkgd->btghk', qb, k_w) + head_bias(dist_w)[None]
        p_w = masked_softmax(s_w, mask_w[None, :, None, None, :])
        o_w = jnp.einsum('btghk,bkgd->btghd', p_w, v_w)
        return gb[..., 0:1] * o_c + gb[..., 1:2] * o_s + gb[..., 2:3] * o_w

    out = lax.map(block, jnp.arange(S // QB))
    return out.transpose(1, 0, 2, 3, 4, 5).reshape(B, S, NSA_WIDTH)

def delta_nsa_mixer(h, w_in, conv_w, a_log, dt_bias, gdn_norm, cmpk_pe, cmpk_w1, cmpk_w2,
                    cmpv_pe, cmpv_w1, cmpv_w2, w_out, rel_bias):
    B, S, _ = h.shape
    cuts = [int(c) for c in np.cumsum(IN_SPLITS)[:-1]]
    (gq, gk, gv, gz, gb, ga, nq, nkc, nvc, nks, nvs, nkw, nvw, ngate) = jnp.split(h @ w_in, cuts, axis=-1)
    o_gdn = gated_deltanet(gq, gk, gv, gz, gb, ga, conv_w, a_log, dt_bias, gdn_norm)
    kv = lambda t: t.reshape(B, S, NSA_GROUPS, NSA_HEAD_DIM)
    o_nsa = nsa_attention(nq.reshape(B, S, NSA_HEADS, NSA_HEAD_DIM), kv(nkc), kv(nvc), kv(nks), kv(nvs),
                          kv(nkw), kv(nvw), ngate.reshape(B, S, NSA_HEADS, 3),
                          cmpk_pe, cmpk_w1, cmpk_w2, cmpv_pe, cmpv_w1, cmpv_w2, rel_bias)
    return jnp.concatenate([o_gdn, o_nsa], axis=-1) @ w_out

def wkv7_scan(r, w, k, v, a, b):
    B, S, H, N = r.shape

    def step(state, inp):
        r_t, w_t, k_t, v_t, a_t, b_t = inp
        sa = jnp.einsum('bhij,bhj->bhi', state, a_t)
        state = state * w_t[:, :, None, :] + sa[..., None] * b_t[:, :, None, :] + v_t[..., None] * k_t[:, :, None, :]
        return state, jnp.einsum('bhij,bhj->bhi', state, r_t)

    xs = tuple(jnp.moveaxis(t, 1, 0) for t in (r, w, k, v, a, b))
    _, y = lax.scan(step, jnp.zeros((B, H, N, N), jnp.float32), xs)
    return jnp.moveaxis(y, 0, 1)

def rwkv7_time_mix(h, mu, w_r, w_k, w_v, w_o, w0, w1, w2, a0, a1, a2, g1, g2, k_k, k_a, r_k, lnx_w, lnx_b):
    B, S, D = h.shape
    heads = lambda t: t.reshape(B, S, RWKV_HEADS, RWKV_HEAD).astype(jnp.float32)
    xx = jnp.pad(h, ((0, 0), (1, 0), (0, 0)))[:, :-1] - h
    xr, xw, xk, xv, xa, xg = (h + xx * mu[j] for j in range(6))
    r = xr @ w_r
    w = -jax.nn.softplus(-(w0 + jnp.tanh(xw @ w1) @ w2)) - 0.5
    k = xk @ w_k
    v = xv @ w_v
    a = jax.nn.sigmoid(a0 + (xa @ a1) @ a2)
    g = jax.nn.sigmoid(xg @ g1) @ g2
    kk = l2norm(heads(k * k_k), eps=1e-12)
    k = k * (1.0 + (a - 1.0) * k_a)
    rh, kh, vh = heads(r), heads(k), heads(v)
    y = wkv7_scan(rh, heads(jnp.exp(-jnp.exp(w))), kh, vh, -kk, kk * heads(a))
    mean = jnp.mean(y, axis=-1, keepdims=True)
    var = jnp.mean(jnp.square(y - mean), axis=-1, keepdims=True)
    y = ((y - mean) * lax.rsqrt(var + RWKV_GN_EPS)).reshape(B, S, D) * lnx_w + lnx_b
    y = y + (jnp.sum(rh * kh * r_k, axis=-1, keepdims=True) * vh).reshape(B, S, D)
    return (y * g) @ w_o

def setup_inputs(seed: int = 0) -> dict:
    key = jax.random.key(seed)
    subkeys = jax.random.split(key, 64)
    counter = iter(range(64))
    nk = lambda: subkeys[next(counter)]
    nrm = lambda shape, scale: scale * jax.random.normal(nk(), shape, jnp.float32)
    gain = lambda shape: 1.0 + nrm(shape, 0.02)
    ne, no = (DEPTH + 1) // 2, DEPTH // 2
    d = D_MODEL
    x = nrm((BATCH, SEQ, d), 1.0)
    rel_bias = nrm((NUM_BUCKETS, NSA_HEADS), 0.5)
    final_norm = gain((d,))
    e_attn_norm = gain((ne, d))
    e_w_in = nrm((ne, d, IN_COLS), d ** -0.5)
    e_conv_w = nrm((ne, GDN_CONV, 3 * GDN_WIDTH), GDN_CONV ** -0.5)
    e_a_log = jnp.log(jax.random.uniform(nk(), (ne, GDN_HEADS), jnp.float32, 1.0, 16.0))
    dt = jnp.exp(jax.random.uniform(nk(), (ne, GDN_HEADS), jnp.float32, math.log(1e-3), math.log(1e-1)))
    e_dt_bias = dt + jnp.log(-jnp.expm1(-dt))
    e_gdn_norm = gain((ne, GDN_HEAD_DIM))
    e_cmpk_pe = nrm((ne, CMP_LEN, NSA_HEAD_DIM), 0.02)
    e_cmpk_w1 = nrm((ne, CMP_LEN * NSA_HEAD_DIM, CMP_HIDDEN), (CMP_LEN * NSA_HEAD_DIM) ** -0.5)
    e_cmpk_w2 = nrm((ne, CMP_HIDDEN, NSA_HEAD_DIM), CMP_HIDDEN ** -0.5)
    e_cmpv_pe = nrm((ne, CMP_LEN, NSA_HEAD_DIM), 0.02)
    e_cmpv_w1 = nrm((ne, CMP_LEN * NSA_HEAD_DIM, CMP_HIDDEN), (CMP_LEN * NSA_HEAD_DIM) ** -0.5)
    e_cmpv_w2 = nrm((ne, CMP_HIDDEN, NSA_HEAD_DIM), CMP_HIDDEN ** -0.5)
    e_w_out = nrm((ne, D_MIX, d), D_MIX ** -0.5)
    e_ffn_norm = gain((ne, d))
    e_ffn_gate = nrm((ne, d, D_FF), d ** -0.5)
    e_ffn_up = nrm((ne, d, D_FF), d ** -0.5)
    e_ffn_down = nrm((ne, D_FF, d), D_FF ** -0.5)
    o_attn_norm = gain((no, d))
    o_mu = jax.random.uniform(nk(), (no, 6, d), jnp.float32)
    o_w_r = nrm((no, d, d), d ** -0.5)
    o_w_k = nrm((no, d, d), d ** -0.5)
    o_w_v = nrm((no, d, d), d ** -0.5)
    o_w_o = nrm((no, d, d), d ** -0.5)
    o_w0 = jax.random.uniform(nk(), (no, d), jnp.float32, -6.0, -1.0)
    o_w1 = nrm((no, d, DECAY_LORA), d ** -0.5)
    o_w2 = nrm((no, DECAY_LORA, d), 0.1 * DECAY_LORA ** -0.5)
    o_a0 = nrm((no, d), 0.1)
    o_a1 = nrm((no, d, AAA_LORA), d ** -0.5)
    o_a2 = nrm((no, AAA_LORA, d), 0.5 * AAA_LORA ** -0.5)
    o_g1 = nrm((no, d, GATE_LORA), d ** -0.5)
    o_g2 = nrm((no, GATE_LORA, d), GATE_LORA ** -0.5)
    o_k_k = 0.85 + nrm((no, d), 0.02)
    o_k_a = gain((no, d))
    o_r_k = nrm((no, RWKV_HEADS, RWKV_HEAD), 0.1)
    o_lnx_w = gain((no, d))
    o_lnx_b = nrm((no, d), 0.01)
    o_ffn_norm = gain((no, d))
    o_ffn_gate = nrm((no, d, D_FF), d ** -0.5)
    o_ffn_up = nrm((no, d, D_FF), d ** -0.5)
    o_ffn_down = nrm((no, D_FF, d), D_FF ** -0.5)
    return {'x': x, 'rel_bias': rel_bias, 'final_norm': final_norm,
            'e_attn_norm': e_attn_norm, 'e_w_in': e_w_in, 'e_conv_w': e_conv_w, 'e_a_log': e_a_log,
            'e_dt_bias': e_dt_bias, 'e_gdn_norm': e_gdn_norm,
            'e_cmpk_pe': e_cmpk_pe, 'e_cmpk_w1': e_cmpk_w1, 'e_cmpk_w2': e_cmpk_w2,
            'e_cmpv_pe': e_cmpv_pe, 'e_cmpv_w1': e_cmpv_w1, 'e_cmpv_w2': e_cmpv_w2,
            'e_w_out': e_w_out, 'e_ffn_norm': e_ffn_norm, 'e_ffn_gate': e_ffn_gate,
            'e_ffn_up': e_ffn_up, 'e_ffn_down': e_ffn_down,
            'o_attn_norm': o_attn_norm, 'o_mu': o_mu, 'o_w_r': o_w_r, 'o_w_k': o_w_k, 'o_w_v': o_w_v,
            'o_w_o': o_w_o, 'o_w0': o_w0, 'o_w1': o_w1, 'o_w2': o_w2, 'o_a0': o_a0, 'o_a1': o_a1,
            'o_a2': o_a2, 'o_g1': o_g1, 'o_g2': o_g2, 'o_k_k': o_k_k, 'o_k_a': o_k_a, 'o_r_k': o_r_k,
            'o_lnx_w': o_lnx_w, 'o_lnx_b': o_lnx_b, 'o_ffn_norm': o_ffn_norm, 'o_ffn_gate': o_ffn_gate,
            'o_ffn_up': o_ffn_up, 'o_ffn_down': o_ffn_down}

def reference(x, rel_bias, final_norm,
              e_attn_norm, e_w_in, e_conv_w, e_a_log, e_dt_bias, e_gdn_norm,
              e_cmpk_pe, e_cmpk_w1, e_cmpk_w2, e_cmpv_pe, e_cmpv_w1, e_cmpv_w2,
              e_w_out, e_ffn_norm, e_ffn_gate, e_ffn_up, e_ffn_down,
              o_attn_norm, o_mu, o_w_r, o_w_k, o_w_v, o_w_o, o_w0, o_w1, o_w2, o_a0, o_a1, o_a2,
              o_g1, o_g2, o_k_k, o_k_a, o_r_k, o_lnx_w, o_lnx_b,
              o_ffn_norm, o_ffn_gate, o_ffn_up, o_ffn_down):
    for layer in range(DEPTH):
        i = layer // 2
        if layer % 2 == 0:
            h = rmsnorm(x, e_attn_norm[i])
            x = x + delta_nsa_mixer(h, e_w_in[i], e_conv_w[i], e_a_log[i], e_dt_bias[i], e_gdn_norm[i],
                                    e_cmpk_pe[i], e_cmpk_w1[i], e_cmpk_w2[i],
                                    e_cmpv_pe[i], e_cmpv_w1[i], e_cmpv_w2[i], e_w_out[i], rel_bias)
            x = x + swiglu(rmsnorm(x, e_ffn_norm[i]), e_ffn_gate[i], e_ffn_up[i], e_ffn_down[i])
        else:
            h = rmsnorm(x, o_attn_norm[i])
            x = x + rwkv7_time_mix(h, o_mu[i], o_w_r[i], o_w_k[i], o_w_v[i], o_w_o[i], o_w0[i], o_w1[i],
                                   o_w2[i], o_a0[i], o_a1[i], o_a2[i], o_g1[i], o_g2[i], o_k_k[i],
                                   o_k_a[i], o_r_k[i], o_lnx_w[i], o_lnx_b[i])
            x = x + swiglu(rmsnorm(x, o_ffn_norm[i]), o_ffn_gate[i], o_ffn_up[i], o_ffn_down[i])
    return rmsnorm(x, final_norm)


_drawn_inputs = setup_inputs


def setup_inputs(seed=0):
    import zlib

    import numpy as np

    out = dict(_drawn_inputs(seed))
    spreads = {}
    factors = {'final_norm': 21.557,
     'e_attn_norm': 3.153,
     'e_gdn_norm': 5.049,
     'e_cmpk_pe': 25.37,
     'e_cmpv_pe': 32.635,
     'e_ffn_norm': 3.255,
     'o_attn_norm': 3.654,
     'o_w1': 40.516,
     'o_w2': 41.853,
     'o_a0': 3.337,
     'o_k_k': 200.0,
     'o_k_a': 6.364,
     'o_lnx_w': 158.087,
     'o_lnx_b': 200.0,
     'o_ffn_norm': 24.861}
    for name, (base, spread) in spreads.items():
        noise = np.random.default_rng([zlib.crc32(name.encode()), seed]).standard_normal(out[name].shape)
        drawn = base * np.exp(spread * noise) if base else spread * noise
        out[name] = __import__('jax').numpy.asarray(drawn.astype(out[name].dtype))
    for name, factor in factors.items():
        out[name] = (out[name] * factor).astype(out[name].dtype)
    return out
```

```python
import math
from contextlib import ExitStack

import concourse.bass as bass
from concourse import mybir

F32 = mybir.dt.float32
ALU = mybir.AluOpType
ACT = mybir.ActivationFunctionType

P = 128
SEQ = 512
D_MODEL = 1024
DT = D_MODEL // P
D_FF = 2816
FT = D_FF // P
EPS = 1e-6
GH, GD = 4, 128
CHUNK = 128
NCHUNK = SEQ // CHUNK
NH, ND = 8, 64
CMP_LEN, CMP_STRIDE = 32, 16
NCMP = SEQ // CMP_STRIDE - CMP_LEN // CMP_STRIDE + 1
RD = 64
EPITCH = SEQ // RD * (RD + 1)
UNIT = DT * P
IN_UNITS = 26
PITCH = SEQ + 4
HD = 4
BIAS_LEN = 640
NEG = -1e30
DECAY = math.exp(-0.5)

COLS, n = {}, 0
for _name, _w in (("ident", P), ("flip", P), ("le", P), ("gt", P), ("ones", P), ("blk", P),
                  ("lvl", 7 * P), ("lvl64", 6 * RD), ("le64", RD), ("lt64", RD), ("gt64", RD),
                  ("id64", RD), ("eps", 4)):
    COLS[_name] = (n, _w)
    n += _w
NCONST = n
VCOLS, n = {}, 0
for _name, _w in (("n0", 8), ("n1", 8), ("n2", 8), ("n3", 8), ("n4", 8), ("mu", 48), ("w0", 8),
                  ("a0", 8), ("k_k", 8), ("k_a", 8), ("r_k", 8), ("lnw", 8), ("lnb", 8),
                  ("conv", 48), ("gnorm", 1), ("alog", 4), ("dtb", 4), ("wsmall", 256),
                  ("cw2", 256), ("pe", 32), ("tbl", 8)):
    VCOLS[_name] = (n, _w)
    n += _w
NVEC = n
del n


class Turns:

    def __init__(self, n):
        self.n, self.pos, self.used = n, 0, [0] * n

    def at(self, j, it=0, per=0):
        s = (self.pos + j) % self.n
        return s, self.used[s] + it * (per // self.n) + j // self.n

    def advance(self, m):
        for j in range(m):
            self.used[(self.pos + j) % self.n] += 1
        self.pos = (self.pos + m) % self.n


def build(nc, xT, cpack, vpack, onehot, wk8, wdn, scratch, g_spill, outT):
    ctx = ExitStack()
    sems = {}

    carried_on = {
        "z_out": ("qt_done", 28), "xt_sub": ("x_step", 52), "x_sub": ("qk_done", 4), "xtm": ("vtok2_mm", 4),
        "m_mm": ("kk_mm", 4), "k_mm": ("qk_mm", 4), "rb_mm": ("ktok_mm", 4), "bt_mm": ("g_sum_mm", 1),
        "kt_mm": ("ks_mm", 4), "vt_mm": ("vnew_mm", 4), "g_mm": ("o_mm", 4), "q_mm": ("qt_mm", 28),
        "xmm": ("xx_mm", 28), "u_mm": ("st_mm", 4), "z_mm": ("decay_mm", 12), "y_mm": ("bias_mm", 8),
        "mean_mm": ("otok_turned", 4), "bonus_mm": ("score_mm", 96), "dev_mm": ("turned", 96), "ksum_mm": ("qk_sum", 8),
        "wa_mm": ("o_sum", 4), "lora_mm": ("vtok_mm", 2), "bda": ("decay_row", 4), "bdb": ("decay_low", 4),
        "tok_out": ("decay_up", 4), "g_out": ("ktok_done", 4), "bdq": ("vnew_done", 4), "bdxt": ("turn_copied", 96),
        "bdu": ("exp_done", 96), "bdz": ("hid_done", 4), "y_out": ("blocks_done", 8),
    }

    def seen(name):
        return carried_on[name][1]

    def sig(name):
        name = carried_on.get(name, (name,))[0]
        if name not in sems:
            sems[name] = ctx.enter_context(nc.semaphore(name))
        return sems[name]

    def sb(name, cols):
        return ctx.enter_context(nc.sbuf_tensor(name, [P, cols], F32))

    with ctx:
        x = sb("x", DT * SEQ)[:, :].rearrange("p (m t) -> p m t", m=DT)
        h_t = sb("h", DT * PITCH)
        h = h_t[:, :].rearrange("p (m t) -> p m t", m=DT)
        ht = h[:, :, HD:HD + SEQ]
        wring = sb("wring", 4 * UNIT)[:, :].rearrange("p (s k) -> p s k", s=4)
        dring_t = sb("dring", 2 * D_FF)
        dring = dring_t[:, :].rearrange("p (s k) -> p s k", s=2)
        con = sb("con", NCONST)
        vec = sb("vec", NVEC)
        norm_t = sb("norm_t", 2 * SEQ)[:, :].rearrange("p (s t) -> p s t", s=2)
        ARENA = 31000
        arena = sb("arena", ARENA)
        bank = [ctx.enter_context(nc.psum_tensor(f"bank{i}", [P, 512], F32)) for i in range(8)]

        def c(name):
            o, w = COLS[name]
            return con[:, o:o + w]

        def v(name):
            o, w = VCOLS[name]
            return vec[:, o:o + w]

        class Carve:
            def __init__(self, base, t=arena, top=ARENA):
                self.at, self.t, self.top = base, t, top

            def __call__(self, cols, shape=None):
                a = self.t[:, self.at:self.at + cols]
                self.at += cols
                assert self.at <= self.top, self.at
                return a if shape is None else a.rearrange("p (a b) -> p a b", a=shape)

        L0 = Carve(0)
        proj = L0(IN_UNITS * SEQ, IN_UNITS)
        bias = L0(NH * SEQ, NH)
        otok = L0(4 * NH * ND, 4)
        tok = L0(P, 4)
        gates_flat = L0(96)
        gates = gates_flat.rearrange("p (q n) -> p q n", q=4)
        g_col, beta, nbeg, gtmp, gaux = (L0(16) for _ in range(5))
        eg, ea = L0(32), L0(4)
        mark = L0.at
        N = Carve(mark)
        kst = [N(2 * SEQ, 2) for _ in range(2)]
        hid = N(4 * 62, 4)
        pebias = N(4)
        kcT = N(32)
        vcT = N(P)
        vtok = N(2 * SEQ, 8)
        q_st = N(SEQ)
        probs = [N(SEQ) for _ in range(2)]
        probsT = [N(SEQ) for _ in range(2)]
        nmx = [N(2) for _ in range(2)]
        sums, rg = N(24), N(24)
        oacc = [N(SEQ) for _ in range(3)]
        conv = [N(SEQ) for _ in range(2)]
        bias_st = N(2 * SEQ, 2)
        B = Carve(mark + 4 * SEQ)
        oh = B(BIAS_LEN)
        brow = B(BIAS_LEN)
        shifted = B(NH * SEQ, NH)
        G = Carve(mark)
        (k_st, qst, v_st, gbc, leg, gtg, egr, dlow, dup, mlow, qk, xi, xit, qt_, ktok, vb, rr, vn,
         st) = (G(SEQ, GH) for _ in range(19))
        gtg_flat, leg_flat = (a.rearrange("p a b -> p (a b)") for a in (gtg, leg))
        rn0 = bias
        hidden = Carve(0)(FT * SEQ, FT)
        sil = Carve(FT * SEQ)(2 * SEQ, 2)
        R = Carve(0)
        g_a = R(DT * SEQ, DT)
        e_flat = R(DT * EPITCH)
        e_a = e_flat.rearrange("p (m t) -> p m t", m=DT)
        e_c = e_flat.rearrange("p (m c t) -> p m c t", m=DT, c=SEQ // RD)
        a_a, v_a, r_a, k_a_ = (R(DT * SEQ, DT) for _ in range(4))
        mixb = R(DT * SEQ, DT)
        left = R.at
        L = Carve(left)
        padmask, hid_g1, hid_g2, hid_wa = L(EPITCH), L(SEQ), L(SEQ), L(SEQ)
        D = Carve(0, dring_t, 2 * D_FF)
        mixa = D(DT * SEQ, DT)
        kk_a = mixa
        ei_flat = dring_t[:, 0:DT * EPITCH]
        ei_a = ei_flat.rearrange("p (m t) -> p m t", m=DT)
        ei_c = ei_flat.rearrange("p (m c t) -> p m c t", m=DT, c=SEQ // RD)
        G_ = Carve(0)
        bdU, bdX, bdQ = (G_(UNIT, DT) for _ in range(3))
        ry_c = G_(SEQ, DT)
        E_ = Carve(DT * SEQ)
        bdA, bdB, bdK, bdM = (E_(UNIT, DT) for _ in range(4))
        M_ = Carve(left - DT * SEQ)
        bdAK, bdBt, bdKt, bdVt = (M_(UNIT, DT) for _ in range(4))
        H_ = Carve(0, h_t, DT * PITCH)
        bdV, bdZ = (H_(UNIT, DT) for _ in range(2))
        rb_c, rk_c, vt_c, x_c = (H_(SEQ, DT) for _ in range(4))
        xt_c, q_c, u_c = (D(SEQ, DT) for _ in range(3))
        C_ = Carve(left)
        ar_c = C_(UNIT, DT)
        z_c, g_c, p_c = C_(SEQ, DT), C_(SEQ, DT), C_(64, DT)
        b_c = norm_t[:, 0, :].rearrange("p (m t) -> p m t", m=DT)
        bdXT = bdQ
        rsd = e_flat[:, 0:DT * SEQ].rearrange("p (m t) -> p m t", m=DT)

        def eps(i):
            o = COLS["eps"][0] + i
            return con[:, o:o + 1]

        def width(u):
            qt = u // 3 % 4
            return P * (qt + 1) if u % 3 < 2 else P // CMP_STRIDE * qt + 7

        PB = (0, 1, 6, 7)
        rings = {e: (Turns(4), Turns(2), Turns(4)) for e in ("sp", "pe", "act", "dve")}

        def k8_product(pe, it, per, j, rhs, gate=None):
            ring, _, banks = rings["pe"]
            s, u = ring.at(j, it, per)
            b, w = banks.at(j, it, per)
            b = PB[b]
            pe.wait_ge(sig(f"w_full{s}"), (u + 1) * 16)
            pe.wait_ge(sig(f"bank_free{b}"), w + 1)
            for k in range(DT):
                if gate:
                    pe.wait_ge(sig(gate[0]), gate[1] + k + 1)
                mm = nc.tensor.matmul(bank[b][:, :], wring[:, s, k * P:(k + 1) * P], rhs[:, k, :],
                                      start=k == 0, stop=k == DT - 1)
            mm.then_inc(sig(f"unit_done{s}"), 1)

        def k8_result(eng, who, it, per, j):
            ring, _, banks = rings[who]
            s, u = ring.at(j, it, per)
            eng.wait_ge(sig(f"unit_done{s}"), u + 1)
            return PB[banks.at(j, it, per)[0]]

        def k8_result_bank(who):
            banks = rings[who][2]
            b = PB[banks.at(0)[0]]
            banks.advance(1)
            return b

        def down_product(pe, it, per, j, gate):
            _, ring, banks = rings["pe"]
            s, u = ring.at(j, it, per)
            b, w = banks.at(j, it, per)
            pe.wait_ge(sig(f"d_full{s}"), (u + 1) * 16)
            pe.wait_ge(sig(f"bank_free{PB[b]}"), w + 1)
            for k in range(FT):
                pe.wait_ge(sig("ff_done"), gate + k + 1)
                mm = nc.tensor.matmul(bank[PB[b]][:, :], dring[:, s, k * P:(k + 1) * P], hidden[:, k, :],
                                      start=k == 0, stop=k == FT - 1)
            mm.then_inc(sig(f"down_done{s}"), 1)

        def skip(who, units, downs=0):
            ring, dr, banks = rings[who]
            ring.advance(units)
            dr.advance(downs)
            banks.advance(units + downs)


        block = ctx.enter_context(nc.Block())

        @block.sync
        def _(sp):
            sp.dma_start(x[:, :, :], xT).then_inc(sig("x_loaded"), 16)
            sp.dma_start(con[:, :], cpack).then_inc(sig("con_loaded"), 16)
            sp.dma_start(vec[:, :], vpack).then_inc(sig("vec_loaded"), 16)
            sp.dma_start(oh[0:33, :], onehot).then_inc(sig("onehot_loaded"), 16)
            ring, downs, _ = rings["sp"]
            loaded = [0, 0]

            def load_units(count):
                first = loaded[0]

                def body(it, per, m):
                    for j in range(m):
                        s, u = ring.at(j, it, per)
                        sp.wait_ge(sig(f"unit_done{s}"), u)
                        sp.dma_start(wring[:, s, :], wk8[bass.ds(it * per + first + j, 1), :, :]
                                     .rearrange("a p k -> p (a k)")).then_inc(sig(f"w_full{s}"), 16)

                if count // 4 > 1:
                    with sp.Fori(0, count // 4) as it:
                        body(it, 4, 4)
                    ring.advance(count // 4 * 4)
                    first += count // 4 * 4
                    count, done = count % 4, count // 4 * 4
                else:
                    done = 0
                body(0, 0, count)
                ring.advance(count)
                loaded[0] = first + count

            for j in range(4):
                sp.dma_start(wring[:, j, :], wk8[j, :, :]).then_inc(sig(f"w_full{j}"), 16)
            ring.advance(4)
            loaded[0] = 4
            def load_down(m):
                s, u = downs.at(0)
                if u:
                    sp.wait_ge(sig(f"down_done{s}"), u)
                sp.dma_start(dring[:, s, :], wdn[m, :, :]).then_inc(sig(f"d_full{s}"), 16)
                downs.advance(1)

            load_units(IN_UNITS + 8 + 8 + 40 - 4)
            load_down(0)
            load_down(1)
            load_units(4 + 4)
            for m in range(2, DT):
                load_down(m)
            load_units(2 + 32 + 40)
            sp.wait_ge(sig("y_read"), 8)
            load_down(8)
            load_down(9)
            load_units(4)
            for m in range(DT + 2, 2 * DT):
                load_down(m)
            for i in range(2):
                sp.wait_ge(sig("h_done"), 32 + 4 * i + 4)
                sp.dma_start(outT[:, 4 * i:4 * i + 4, :], ht[:, 4 * i:4 * i + 4, :]).then_inc(sig("stored"), 16)
            sp.wait_ge(sig("stored"), 32)

        @block.gpsimd
        def _(pool):
            pool.wait_ge(sig("bias_row"), 2)
            pool.dma_start(scratch, brow[0:NH, :]).then_inc(sig("row_stored"), 16)
            pool.wait_ge(sig("row_stored"), 16)
            pool.dma_start(shifted[:, :, :], bass.AP(scratch.tensor, 0, [[1, P], [BIAS_LEN, NH], [1, SEQ]])
                           ).then_inc(sig("shifted_loaded"), 16)
            pool.wait_ge(sig("proj_done"), IN_UNITS - 12)
            pool.wait_ge(sig("bias_done"), NH)
            with pool.Fori(0, 4) as j:
                pool.wait_ge(sig("pair_done"), j + 1)
                nc.gpsimd.tensor_copy(q_st, proj[:, bass.ds(16 + j, 1), :].rearrange("p a t -> p (a t)")
                                      ).then_inc(sig("staged"), 1)
                for s in range(2):
                    nc.gpsimd.tensor_copy(bias_st[:, s, :], bias[:, bass.ds(4 * s + j, 1), :]
                                          .rearrange("p a t -> p (a t)")).then_inc(sig("staged"), 1)

            pool.wait_ge(sig("qk_normed"), 8)
            pool.wait_ge(sig("g_done"), 1)
            def every_head(a):
                return a.unsqueeze(1).broadcast_to([P, GH, P])
            with pool.Fori(0, NCHUNK) as n:
                pool.wait_ge(sig("chunk_done"), n + 1)
                g_n = g_col[:, bass.ds(4 * n, 4)].unsqueeze(2).broadcast_to([P, GH, P])
                for dst, src in ((gbc, c("ones")), (gtg, c("gt")), (leg, c("le"))):
                    nc.gpsimd.tensor_tensor(dst, every_head(src), g_n, ALU.mult).then_inc(sig("g_spread"), 1)
                for dst, a in ((k_st, 4), (qst, 0), (v_st, 8)):
                    nc.gpsimd.tensor_copy(dst, proj[:, a:a + 4, bass.ds(CHUNK * n, CHUNK)]
                                          ).then_inc(sig("chunk_staged"), 1)
                pool.wait_ge(sig("qk_mm"), n + 1)
                pool.wait_ge(sig("decay_row"), n + 1)
                nc.gpsimd.tensor_tensor(qst, qst, egr, ALU.mult).then_inc(sig("q_decayed"), 1)
                pool.wait_ge(sig("ktok_done"), n + 1)
                nc.gpsimd.tensor_tensor(ktok, ktok, eg[:, bass.ds(16 + 4 * n, 4)].unsqueeze(2)
                                        .broadcast_to([P, GH, P]), ALU.mult).then_inc(sig("k_decayed"), 1)

            pool.wait_ge(sig("lora_out"), DT)
            pool.dma_start(g_spill, g_a[:, :, :]).then_inc(sig("g_stored"), 16)
            pool.wait_ge(sig("g_stored"), 16)
            pool.wait_ge(sig("scan_ready"), 1)
            for a in (bdA, bdB, bdK, bdM, bdAK, bdBt, bdKt, bdVt, bdV, bdZ, bdU, bdX, bdQ, z_c):
                nc.gpsimd.memset(a, 0.0).then_inc(sig("bd_zero"), 1)

            def chunk(n):
                for lv in range(5):
                    for g in range(2):
                        pool.wait_ge(sig("x_sub"), seen("x_sub") + n * 10 + 2 * lv + g + 1)
                        pool.sem_inc(sig("carrier"), 1)
                        for e in range(2):
                            nc.gpsimd.tensor_copy(bdX[RD * e:RD * e + RD, 4 * g:4 * g + 4, RD * e:RD * e + RD],
                                                  x_c[RD * e:RD * e + RD, 4 * g:4 * g + 4, :]).then_inc(sig("bdx"), 1)

            with pool.Fori(0, SEQ // RD - 1) as n:
                chunk(n)
            chunk(SEQ // RD - 1)
            pool.wait_ge(sig("y_out"), seen("y_out") + SEQ // RD)
            pool.dma_start(g_a[:, :, :], g_spill).then_inc(sig("g_loaded"), 16)


        @block.scalar
        def _(act):
            for b in PB:
                act.sem_inc(sig(f"bank_free{b}"), 1)
            act.sem_inc(sig("silu_done"), 2)
            act.sem_inc(sig("o_copied"), 1)
            act.wait_ge(sig("x_loaded"), 16)
            act.wait_ge(sig("con_loaded"), 16)

            def norm(r):
                nc.scalar.activation(ht[:, 0:4, :], x[:, 0:4, :], ACT.Square).then_inc(sig("sq_a"), 1)
                act.wait_ge(sig("sum_done"), r + 1)
                nc.scalar.activation(norm_t[:, 0, :], bank[2][:, :], ACT.Sqrt, bias=eps(0),
                                     scale=1.0 / D_MODEL).then_inc(sig("rms_done"), 1)

            norm(0)
            with act.Fori(0, 3) as it:
                for j in range(4):
                    act.wait_ge(sig("conv_done"), it * 4 + j + 1)
                    nc.scalar.activation(proj[:, bass.ds(it * 4 + j, 1), :].rearrange("p a t -> p (a t)"),
                                         conv[j % 2], ACT.Silu).then_inc(sig("silu_done"), 1)
            skip("act", 12)
            for i in range(12, IN_UNITS):
                b = k8_result(act, "act", 0, 0, 0)
                skip("act", 1)
                fn, scale = (ACT.Silu, 1.0) if i < 16 else (ACT.Copy, ND ** -0.5 if i < 20 else 1.0)
                nc.scalar.activation(proj[:, i, :], bank[b][:, :], fn, scale=scale
                                     ).then_inc(sig("proj_done"), 1)
                act.wait_ge(sig("proj_done"), i - 11)
                act.sem_inc(sig(f"bank_free{b}"), 1)
            act.wait_ge(sig("small_done"), 1)
            nc.scalar.activation(tok[:, :, :], bank[2][:, 0:P].rearrange("p (a b) -> p a b", a=4),
                                 ACT.Copy).then_inc(sig("tok_done"), 1)
            for i in range(2):
                src = proj[:, 20 + i, :]
                for g in range(2):
                    nc.scalar.activation(kst[i][0:64, g, :], src[64 * g:64 * g + 64, :], ACT.Copy
                                         ).then_inc(sig("blocks_done"), 1)
                    nc.scalar.activation(kst[i][64:128, g, 0:SEQ - 1], src[64 * g:64 * g + 64, 1:SEQ], ACT.Copy
                                         ).then_inc(sig("blocks_done"), 1)
            for i in range(NH):
                act.wait_ge(sig("bias_mm"), i + 1)
                nc.scalar.activation(bias[:, i, :], bank[4 + i % 4][:, :], ACT.Copy).then_inc(sig("bias_done"), 1)
            rings["act"][0].advance(8)
            ring = rings["act"][0]
            for s in range(4):
                act.wait_ge(sig(f"unit_done{s}"), ring.used[s])
            nc.scalar.activation(pebias, bank[3][:, 0:4], ACT.Copy).then_inc(sig("pebias_done"), 1)
            act.wait_ge(sig("pebias_done"), 1)
            for i in range(4):
                nc.scalar.activation(hid[:, i, :], bank[2][:, 64 * i:64 * i + 62], ACT.Silu,
                                     bias=pebias[:, i:i + 1]).then_inc(sig("hid_done"), 1)
            for i in range(2):
                act.wait_ge(sig("vtok_mm"), i + 1)
                nc.scalar.activation(vtok[:, 4 * i:4 * i + 4, :], bank[6 + i][:, :].rearrange("p (a b) -> p a b", a=4),
                                     ACT.Copy).then_inc(sig("vtok_done"), 1)
            act.wait_ge(sig("tok_done"), 1)
            nc.scalar.activation(gates[:, :, :], tok[:, :, 8:32], ACT.Sigmoid).then_inc(sig("gates_done"), 1)
            nc.scalar.activation(beta.rearrange("p (a b) -> p a b", a=4), tok[:, :, 0:4], ACT.Sigmoid
                                 ).then_inc(sig("gates_done"), 1)
            with act.Fori(0, 4) as j:
                def exp_(u):
                    act.wait_ge(sig("scored"), j * 24 + u + 3)
                    w = width(u)
                    nc.scalar.activation(probs[u % 2][:, 0:w], probs[u % 2][:, 0:w], ACT.Exp,
                                         bias=nmx[u % 2][:, 1:2], accum_out=sums[:, u:u + 1]
                                         ).then_inc(sig("exp_done"), 1)

                def evac(u):
                    act.wait_ge(sig("turned"), j * 24 + u + 1)
                    w, r = (P, width(u)) if u % 3 == 2 else (width(u), P)
                    nc.scalar.activation(probsT[u % 2][0:r, 0:w], bank[4][0:r, 0:w], ACT.Copy
                                         ).then_inc(sig("turn_copied"), 1)

                exp_(0)
                for u in range(24):
                    if u < 23:
                        exp_(u + 1)
                    evac(u)
            for i in range(4):
                act.wait_ge(sig("otok_turned"), i + 1)
                nc.scalar.activation(ht[:, 4 + i, :], bank[2 + i][:, :], ACT.Copy).then_inc(sig("mix_nsa"), 1)

            act.wait_ge(sig("g_arg"), 1)
            nc.scalar.activation(gaux, gtmp, ACT.Abs).then_inc(sig("g_step"), 1)
            act.wait_ge(sig("g_step"), 1)
            nc.scalar.activation(gaux, gaux, ACT.Exp, scale=-1.0).then_inc(sig("g_step"), 1)
            nc.scalar.activation(ea, v("alog"), ACT.Exp).then_inc(sig("g_step"), 1)
            act.wait_ge(sig("g_step"), 3)
            nc.scalar.activation(gaux, gaux, ACT.Ln, bias=c("ones")[:, 0:1]).then_inc(sig("g_step"), 1)
            act.wait_ge(sig("pair_done"), 5)
            nc.scalar.activation(rn0[:, 0:4, :], proj[:, 0:4, :], ACT.Square).then_inc(sig("qk_sq"), 1)
            nc.scalar.activation(rn0[:, 4:8, :], proj[:, 4:8, :], ACT.Square).then_inc(sig("qk_sq"), 1)
            act.wait_ge(sig("g_sum_mm"), 1)
            nc.scalar.activation(eg, bank[2][:, 0:32], ACT.Exp).then_inc(sig("eg_done"), 1)
            for i in range(8):
                act.wait_ge(sig("qk_sum"), i + 1)
                nc.scalar.activation(rn0[:, i, :], bank[4 + i % 4][:, :], ACT.Sqrt,
                                     bias=eps(3 if i < 4 else 0), scale=float(GD) if i < 4 else 1.0
                                     ).then_inc(sig("qk_root"), 1)
            with act.Fori(0, NCHUNK) as n:
                act.wait_ge(sig("decay_mm"), 3 * n + 1)
                nc.scalar.activation(egr, bank[2][:, :].rearrange("p (a b) -> p a b", a=GH), ACT.Exp
                                     ).then_inc(sig("decay_row"), 1)
                act.wait_ge(sig("decay_mm"), 3 * n + 2)
                nc.scalar.activation(dlow, bank[3][:, :].rearrange("p (a b) -> p a b", a=GH), ACT.Exp
                                     ).then_inc(sig("decay_low"), 1)
                act.wait_ge(sig("decay_mm"), 3 * n + 3)
                nc.scalar.activation(dup, bank[4][:, :].rearrange("p (a b) -> p a b", a=GH), ACT.Exp
                                     ).then_inc(sig("decay_up"), 1)
                act.wait_ge(sig("ktok_mm"), n + 1)
                nc.scalar.activation(ktok, bank[7][:, :].rearrange("p (a b) -> p a b", a=GH), ACT.Copy
                                     ).then_inc(sig("ktok_done"), 1)
                act.wait_ge(sig("vnew_mm"), n + 1)
                nc.scalar.activation(vn, bank[7][:, :].rearrange("p (a b) -> p a b", a=GH), ACT.Copy
                                     ).then_inc(sig("vnew_done"), 1)
                act.wait_ge(sig("o_mm"), n + 1)
                nc.scalar.activation(ht[:, 0:4, bass.ds(CHUNK * n, CHUNK)],
                                     bank[2][:, :].rearrange("p (a b) -> p a b", a=GH), ACT.Copy
                                     ).then_inc(sig("o_copied"), 1)
            act.wait_ge(sig("o_copied"), NCHUNK + 1)
            nc.scalar.activation(rn0[:, 0:4, :], ht[:, 0:4, :], ACT.Square).then_inc(sig("o_sq"), 1)
            for i in range(4):
                act.wait_ge(sig("o_sum"), i + 1)
                nc.scalar.activation(rn0[:, 4 + i, :], bank[4 + i][:, :], ACT.Sqrt, bias=eps(0), scale=1.0 / GD
                                     ).then_inc(sig("o_root"), 1)

            def gate_ups(f):
                with act.Fori(0, FT // 2) as it:
                    for j in (0, 2):
                        b = k8_result(act, "act", it, 4, j)
                        act.wait_ge(sig("ff_done"), f * FT + it * 2 + j // 2 + 1)
                        nc.scalar.activation(sil[:, j // 2, :], bank[b][:, :], ACT.Silu).then_inc(sig("sil_done"), 1)
                skip("act", 2 * FT)

            skip("act", DT)
            act.wait_ge(sig("x_added"), DT)
            norm(1)
            gate_ups(0)
            skip("act", 0, DT)
            act.wait_ge(sig("x_added"), 2 * DT)
            norm(2)

            def lora_results(fn, dst, bias=None):
                for m in range(DT):
                    b = k8_result_bank("act")
                    act.wait_ge(sig("lora_mm"), seen("lora_mm") + lora[0] + 1)
                    lora[0] += 1
                    nc.scalar.activation(dst[:, m, :], bank[b][:, :], fn,
                                         **({"bias": bias[:, m:m + 1]} if bias is not None else {})
                                         ).then_inc(sig("lora_out"), 1)
                    act.wait_ge(sig("lora_out"), lora[0])
                    act.sem_inc(sig(f"bank_free{b}"), 1)

            lora = [0]
            for i, (dst, rows) in enumerate(((hid_g1, P), (hid_g2, 32))):
                b = k8_result(act, "act", 0, 0, 0)
                skip("act", 1)
                nc.scalar.activation(dst[0:rows, :], bank[b][0:rows, :], ACT.Sigmoid).then_inc(sig("hid_g"), 1)
                act.wait_ge(sig("hid_g"), i + 1)
                act.sem_inc(sig(f"bank_free{b}"), 1)
            lora_results(ACT.Copy, g_a)
            rings["act"][0].advance(4)
            for i, fn in enumerate((ACT.Tanh, ACT.Copy)):
                b = k8_result_bank("act")
                act.wait_ge(sig("wa_mm"), seen("wa_mm") + i + 1)
                nc.scalar.activation(hid_wa[64 * i:64 * i + 64, :], bank[b][64 * i:64 * i + 64, :], fn
                                     ).then_inc(sig("hid_wa"), 1)
                act.wait_ge(sig("hid_wa"), i + 1)
                act.sem_inc(sig(f"bank_free{b}"), 1)
                if i == 0:
                    lora_results(ACT.Sigmoid, k_a_, v("w0"))
                    act.wait_ge(sig("pads"), 1)
                    nc.scalar.activation(e_c[:, :, :, 1:], k_a_.rearrange("p m (c t) -> p m c t", t=RD), ACT.Exp,
                                         scale=-DECAY).then_inc(sig("decay_exp"), 1)
            lora_results(ACT.Sigmoid, a_a, v("a0"))
            with act.Fori(0, 2) as it:
                for j in range(4):
                    b = k8_result(act, "act", it, 4, j)
                    act.sem_inc(sig("carrier"), 1)
                    nc.scalar.activation(v_a[:, bass.ds(it * 4 + j, 1), :].rearrange("p a t -> p (a t)"),
                                         bank[b][:, :], ACT.Copy).then_inc(sig("v_out"), 1)
                    act.wait_ge(sig("v_out"), it * 4 + j + 1)
                    act.sem_inc(sig(f"bank_free{b}"), 1)
            skip("act", 8)
            skip("act", 8)
            act.wait_ge(sig("r_out"), 8)
            act.wait_ge(sig("pads"), 2)
            nc.scalar.activation(ei_c[:, :, :, 1:], k_a_.rearrange("p m (c t) -> p m c t", t=RD), ACT.Exp,
                                 scale=DECAY).then_inc(sig("decay_exp"), 1)
            act.wait_ge(sig("decay_exp"), 2)
            act.wait_ge(sig("mixed"), 48)
            for m in range(DT):
                b = k8_result(act, "act", 0, 0, 0)
                skip("act", 1)
                nc.scalar.activation(k_a_[:, m, :], bank[b][:, :], ACT.Copy).then_inc(sig("k_out"), 1)
                nc.scalar.activation(ht[:, m, :], bank[b][:, :], ACT.Square, scale=v("k_k")[:, m:m + 1]
                                     ).then_inc(sig("k_out"), 1)
                act.wait_ge(sig("k_out"), 2 * m + 2)
                act.sem_inc(sig(f"bank_free{b}"), 1)
                if m:
                    act.wait_ge(sig("ksum_mm"), seen("ksum_mm") + m)
                    nc.scalar.activation(ht[:, m - 1, :], bank[2 + (m - 1) % 4][:, :], ACT.Sqrt, bias=eps(1)
                                         ).then_inc(sig("k_root"), 1)
            act.wait_ge(sig("ksum_mm"), seen("ksum_mm") + DT)
            nc.scalar.activation(ht[:, DT - 1, :], bank[2 + (DT - 1) % 4][:, :], ACT.Sqrt, bias=eps(1)
                                 ).then_inc(sig("k_root"), 1)
            act.wait_ge(sig("bd_zero"), 14)
            def half(dst, src, e, s, fn=ACT.Copy):
                nc.scalar.activation(dst[RD * e:RD * e + RD, :, RD * e:RD * e + RD], src, fn).then_inc(sig(s), 1)

            def stage(n, i):
                e = i % 2
                src = (kk_a, a_a)[i // 2][RD * e:RD * e + RD, :, bass.ds(RD * n, RD)]
                half((bdA, bdB)[i // 2], src, e, ("bda", "bdb")[i // 2])

            def chunk(n, more):
                for i, (dst, s) in enumerate(((bdBt, "bt_mm"), (bdKt, "kt_mm"), (bdVt, "vt_mm"))):
                    act.wait_ge(sig(s), seen(s) + n + 1)
                    src = bank[4 + i][:, :].rearrange("p (m t) -> p m t", m=DT)
                    for e in range(2):
                        half(dst, src[RD * e:RD * e + RD, :, :], e, "tok_out")
                nc.scalar.activation(vt_c, bank[6][:, :].rearrange("p (m t) -> p m t", m=DT), ACT.Copy
                                     ).then_inc(sig("tok_out"), 1)
                for lv in range(5):
                    for g in range(2):
                        act.wait_ge(sig("q_out"), n * 12 + 2 * lv + g + 1)
                        for e in range(2):
                            nc.scalar.activation(bdQ[RD * e:RD * e + RD, 4 * g:4 * g + 4, RD * e:RD * e + RD],
                                                 q_c[RD * e:RD * e + RD, 4 * g:4 * g + 4, :], ACT.Copy
                                                 ).then_inc(sig("bdq"), 1)
                    if more and lv in (1, 2):
                        stage(n + 1, lv + 1)
                act.wait_ge(sig("g_mm"), seen("g_mm") + n + 1)
                nc.scalar.activation(g_c, bank[1][:, :].rearrange("p (m t) -> p m t", m=DT), ACT.Copy, scale=-1.0
                                     ).then_inc(sig("g_out"), 1)
                if more:
                    stage(n + 1, 0)
                    stage(n + 1, 1)
                act.wait_ge(sig("xt_sub"), seen("xt_sub") + n * 12 + 12)
                for e in range(2):
                    half(bdXT, xt_c[RD * e:RD * e + RD, :, :], e, "bdxt")
                act.wait_ge(sig("u_out"), n + 1)
                for e in range(2):
                    half(bdU, u_c[RD * e:RD * e + RD, :, :], e, "bdu")
                act.wait_ge(sig("y_mm"), seen("y_mm") + n + 1)
                act.sem_inc(sig("carrier"), 1)
                nc.scalar.activation(kk_a[:, :, bass.ds(RD * n, RD)], bank[3][:, :].rearrange("p (m t) -> p m t", m=DT),
                                     ACT.Copy).then_inc(sig("y_out"), 1)
                act.wait_ge(sig("z_out"), seen("z_out") + 2 * n + 2)
                for e in range(2):
                    half(bdZ, z_c[RD * e:RD * e + RD, :, :], e, "bdz")

            for i in range(4):
                stage(0, i)
            with act.Fori(0, SEQ // RD - 1) as n:
                chunk(n, True)
            chunk(SEQ // RD - 1, False)
            act.wait_ge(sig("bdz"), seen("bdz") + 2 * SEQ // RD)
            for m in range(DT):
                act.wait_ge(sig("centered"), m + 1)
                nc.scalar.activation(ht[:, m, :], mixb[:, m, :], ACT.Square).then_inc(sig("dev_sq"), 1)
            for m in range(DT):
                act.wait_ge(sig("dev_mm"), seen("dev_mm") + m + 1)
                nc.scalar.activation(rsd[:, m, :], bank[4 + m % 2][:, :], ACT.Sqrt, bias=eps(2), scale=1.0 / RD
                                     ).then_inc(sig("dev_root"), 1)
            skip("act", DT)
            act.wait_ge(sig("x_added"), 3 * DT)
            norm(3)
            gate_ups(1)
            skip("act", 0, DT)
            act.wait_ge(sig("x_added"), 4 * DT)
            norm(4)


        @block.vector
        def _(dve):
            nc.vector.sem_inc(sig("scored"), 2)
            nc.vector.sem_inc(sig("pv_read"), 1)
            nc.vector.sem_inc(sig("pair_done"), 1)
            nc.vector.sem_inc(sig("chunk_done"), 1)
            nc.vector.sem_inc(sig("ff_done"), 2)
            dve.wait_ge(sig("x_loaded"), 16)
            dve.wait_ge(sig("con_loaded"), 16)

            def norm(r):
                nc.vector.tensor_tensor(ht[:, 4:8, :], x[:, 4:8, :], x[:, 4:8, :], ALU.mult
                                        ).then_inc(sig("sq_d"), 1)
                dve.wait_ge(sig("rms_done"), r + 1)
                nc.vector.reciprocal(norm_t[:, 1, :], norm_t[:, 0, :]).then_inc(sig("rrms_done"), 1)
                dve.wait_ge(sig("rrms_done"), r + 1)
                for k in range(DT):
                    nc.vector.scalar_tensor_tensor(ht[:, k, :], x[:, k, :], v(f"n{r}")[:, k:k + 1],
                                                   norm_t[:, 1, :], ALU.mult, ALU.mult
                                                   ).then_inc(sig("h_done"), 1)

            dve.wait_ge(sig("vec_loaded"), 16)
            norm(0)
            dve.wait_ge(sig("row_mm"), 1)
            nc.vector.tensor_copy(brow[0:NH, 0:512], bank[3][0:NH, :]).then_inc(sig("bias_row"), 1)
            nc.vector.tensor_copy(brow[0:NH, 512:BIAS_LEN], bank[4][0:NH, 0:128]).then_inc(sig("bias_row"), 1)
            with dve.Fori(0, 3) as it:
                for j in range(4):
                    b = k8_result(dve, "dve", it, 4, j)
                    dve.wait_ge(sig("silu_done"), it * 4 + j + 1)
                    taps = v("conv").rearrange("p (i w) -> p i w", w=4)
                    tap = lambda w: taps[:, bass.ds(it * 4 + j, 1), w]
                    nc.vector.tensor_scalar(conv[j % 2], bank[b][:, :], tap(3), None, ALU.mult
                                            ).then_inc(sig("tap"), 1)
                    for d in (1, 2, 3):
                        dve.wait_ge(sig("tap"), (it * 4 + j) * 3 + d)
                        ins = nc.vector.scalar_tensor_tensor(conv[j % 2][:, d:SEQ], bank[b][:, 0:SEQ - d],
                                                             tap(3 - d), conv[j % 2][:, d:SEQ],
                                                             ALU.mult, ALU.add)
                        ins.then_inc(sig("tap" if d < 3 else "conv_done"), 1)
                    dve.wait_ge(sig("conv_done"), it * 4 + j + 1)
                    dve.sem_inc(sig(f"bank_free{b}"), 1)
            skip("dve", IN_UNITS)
            rings["dve"][0].advance(8)
            dve.wait_ge(sig("cmp_mm"), 1)
            nc.vector.tensor_copy(kcT[:, 0:NCMP], bank[4][:, 0:NCMP]).then_inc(sig("cmp_done"), 1)
            nc.vector.tensor_copy(vcT[0:NCMP, :], bank[5][0:NCMP, 0:P]).then_inc(sig("cmp_done"), 1)
            dve.wait_ge(sig("gates_done"), 2)
            with dve.Fori(0, 4) as j:
                dve.wait_ge(sig("staged"), 3 * j + 3)
                for u in range(24):
                    s, qt, br = u // 12, u // 3 % 4, u % 3
                    w = width(u)
                    dve.wait_ge(sig("score_mm"), j * 24 + u + 1)
                    if br < 2:
                        bb = bias_st[:, s, SEQ - P - P * qt:]
                    else:
                        bb = bias_st[:, s, 415 - P * qt:415 - P * qt + 16 * (w - 1) + 1:16]
                    dve.sem_inc(sig("carrier"), 1)
                    nc.vector.tensor_tensor_reduce(
                        out=probs[u % 2][:, 0:w], in0=bank[2 + u % 2][:, 0:w], in1=bb, scale=1.0,
                        scalar=NEG, op0=ALU.add, op1=ALU.max, accum_out=nmx[u % 2][:, 0:1]
                    ).then_inc(sig("max_done"), 1)
                    dve.wait_ge(sig("max_done"), j * 24 + u + 1)
                    nc.vector.tensor_scalar(nmx[u % 2][:, 1:2], nmx[u % 2][:, 0:1], 0.1 * NEG, -1.0,
                                            ALU.max, ALU.mult).then_inc(sig("scored"), 1)
                dve.wait_ge(sig("exp_done"), j * 24 + 24)
                nc.vector.tensor_scalar(rg, sums, 1e-30, None, ALU.max).then_inc(sig("rg_step"), 1)
                dve.wait_ge(sig("rg_step"), 3 * j + 1)
                nc.vector.reciprocal(rg, rg).then_inc(sig("rg_step"), 1)
                dve.wait_ge(sig("rg_step"), 3 * j + 2)
                gv = gates_flat.rearrange("p (q s h b) -> p s q h b", q=4, s=2, h=4)[:, :, :, bass.ds(j, 1), :]
                nc.vector.tensor_tensor(rg.rearrange("p (s q b) -> p s q b", s=2, q=4),
                                        rg.rearrange("p (s q b) -> p s q b", s=2, q=4),
                                        gv.rearrange("p s q h b -> p s q (h b)"), ALU.mult
                                        ).then_inc(sig("rg_step"), 1)
                dve.wait_ge(sig("rg_step"), 3 * j + 3)
                dve.wait_ge(sig("pv_mm"), j + 1)
                for br in range(3):
                    scale = rg.rearrange("p (a b) -> p a b", b=3)[:, :, br:br + 1].broadcast_to([P, 8, ND])
                    nc.vector.tensor_tensor(oacc[br].rearrange("p (a d) -> p a d", a=8),
                                            bank[5 + br][:, :].rearrange("p (a d) -> p a d", a=8), scale,
                                            ALU.mult).then_inc(sig("branch"), 1)
                dve.wait_ge(sig("branch"), 4 * j + 3)
                dve.sem_inc(sig("pv_read"), 1)
                nc.vector.tensor_tensor(oacc[0], oacc[0], oacc[1], ALU.add).then_inc(sig("branch"), 1)
                dve.wait_ge(sig("branch"), 4 * j + 4)
                ov = otok.rearrange("p q (s h d) -> p s q h d", s=2, h=4)[:, :, :, bass.ds(j, 1), :]
                nc.vector.tensor_tensor(ov.rearrange("p s q h d -> p s q (h d)"),
                                        oacc[0].rearrange("p (s q d) -> p s q d", s=2, q=4),
                                        oacc[2].rearrange("p (s q d) -> p s q d", s=2, q=4), ALU.add
                                        ).then_inc(sig("pair_done"), 1)

            nc.vector.tensor_tensor(gtmp.rearrange("p (a b) -> p a b", a=4), tok[:, :, 4:8],
                                    v("dtb").unsqueeze(1).broadcast_to([P, 4, 4]), ALU.add
                                    ).then_inc(sig("g_arg"), 1)
            dve.wait_ge(sig("g_step"), 4)
            dve.wait_ge(sig("g_arg"), 1)
            nc.vector.scalar_tensor_tensor(g_col, gtmp, 0.0, gaux, ALU.max, ALU.add).then_inc(sig("g_pos"), 1)
            dve.wait_ge(sig("g_pos"), 1)
            nc.vector.scalar_tensor_tensor(g_col.rearrange("p (a b) -> p a b", a=4),
                                           g_col.rearrange("p (a b) -> p a b", a=4), -1.0,
                                           ea.unsqueeze(1).broadcast_to([P, 4, 4]), ALU.mult, ALU.mult
                                           ).then_inc(sig("g_done"), 1)
            nc.vector.memset(st, 0.0).then_inc(sig("st_zero"), 1)
            dve.wait_ge(sig("eg_done"), 1)
            nc.vector.scalar_tensor_tensor(nbeg, beta, -1.0, eg[:, 0:16], ALU.mult, ALU.mult
                                           ).then_inc(sig("nbeg_done"), 1)
            for i in range(8):
                dve.wait_ge(sig("qk_root"), i + 1)
                nc.vector.reciprocal(rn0[:, i, :], rn0[:, i, :]).then_inc(sig("qk_recip"), 1)
                dve.wait_ge(sig("qk_recip"), i + 1)
                nc.vector.tensor_tensor(proj[:, i, :], proj[:, i, :], rn0[:, i, :], ALU.mult
                                        ).then_inc(sig("qk_normed"), 1)

            def heads(b):
                return bank[b][:, :].rearrange("p (a b) -> p a b", a=GH)

            def every_head(a):
                return a.unsqueeze(1).broadcast_to([P, GH, P])

            def per_token(a, n):
                return a[:, bass.ds(4 * n, 4)].unsqueeze(2).broadcast_to([P, GH, P])

            with dve.Fori(0, NCHUNK) as n:
                dve.wait_ge(sig("decay_low"), n + 1)
                nc.vector.tensor_tensor(dlow, dlow, every_head(c("gt")), ALU.mult).then_inc(sig("mstep"), 1)
                dve.wait_ge(sig("mstep"), 2 * n + 1)
                nc.vector.tensor_tensor(dlow, dlow, per_token(beta, n), ALU.mult).then_inc(sig("mstep"), 1)
                dve.wait_ge(sig("mstep"), 2 * n + 2)
                dve.wait_ge(sig("kk_mm"), n + 1)
                nc.vector.tensor_tensor(mlow, heads(5), dlow, ALU.mult).then_inc(sig("m_done"), 1)
                nc.vector.tensor_copy(xi, every_head(c("ident"))).then_inc(sig("x_init"), 1)
                nc.vector.tensor_copy(xit, every_head(c("ident"))).then_inc(sig("x_init"), 1)
                dve.wait_ge(sig("decay_up"), n + 1)
                nc.vector.tensor_tensor(dup, dup, every_head(c("le")), ALU.mult).then_inc(sig("up_masked"), 1)
                dve.wait_ge(sig("up_masked"), n + 1)
                dve.wait_ge(sig("qk_mm"), n + 1)
                nc.vector.tensor_tensor(qk, heads(6), dup, ALU.mult).then_inc(sig("qk_done"), 1)
                dve.wait_ge(sig("vtok2_mm"), n + 1)
                nc.vector.tensor_tensor(vb, heads(2), per_token(beta, n), ALU.mult).then_inc(sig("vb_done"), 1)
                dve.wait_ge(sig("ks_mm"), n + 1)
                nc.vector.tensor_tensor(rr, heads(6), per_token(nbeg, n), ALU.mult).then_inc(sig("rhs_step"), 1)
                dve.wait_ge(sig("rhs_step"), n + 1)
                dve.wait_ge(sig("vb_done"), n + 1)
                nc.vector.tensor_tensor(rr, rr, vb, ALU.add).then_inc(sig("rhs_done"), 1)
                for lv in range(7):
                    dve.wait_ge(sig("qt_mm"), n * 7 + lv + 1)
                    nc.vector.tensor_tensor(qt_, heads(3), every_head(c("lvl")[:, P * lv:P * lv + P]), ALU.mult
                                            ).then_inc(sig("qt_done"), 1)
                    dve.wait_ge(sig("xx_mm"), n * 7 + lv + 1)
                    if lv < 6:
                        nc.vector.tensor_tensor(xi, xi, heads(4), ALU.subtract).then_inc(sig("x_step"), 1)
                    nc.vector.tensor_tensor(xit, xit, heads(5), ALU.subtract).then_inc(sig("x_step"), 1)
                dve.wait_ge(sig("st_mm"), n + 1)
                nc.vector.tensor_tensor(st, st, egr[:, :, P - 1:P].broadcast_to([P, GH, P]), ALU.mult
                                        ).then_inc(sig("st_step"), 1)
                dve.wait_ge(sig("st_step"), n + 1)
                nc.vector.tensor_tensor(st, st, heads(3), ALU.add).then_inc(sig("chunk_done"), 1)
            for i in range(4):
                dve.wait_ge(sig("o_root"), i + 1)
                nc.vector.reciprocal(rn0[:, 4 + i, :], rn0[:, 4 + i, :]).then_inc(sig("o_step"), 1)
                dve.wait_ge(sig("o_step"), 2 * i + 1)
                nc.vector.scalar_tensor_tensor(ht[:, i, :], ht[:, i, :], v("gnorm"), rn0[:, 4 + i, :],
                                               ALU.mult, ALU.mult).then_inc(sig("o_step"), 1)
                dve.wait_ge(sig("o_step"), 2 * i + 2)
                nc.vector.tensor_tensor(ht[:, i, :], ht[:, i, :], proj[:, 12 + i, :], ALU.mult
                                        ).then_inc(sig("mix_gdn"), 1)

            def add_results(units, total):
                with dve.Fori(0, units // 4) as it:
                    for j in range(4):
                        b = k8_result(dve, "dve", it, 4, j)
                        xm = x[:, bass.ds(it * 4 + j, 1), :].rearrange("p a t -> p (a t)")
                        nc.vector.tensor_tensor(xm, xm, bank[b][:, :], ALU.add).then_inc(sig("x_added"), 1)
                        dve.wait_ge(sig("x_added"), total - units + 1 + it * 4 + j)
                        dve.sem_inc(sig(f"bank_free{b}"), 1)
                skip("dve", units)

            add_results(DT, DT)

            def gate_ups(f):
                with dve.Fori(0, FT // 2) as it:
                    for j in (0, 2):
                        p = it * 2 + j // 2
                        bg = k8_result(dve, "dve", it, 4, j)
                        bu = k8_result(dve, "dve", it, 4, j + 1)
                        dve.wait_ge(sig("sil_done"), f * FT + p + 1)
                        nc.vector.tensor_tensor(hidden[:, bass.ds(p, 1), :].rearrange("p a t -> p (a t)"),
                                                sil[:, j // 2, :], bank[bu][:, :], ALU.mult).then_inc(sig("ff_done"), 1)
                        dve.wait_ge(sig("ff_done"), f * FT + p + 3)
                        dve.sem_inc(sig(f"bank_free{bg}"), 1)
                        dve.sem_inc(sig(f"bank_free{bu}"), 1)
                skip("dve", 2 * FT)

            def add_down(total):
                ring, banks = rings["dve"][1:]
                with dve.Fori(0, DT // 4) as it:
                    for j in range(4):
                        s, u = ring.at(j, it, 4)
                        dve.wait_ge(sig(f"down_done{s}"), u + 1)
                        b = PB[banks.at(j, it, 4)[0]]
                        xm = x[:, bass.ds(it * 4 + j, 1), :].rearrange("p a t -> p (a t)")
                        nc.vector.tensor_tensor(xm, xm, bank[b][:, :], ALU.add).then_inc(sig("x_added"), 1)
                        dve.wait_ge(sig("x_added"), total - DT + 1 + it * 4 + j)
                        dve.sem_inc(sig(f"bank_free{b}"), 1)
                skip("dve", 0, DT)

            norm(1)
            gate_ups(0)
            add_down(2 * DT)
            nc.vector.memset(h[:, :, HD - 1:HD], 0.0).then_inc(sig("pads_h"), 1)
            nc.vector.memset(padmask, 0.0).then_inc(sig("pads_h"), 1)
            dve.wait_ge(sig("pads_h"), 2)
            nc.vector.memset(padmask.rearrange("p (c t) -> p c t", t=RD + 1)[:, :, 0:1], 1.0).then_inc(sig("pads_h"), 1)
            nc.vector.memset(e_c[:, :, :, 0:1].rearrange("p m c t -> p (m c) t"), 0.0).then_inc(sig("pads"), 1)
            norm(2)
            dve.wait_ge(sig("h_done"), 3 * DT)

            mixes = [0]

            def mix(i, dst):
                mixes[0] += 1
                if mixes[0] > 2:
                    dve.wait_ge(sig("mix_used"), mixes[0] - 2)
                for k in range(DT):
                    nc.vector.tensor_tensor(dst[:, k, :], h[:, k, HD - 1:HD - 1 + SEQ], ht[:, k, :], ALU.subtract
                                            ).then_inc(sig("mix_diff"), 1)
                    dve.wait_ge(sig("mix_diff"), (mixes[0] - 1) * DT + k + 1)
                    nc.vector.scalar_tensor_tensor(dst[:, k, :], dst[:, k, :], v("mu")[:, DT * i + k:DT * i + k + 1],
                                                   ht[:, k, :], ALU.mult, ALU.add).then_inc(sig("mixed"), 1)

            mix(5, mixa)
            mix(1, mixb)
            mix(4, mixa)
            dve.wait_ge(sig("decay_exp"), 1)
            dve.wait_ge(sig("pads_h"), 3)
            for m in range(DT):
                nc.vector.tensor_tensor_scan(e_a[:, m, :], e_a[:, m, :], padmask, 0.0, ALU.mult, ALU.add
                                             ).then_inc(sig("decay_scan"), 1)
            mix(3, mixb)
            mix(0, mixa)
            skip("dve", 2)
            rings["dve"][2].advance(8 + 1 + 8 + 1 + 8)
            rings["dve"][0].advance(4)
            skip("dve", DT)
            dve.wait_ge(sig("decay_scan"), DT)
            mix(2, mixb)
            with dve.Fori(0, 2) as it:
                for j in range(4):
                    b = k8_result(dve, "dve", it, 4, j)
                    m = it * 4 + j
                    nc.vector.tensor_tensor(r_a[:, bass.ds(m, 1), :].rearrange("p a (c t) -> p (a c) t", t=RD),
                                            bank[b][:, :].rearrange("p (c t) -> p c t", t=RD),
                                            e_c[:, bass.ds(m, 1), :, 1:].rearrange("p a c t -> p (a c) t"), ALU.mult
                                            ).then_inc(sig("r_out"), 1)
                    dve.wait_ge(sig("r_out"), m + 1)
                    dve.sem_inc(sig(f"bank_free{b}"), 1)
            skip("dve", DT)
            nc.vector.memset(ei_c[:, :, :, 0:1].rearrange("p m c t -> p (m c) t"), 0.0).then_inc(sig("pads"), 1)
            dve.wait_ge(sig("decay_exp"), 2)
            for m in range(DT):
                nc.vector.tensor_tensor_scan(ei_a[:, m, :], ei_a[:, m, :], padmask, 0.0, ALU.mult, ALU.add
                                             ).then_inc(sig("decay_scan"), 1)
            skip("dve", DT)
            dve.wait_ge(sig("decay_scan"), 2 * DT)
            nc.vector.tensor_copy(p_c, e_c[:, :, :, RD:RD + 1].rearrange("p m c t -> p m (c t)")
                                  ).then_inc(sig("pc_done"), 1)
            steps = [0]

            def step(ins):
                ins.then_inc(sig("key_step"), 1)
                steps[0] += 1
                dve.wait_ge(sig("key_step"), steps[0])

            def chunked(a, m):
                return a[:, m, :].rearrange("p (c t) -> p c t", t=RD)

            for m in range(DT):
                dve.wait_ge(sig("k_root"), m + 1)
                step(nc.vector.reciprocal(ht[:, m, :], ht[:, m, :]))
                nc.vector.tensor_scalar(norm_t[:, m % 2, :], a_a[:, m, :], -1.0, v("k_a")[:, m:m + 1], ALU.add, ALU.mult
                                        ).then_inc(sig("key_mod"), 1)
                step(nc.vector.scalar_tensor_tensor(ht[:, m, :], k_a_[:, m, :], v("k_k")[:, m:m + 1], ht[:, m, :],
                                                    ALU.mult, ALU.mult))
                dve.wait_ge(sig("key_mod"), m + 1)
                step(nc.vector.scalar_tensor_tensor(k_a_[:, m, :], norm_t[:, m % 2, :], 1.0, k_a_[:, m, :],
                                                    ALU.add, ALU.mult))
                step(nc.vector.tensor_tensor(a_a[:, m, :], a_a[:, m, :], ht[:, m, :], ALU.mult))
                step(nc.vector.tensor_tensor(chunked(k_a_, m), chunked(k_a_, m), ei_c[:, m, :, 1:], ALU.mult))
                step(nc.vector.tensor_tensor(chunked(a_a, m), chunked(a_a, m), ei_c[:, m, :, 1:], ALU.mult))
                step(nc.vector.tensor_tensor(chunked(kk_a, m), chunked(ht, m), e_c[:, m, :, 0:RD], ALU.mult))
            dve.sem_inc(sig("scan_ready"), 1)
            dve.wait_ge(sig("bd_zero"), 14)

            def tiles(b):
                return bank[b][:, :].rearrange("p (m t) -> p m t", m=DT)

            def all_tiles(name, e=None, n=DT):
                a = c(name) if e is None else c(name)[RD * e:RD * e + RD, :]
                return a.unsqueeze(1).broadcast_to([P if e is None else RD, n, RD])

            def stage(n, i):
                now, e = bass.ds(RD * n, RD), (i - 3) % 2
                lo = slice(RD * e, RD * e + RD)
                dst, src = ((b_c, a_a[:, :, now]), (ar_c[:, :, 0:RD], kk_a[:, :, now]), (ar_c[:, :, RD:], r_a[:, :, now]),
                            (bdK[lo, :, lo], k_a_[lo, :, now]), (bdK[lo, :, lo], k_a_[lo, :, now]),
                            (bdV[lo, :, lo], v_a[lo, :, now]), (bdV[lo, :, lo], v_a[lo, :, now]))[i]
                nc.vector.tensor_copy(dst, src).then_inc(sig("rhs_staged"), 1)

            def chunk(n, more):
                dve.wait_ge(sig("m_mm"), seen("m_mm") + n + 1)
                for e in range(2):
                    nc.vector.tensor_tensor(bdM[RD * e:RD * e + RD, :, RD * e:RD * e + RD],
                                            tiles(0)[RD * e:RD * e + RD, :, :], all_tiles("gt64", e), ALU.mult
                                            ).then_inc(sig("m_out"), 1)
                for dst in (x_c, xt_c):
                    nc.vector.tensor_copy(dst, all_tiles("id64")).then_inc(sig("m_out"), 1)
                for e in range(2):
                    nc.vector.tensor_copy(bdX[RD * e:RD * e + RD, :, RD * e:RD * e + RD], all_tiles("id64", e)
                                          ).then_inc(sig("m_out"), 1)
                dve.wait_ge(sig("k_mm"), seen("k_mm") + n + 1)
                for g in range(2):
                    kb = bank[1 + g][:, :].rearrange("p (m t) -> p m t", m=4)
                    for e in range(2):
                        nc.vector.tensor_tensor(bdAK[RD * e:RD * e + RD, 4 * g:4 * g + 4, RD * e:RD * e + RD],
                                                kb[RD * e:RD * e + RD, :, 0:RD], all_tiles("lt64", e, 4), ALU.mult
                                                ).then_inc(sig("ak_out"), 1)
                    nc.vector.tensor_tensor(rk_c[:, 4 * g:4 * g + 4, :], kb[:, :, RD:], all_tiles("le64", None, 4),
                                            ALU.mult).then_inc(sig("ak_out"), 1)
                dve.wait_ge(sig("rb_mm"), seen("rb_mm") + n + 1)
                nc.vector.tensor_tensor(rb_c, tiles(3), all_tiles("le64"), ALU.mult).then_inc(sig("rb_out"), 1)
                nc.vector.tensor_copy(ry_c, ar_c[:, :, RD:]).then_inc(sig("rb_out"), 1)
                ahead = list(range(7)) if more else []
                for lv in range(6):
                    for g in range(2):
                        dve.wait_ge(sig("q_mm"), seen("q_mm") + n * 12 + 2 * lv + g + 1)
                        qb = bank[(7, 0)[g]][:, 0:256].rearrange("p (m t) -> p m t", m=4)
                        lm = c("lvl64")[:, RD * lv:RD * lv + RD].unsqueeze(1).broadcast_to([P, 4, RD])
                        nc.vector.tensor_tensor(q_c[:, 4 * g:4 * g + 4, :], qb, lm, ALU.mult).then_inc(sig("q_out"), 1)
                        if lv > 1 and ahead:
                            stage(n + 1, ahead.pop(0))
                    for g in range(2):
                        for a, s, sub, b, k in ((xt_c, "xtm", "xt_sub", 4, 12), (x_c, "xmm", "x_sub", 2, 10)):
                            if lv == 5 and a is x_c:
                                continue
                            dve.wait_ge(sig(s), seen(s) + n * k + 2 * lv + g + 1)
                            nc.vector.tensor_tensor(a[:, 4 * g:4 * g + 4, :], a[:, 4 * g:4 * g + 4, :],
                                                    bank[b + g][:, 0:256].rearrange("p (m t) -> p m t", m=4),
                                                    ALU.subtract).then_inc(sig(sub), 1)
                dve.wait_ge(sig("u_mm"), seen("u_mm") + n + 1)
                nc.vector.tensor_copy(u_c, tiles(7)).then_inc(sig("u_out"), 1)
                dve.wait_ge(sig("z_mm"), seen("z_mm") + n + 1)
                nc.vector.tensor_tensor(z_c, z_c, tiles(6), ALU.add).then_inc(sig("z_out"), 1)
                dve.wait_ge(sig("z_out"), seen("z_out") + 2 * n + 1)
                nc.vector.tensor_tensor(z_c, z_c, p_c[:, :, bass.ds(n, 1)].broadcast_to([P, DT, RD]), ALU.mult
                                        ).then_inc(sig("z_out"), 1)

            for i in range(7):
                stage(0, i)
            with dve.Fori(0, SEQ // RD - 1) as n:
                chunk(n, True)
            chunk(SEQ // RD - 1, False)
            dve.wait_ge(sig("y_out"), seen("y_out") + SEQ // RD)
            for m in range(DT):
                nc.vector.scalar_tensor_tensor(r_a[:, m, :], r_a[:, m, :], v("r_k")[:, m:m + 1], k_a_[:, m, :],
                                               ALU.mult, ALU.mult).then_inc(sig("rk_done"), 1)
            for m in range(DT):
                dve.wait_ge(sig("mean_mm"), seen("mean_mm") + m + 1)
                nc.vector.scalar_tensor_tensor(mixb[:, m, :], bank[2 + m % 2][:, :], -1.0 / RD, kk_a[:, m, :],
                                               ALU.mult, ALU.add).then_inc(sig("centered"), 1)
            dve.wait_ge(sig("centered"), DT)
            dve.sem_inc(sig("y_read"), 8)
            for m in range(DT):
                dve.wait_ge(sig("bonus_mm"), seen("bonus_mm") + m + 1)
                nc.vector.tensor_tensor(v_a[:, m, :], bank[(0, 1)[m % 2]][:, :], v_a[:, m, :], ALU.mult
                                        ).then_inc(sig("bonus"), 1)
                dve.wait_ge(sig("dev_root"), m + 1)
                step(nc.vector.reciprocal(rsd[:, m, :], rsd[:, m, :]))
                step(nc.vector.tensor_tensor(mixb[:, m, :], mixb[:, m, :], rsd[:, m, :], ALU.mult))
                step(nc.vector.tensor_scalar(mixb[:, m, :], mixb[:, m, :], v("lnw")[:, m:m + 1], v("lnb")[:, m:m + 1],
                                             ALU.mult, ALU.add))
                dve.wait_ge(sig("bonus"), m + 1)
                step(nc.vector.tensor_tensor(mixb[:, m, :], mixb[:, m, :], v_a[:, m, :], ALU.add))
                dve.wait_ge(sig("g_loaded"), 16)
                nc.vector.tensor_tensor(k_a_[:, m, :], mixb[:, m, :], g_a[:, m, :], ALU.mult).then_inc(sig("gated"), 1)
            add_results(DT, 3 * DT)
            norm(3)
            gate_ups(1)
            add_down(4 * DT)
            norm(4)

        @block.tensor
        def _(pe):
            pe.wait_ge(sig("con_loaded"), 16)

            def norm_sum(r):
                for k in range(DT):
                    pe.wait_ge(sig("sq_a" if k < 4 else "sq_d"), r + 1)
                    mm = nc.tensor.matmul(bank[2][:, :], c("ones"), ht[:, k, :], start=k == 0, stop=k == DT - 1)
                mm.then_inc(sig("sum_done"), 1)

            norm_sum(0)
            pe.wait_ge(sig("vec_loaded"), 16)
            pe.wait_ge(sig("onehot_loaded"), 16)
            nc.tensor.matmul(bank[3][0:NH, :], v("tbl")[0:33, :], oh[0:33, 0:512], start=True, stop=True)
            nc.tensor.matmul(bank[4][0:NH, 0:128], v("tbl")[0:33, :], oh[0:33, 512:BIAS_LEN],
                             start=True, stop=True).then_inc(sig("row_mm"), 1)
            for _ in range(2):
                with pe.Fori(0, 3) as it:
                    for j in range(4):
                        k8_product(pe, it, 4, j, ht, ("h_done", 0))
                skip("pe", 12)
            for j in range(2):
                k8_product(pe, 0, 0, j, ht)
            skip("pe", 2)
            ws = v("wsmall").rearrange("p (k n) -> p k n", k=DT)
            for t in range(4):
                for k in range(DT):
                    mm = nc.tensor.matmul(bank[2][:, 32 * t:32 * t + 32], ht[:, k, P * t:P * t + P], ws[:, k, :],
                                          start=k == 0, stop=k == DT - 1)
            mm.then_inc(sig("small_done"), 1)
            pe.wait_ge(sig("shifted_loaded"), 16)
            pe.wait_ge(sig("proj_done"), IN_UNITS - 12)
            for i in range(NH):
                if i >= 4:
                    pe.wait_ge(sig("bias_done"), i - 3)
                nc.tensor.matmul(bank[4 + i % 4][:, :], c("flip"), shifted[:, i, :], start=True, stop=True
                                 ).then_inc(sig("bias_mm"), 1)
            pe.wait_ge(sig("blocks_done"), 8)
            pe.wait_ge(sig("tok_done"), 1)
            ring = rings["pe"][0]
            pv = v("pe").rearrange("p (i m) -> p i m", i=2)
            for i in range(8):
                s, u = ring.at(0)
                pe.wait_ge(sig(f"w_full{s}"), 16 * (u + 1))
                for m in range(8):
                    tap = 8 * (i % 2) + m
                    w = wring[:, s, P * m:P * m + P]
                    nc.tensor.matmul(bank[2][:, 64 * (i // 2):64 * (i // 2) + 62], w,
                                     kst[i // 4][:, :, 2 * tap:2 * tap + CMP_STRIDE * (NCMP - 1) + 1:CMP_STRIDE],
                                     start=tap == 0, stop=tap == 15)
                    mm = nc.tensor.matmul(bank[3][:, i // 2:i // 2 + 1], w, pv[:, i // 4, tap:tap + 1],
                                          start=tap == 0, stop=tap == 15)
                mm.then_inc(sig(f"unit_done{s}"), 1)
                ring.advance(1)
            pe.wait_ge(sig("bias_done"), NH)
            pe.wait_ge(sig("hid_done"), 4)
            cw = v("cw2").rearrange("p (i k n) -> p i k n", i=2, k=2)
            for g in range(2):
                for k in range(2):
                    nc.tensor.matmul(bank[4][64 * g:64 * g + 64, 0:NCMP], cw[:, 0, k, :],
                                     hid[:, k, NCMP * g:NCMP * g + NCMP], start=k == 0, stop=k == 1)
            for g in range(2):
                for k in range(2):
                    mm = nc.tensor.matmul(bank[5][0:NCMP, 64 * g:64 * g + 64],
                                          hid[:, 2 + k, NCMP * g:NCMP * g + NCMP], cw[:, 1, k, :],
                                          start=k == 0, stop=k == 1)
            mm.then_inc(sig("cmp_mm"), 1)
            pe.wait_ge(sig("proj_done"), IN_UNITS - 12)
            for i in range(2):
                for t in range(4):
                    mm = nc.tensor.transpose(bank[6 + i][:, P * t:P * t + P], proj[:, 23 + 2 * i, P * t:P * t + P],
                                             c("ident"))
                mm.then_inc(sig("vtok_mm"), 1)
            pe.wait_ge(sig("cmp_done"), 2)
            pe.wait_ge(sig("vtok_done"), 2)
            with pe.Fori(0, 4) as j:
                pe.wait_ge(sig("staged"), 3 * j + 3)

                def score(u):
                    s, qt, br = u // 12, u // 3 % 4, u % 3
                    keys = (proj[:, 22, :], proj[:, 24, :], kcT)[br]
                    pe.wait_ge(sig("scored"), j * 24 + u + 1)
                    nc.tensor.matmul(bank[2 + u % 2][:, 0:width(u)], q_st[64 * s:64 * s + 64, P * qt:P * qt + P],
                                     keys[64 * s:64 * s + 64, 0:width(u)], start=True, stop=True
                                     ).then_inc(sig("score_mm"), 1)

                def turn(u):
                    pe.wait_ge(sig("exp_done"), j * 24 + u + 1)
                    w = width(u)
                    for b in range(-(-w // P)):
                        n = min(P, w - P * b)
                        mm = nc.tensor.transpose(bank[4][0:n, P * b:P * b + P], probs[u % 2][:, P * b:P * b + n],
                                                 c("ident"))
                    mm.then_inc(sig("turned"), 1)

                def weigh(u):
                    s, qt, br = u // 12, u // 3 % 4, u % 3
                    w = width(u)
                    pe.wait_ge(sig("turn_copied"), j * 24 + u + 1)
                    nb = -(-w // P)
                    for b in range(nb):
                        n = min(P, w - P * b)
                        vals = vtok[:, 4 * br + b, 64 * s:64 * s + 64] if br < 2 else vcT[0:n, 64 * s:64 * s + 64]
                        o = (4 * s + qt) * ND
                        mm = nc.tensor.matmul(bank[5 + br][:, o:o + ND], probsT[u % 2][0:n, P * b:P * b + P], vals,
                                              start=b == 0, stop=b == nb - 1)
                    if u == 23:
                        mm.then_inc(sig("pv_mm"), 1)

                score(0)
                score(1)
                pe.wait_ge(sig("pv_read"), j + 1)
                for u in range(24):
                    turn(u)
                    if u < 22:
                        score(u + 2)
                    weigh(u)
            pe.wait_ge(sig("pair_done"), 5)
            for i in range(4):
                for t in range(4):
                    mm = nc.tensor.transpose(bank[2 + i][:, P * t:P * t + P], otok[:, t, P * i:P * i + P], c("ident"))
                mm.then_inc(sig("otok_turned"), 1)

            pe.wait_ge(sig("g_done"), 1)
            nc.tensor.matmul(bank[2][:, 0:16], c("le"), g_col, start=True, stop=True)
            nc.tensor.matmul(bank[2][:, 16:32], c("gt"), g_col, start=True, stop=True).then_inc(sig("g_sum_mm"), 1)
            pe.wait_ge(sig("mix_nsa"), 4)
            for i in range(8):
                pe.wait_ge(sig("qk_sq"), 1 + i // 4)
                if i >= 4:
                    pe.wait_ge(sig("qk_root"), i - 3)
                nc.tensor.matmul(bank[4 + i % 4][:, :], c("ones"), rn0[:, i, :], start=True, stop=True
                                 ).then_inc(sig("qk_sum"), 1)
            pe.wait_ge(sig("qk_root"), 8)
            pe.wait_ge(sig("eg_done"), 1)
            pe.wait_ge(sig("st_zero"), 1)
            with pe.Fori(0, NCHUNK) as n:
                def four(b, lhs, rhs, s, first=True, last=True):
                    for i in range(GH):
                        mm = nc.tensor.matmul(bank[b][:, P * i:P * i + P], lhs(i), rhs(i), start=first, stop=last)
                    mm.then_inc(sig(s), 1)

                pe.wait_ge(sig("g_spread"), 3 * n + 3)
                pe.wait_ge(sig("o_copied"), n + 1)
                four(2, lambda i: gbc[:, i, :], lambda i: c("le"), "decay_mm")
                nc.tensor.matmul(bank[3][:, :], c("le"), gtg_flat, start=True, stop=True).then_inc(sig("decay_mm"), 1)
                nc.tensor.matmul(bank[4][:, :], c("gt"), leg_flat, start=True, stop=True).then_inc(sig("decay_mm"), 1)
                pe.wait_ge(sig("chunk_staged"), 3 * n + 3)
                four(5, lambda i: k_st[:, i, :], lambda i: k_st[:, i, :], "kk_mm")
                four(6, lambda i: k_st[:, i, :], lambda i: qst[:, i, :], "qk_mm")
                for i in range(GH):
                    mm = nc.tensor.transpose(bank[7][:, P * i:P * i + P], k_st[:, i, :], c("ident"))
                mm.then_inc(sig("ktok_mm"), 1)
                pe.wait_ge(sig("decay_row"), n + 1)
                for i in range(GH):
                    mm = nc.tensor.transpose(bank[2][:, P * i:P * i + P], v_st[:, i, :], c("ident"))
                mm.then_inc(sig("vtok2_mm"), 1)
                pe.wait_ge(sig("qk_done"), n + 1)
                four(6, lambda i: k_st[:, i, :], lambda i: st[:, i, :], "ks_mm")
                pe.wait_ge(sig("m_done"), n + 1)
                pe.wait_ge(sig("x_init"), 2 * n + 2)
                pe.wait_ge(sig("decay_low"), n + 1)
                pe.wait_ge(sig("decay_up"), n + 1)
                for lv in range(7):
                    if lv:
                        pe.wait_ge(sig("x_step"), n * 13 + 2 * lv)
                    four(3, lambda i: mlow[:, i, :], lambda i: xit[:, i, :], "qt_mm")
                    pe.wait_ge(sig("qt_done"), n * 7 + lv + 1)
                    if lv < 6:
                        for i in range(GH):
                            nc.tensor.matmul(bank[4][:, P * i:P * i + P], qt_[:, i, :], xi[:, i, :], start=True, stop=True)
                    four(5, lambda i: xi[:, i, :], lambda i: qt_[:, i, :], "xx_mm")
                pe.wait_ge(sig("x_step"), n * 13 + 13)
                pe.wait_ge(sig("rhs_done"), n + 1)
                pe.wait_ge(sig("ktok_done"), n + 1)
                four(7, lambda i: xit[:, i, :], lambda i: rr[:, i, :], "vnew_mm")
                pe.wait_ge(sig("q_decayed"), n + 1)
                pe.wait_ge(sig("vnew_done"), n + 1)
                pe.wait_ge(sig("vb_done"), n + 1)
                for i in range(GH):
                    nc.tensor.matmul(bank[2][:, P * i:P * i + P], st[:, i, :], qst[:, i, :], start=True, stop=False)
                    mm = nc.tensor.matmul(bank[2][:, P * i:P * i + P], vn[:, i, :], qk[:, i, :], start=False, stop=True)
                mm.then_inc(sig("o_mm"), 1)
                pe.wait_ge(sig("k_decayed"), n + 1)
                four(3, lambda i: ktok[:, i, :], lambda i: vn[:, i, :], "st_mm")
            pe.wait_ge(sig("o_sq"), 1)
            for i in range(4):
                nc.tensor.matmul(bank[4 + i][:, :], c("ones"), rn0[:, i, :], start=True, stop=True
                                 ).then_inc(sig("o_sum"), 1)
            pe.wait_ge(sig("mix_gdn"), 4)
            pe.wait_ge(sig("mix_nsa"), 4)
            with pe.Fori(0, DT // 4) as it:
                for j in range(4):
                    k8_product(pe, it, 4, j, ht)
            skip("pe", DT)

            def gate_ups(r):
                with pe.Fori(0, FT // 2) as it:
                    for j in range(4):
                        k8_product(pe, it, 4, j, ht, ("h_done", DT * r))
                skip("pe", 2 * FT)

            def downs(gate):
                with pe.Fori(0, 2) as it:
                    for j in range(4):
                        down_product(pe, it, 4, j, gate)
                skip("pe", 0, DT)

            norm_sum(1)
            gate_ups(1)
            downs(2)
            norm_sum(2)

            ring, _, banks = rings["pe"]

            def free_bank():
                b, w = banks.at(0)
                pe.wait_ge(sig(f"bank_free{PB[b]}"), w + 1)
                banks.advance(1)
                return PB[b]

            done = {}

            def bump(s):
                done[s] = done.get(s, 0) + 1
                return sig(s)

            def lora_out(parts):
                for m in range(DT):
                    b = free_bank()
                    for i, (w, rhs) in enumerate(parts):
                        mm = nc.tensor.matmul(bank[b][:, :], w[:, P * m:P * m + P], rhs, start=i == 0,
                                              stop=i == len(parts) - 1)
                    mm.then_inc(bump("lora_mm"), 1)

            for _ in range(2):
                k8_product(pe, 0, 0, 0, mixa, ("mixed", 0))
                skip("pe", 1)
            pe.wait_ge(sig("mixed"), DT)
            (s2, c2), (s3, c3) = ring.at(0), ring.at(1)
            pe.wait_ge(sig(f"w_full{s2}"), 16 * (c2 + 1))
            pe.wait_ge(sig(f"w_full{s3}"), 16 * (c3 + 1))
            pe.wait_ge(sig("hid_g"), 2)
            lora_out(((wring[:, s2, :], hid_g1), (wring[0:32, s3, :], hid_g2[0:32, :])))
            pe.wait_ge(sig("lora_mm"), seen("lora_mm") + DT)
            pe.sem_inc(sig(f"unit_done{s2}"), 1)
            pe.sem_inc(sig(f"unit_done{s3}"), 1)
            pe.sem_inc(sig("mix_used"), 1)
            ring.advance(2)
            (s4, c4), (s5, c5) = ring.at(0), ring.at(1)
            pe.wait_ge(sig(f"w_full{s4}"), 16 * (c4 + 1))
            pe.wait_ge(sig(f"w_full{s5}"), 16 * (c5 + 1))
            for i, mx in enumerate((mixb, mixa)):
                b = free_bank()
                for k in range(DT):
                    pe.wait_ge(sig("mixed"), DT * (i + 1) + k + 1)
                    mm = nc.tensor.matmul(bank[b][64 * i:64 * i + 64, :], wring[:, s4, P * k + 64 * i:P * k + 64 * i + 64],
                                          mx[:, k, :], start=k == 0, stop=k == DT - 1)
                mm.then_inc(sig("wa_mm"), 1)
                pe.wait_ge(sig("hid_wa"), i + 1)
                pe.sem_inc(sig("mix_used"), 1)
                lora_out(((wring[64 * i:64 * i + 64, s5, :], hid_wa[64 * i:64 * i + 64, :]),))
            pe.wait_ge(sig("lora_mm"), seen("lora_mm") + 3 * DT)
            pe.sem_inc(sig(f"unit_done{s4}"), 1)
            pe.sem_inc(sig(f"unit_done{s5}"), 1)
            ring.advance(2)
            for i, mx in enumerate((mixb, mixa)):
                with pe.Fori(0, 2) as it:
                    for j in range(4):
                        k8_product(pe, it, 4, j, mx, ("mixed", DT * (3 + i)))
                skip("pe", DT)
                s, u = ring.at(3)
                pe.wait_ge(sig(f"unit_done{s}"), u)
                pe.sem_inc(sig("mix_used"), 1)
            for m in range(DT):
                k8_product(pe, 0, 0, 0, mixb, ("mixed", 5 * DT))
                skip("pe", 1)
                if m:
                    pe.wait_ge(sig("k_out"), 2 * m)
                    if m > 4:
                        pe.wait_ge(sig("k_root"), m - 4)
                    nc.tensor.matmul(bank[2 + (m - 1) % 4][:, :], c("blk"), ht[:, m - 1, :], start=True, stop=True
                                     ).then_inc(sig("ksum_mm"), 1)
            pe.wait_ge(sig("k_out"), 2 * DT)
            pe.wait_ge(sig("k_root"), DT - 4)
            nc.tensor.matmul(bank[2 + (DT - 1) % 4][:, :], c("blk"), ht[:, DT - 1, :], start=True, stop=True
                             ).then_inc(sig("ksum_mm"), 1)

            pe.wait_ge(sig("pc_done"), 1)
            pe.wait_ge(sig("k_root"), DT)
            def tiles(b, parts, s=None, lo=0, hi=DT, w=RD, start=None, stop=None):
                for m in range(lo, hi):
                    o = (m - lo) * w
                    for i, (lhs, rhs) in enumerate(parts):
                        if start is None:
                            mm = nc.tensor.matmul(bank[b][:, o:o + w], lhs[:, m, :], rhs(m), start=i == 0,
                                                  stop=i == len(parts) - 1)
                        else:
                            mm = nc.tensor.matmul(bank[b][:, o:o + w], lhs[:, m, :], rhs(m),
                                                  start=start and m == lo and i == 0, stop=stop,
                                                  skip_group_check=True)
                if s:
                    mm.then_inc(sig(s), 1)

            def stacked(a):
                return lambda m: a[:, m, :]

            def chunk(n):
                pe.wait_ge(sig("bda"), seen("bda") + 2 * n + 2)
                pe.wait_ge(sig("rhs_staged"), 7 * n + 7)
                tiles(0, ((bdA, stacked(b_c)),), "m_mm")
                tiles(1, ((bdK, stacked(ar_c)),), None, 0, 4, P)
                tiles(2, ((bdK, stacked(ar_c)),), "k_mm", 4, 8, P)
                pe.wait_ge(sig("bdb"), seen("bdb") + 2 * n + 2)
                tiles(4, ((bdB, lambda m: c("id64")),), "bt_mm")
                tiles(5, ((bdK, lambda m: c("id64")),), "kt_mm")
                pe.wait_ge(sig("y_out"), seen("y_out") + n)
                tiles(3, ((bdB, lambda m: ar_c[:, m, RD:]),), "rb_mm")
                pe.wait_ge(sig("z_out"), seen("z_out") + 2 * n)
                tiles(6, ((bdV, lambda m: c("id64")),), "vt_mm")
                pe.wait_ge(sig("m_out"), 6 * n + 6)
                pe.wait_ge(sig("ak_out"), 6 * n + 6)
                pe.wait_ge(sig("rb_out"), 2 * n + 2)
                pe.wait_ge(sig("tok_out"), seen("tok_out") + 7 * n + 4)
                for lv in range(6):
                    if lv == 5:
                        pe.wait_ge(sig("tok_out"), seen("tok_out") + 7 * n + 7)
                        tiles(1, ((bdA, stacked(z_c)), (bdAK, stacked(vt_c))), "g_mm")
                    for g in range(2):
                        if lv:
                            pe.wait_ge(sig("xt_sub"), seen("xt_sub") + n * 12 + 2 * (lv - 1) + g + 1)
                        tiles((7, 0)[g], ((bdM, stacked(xt_c)),), "q_mm", 4 * g, 4 * g + 4)
                    for g in range(2):
                        pe.wait_ge(sig("q_out"), n * 12 + 2 * lv + g + 1)
                        if lv:
                            pe.wait_ge(sig("bdx"), n * 20 + 4 * (lv - 1) + 2 * g + 2)
                        tiles(4 + g, ((bdX, stacked(q_c)),), "xtm", 4 * g, 4 * g + 4)
                        if lv < 5:
                            pe.wait_ge(sig("bdq"), seen("bdq") + n * 20 + 4 * lv + 2 * g + 2)
                            tiles(2 + g, ((bdQ, stacked(x_c)),), "xmm", 4 * g, 4 * g + 4)
                pe.wait_ge(sig("x_sub"), seen("x_sub") + n * 10 + 10)
                pe.wait_ge(sig("bdz"), seen("bdz") + 2 * n)
                tiles(6, ((bdKt, stacked(vt_c)),), None, start=True, stop=False)
                tiles(3, ((bdZ, stacked(ry_c)), (bdVt, stacked(rk_c))), None, start=True, stop=False)
                pe.wait_ge(sig("bdxt"), seen("bdxt") + 2 * n + 2)
                pe.wait_ge(sig("g_out"), seen("g_out") + n + 1)
                tiles(7, ((bdXT, stacked(g_c)),), "u_mm")
                pe.wait_ge(sig("u_out"), n + 1)
                tiles(6, ((bdBt, stacked(u_c)),), "z_mm", start=False, stop=True)
                pe.wait_ge(sig("bdu"), seen("bdu") + 2 * n + 2)
                tiles(3, ((bdU, stacked(rb_c)),), "y_mm", start=False, stop=True)

            pe.wait_ge(sig("bd_zero"), 14)
            with pe.Fori(0, SEQ // RD - 1) as n:
                chunk(n)
            chunk(SEQ // RD - 1)
            pe.wait_ge(sig("y_out"), seen("y_out") + SEQ // RD)
            for m in range(DT):
                if m > 1:
                    pe.wait_ge(sig("centered"), m - 1)
                nc.tensor.matmul(bank[2 + m % 2][:, :], c("blk"), kk_a[:, m, :], start=True, stop=True
                                 ).then_inc(sig("mean_mm"), 1)
            for m in range(DT):
                pe.wait_ge(sig("rk_done"), m + 1)
                if m > 1:
                    pe.wait_ge(sig("bonus"), m - 1)
                nc.tensor.matmul(bank[(0, 1)[m % 2]][:, :], c("blk"), r_a[:, m, :], start=True, stop=True
                                 ).then_inc(sig("bonus_mm"), 1)
                pe.wait_ge(sig("dev_sq"), m + 1)
                if m > 1:
                    pe.wait_ge(sig("dev_root"), m - 1)
                nc.tensor.matmul(bank[4 + m % 2][:, :], c("blk"), ht[:, m, :], start=True, stop=True
                                 ).then_inc(sig("dev_mm"), 1)
            pe.wait_ge(sig("gated"), DT)
            with pe.Fori(0, DT // 4) as it:
                for j in range(4):
                    k8_product(pe, it, 4, j, k_a_)
            skip("pe", DT)
            norm_sum(3)
            gate_ups(3)
            downs(2 + FT)
            norm_sum(4)


def constants():
    import numpy as np
    p, q = np.arange(P)[:, None], np.arange(P)[None, :]
    r = np.arange(RD)[None, :]
    a = np.zeros((P, NCONST), np.float32)

    def put(name, value):
        o, w = COLS[name]
        a[:, o:o + w] = value

    put("ident", p == q)
    put("flip", p + q == P - 1)
    put("le", p <= q)
    put("gt", p > q)
    put("ones", 1.0)
    put("blk", p // RD == q // RD)
    put("lvl", np.concatenate([(p // b % 2 == 0) & (q // b == p // b + 1) for b in (1, 2, 4, 8, 16, 32, 64)], 1))
    pr = p % RD
    put("lvl64", np.concatenate([(pr // b % 2 == 0) & (r // b == pr // b + 1) for b in (1, 2, 4, 8, 16, 32)], 1))
    put("le64", pr <= r)
    put("lt64", pr < r)
    put("gt64", pr > r)
    put("id64", pr == r)
    put("eps", np.array([[EPS, 1e-12, 64e-5, GD * EPS]], np.float32))
    dist = 511 - np.arange(BIAS_LEN)
    n = np.maximum(dist, 0)
    large = 16 + (np.log(np.maximum(n, 1).astype(np.float32) / np.float32(16)) / np.float32(np.log(128 / 16))
                  * np.float32(16)).astype(np.int32)
    bucket = np.where(n < 16, n, np.minimum(large, 31))
    onehot = np.zeros((33, BIAS_LEN), np.float32)
    onehot[bucket, np.arange(BIAS_LEN)] = dist >= 0
    onehot[32] = dist < 0
    return a, onehot


def kernel(**inputs):
    import numpy as np
    import concourse.bacc as bacc
    from concourse.bass_utils import run_bass_kernel_spmd

    i = {k: np.asarray(v) for k, v in inputs.items()}

    def columns(a):
        return np.ascontiguousarray(a.reshape(-1, P).T)

    def units(w):
        k, n = w.shape
        return w.reshape(k // P, P, n // P, P).transpose(2, 1, 0, 3).reshape(n // P, P, k)

    cpack, onehot = constants()
    w_in = i["e_w_in"][0]
    cut = np.cumsum([0] + [512] * 4 + [4] * 2 + [512] + [128] * 6 + [24])
    part = [w_in[:, a:b] for a, b in zip(cut[:-1], cut[1:])]
    nq = part[6].reshape(D_MODEL, 2, 4, ND).transpose(0, 2, 1, 3).reshape(D_MODEL, 512)
    w_in_units = units(np.concatenate(part[0:4] + [nq] + part[7:13], 1))
    gate = part[13].reshape(D_MODEL, NH, 3)[:, :, [1, 2, 0]].reshape(D_MODEL, 24)
    small = np.concatenate([part[4], part[5], gate], 1)

    def compress(w):
        w = w.reshape(2, 8, P, 2, P)
        return w.transpose(3, 0, 2, 1, 4).reshape(4, P, UNIT)

    def pad_unit(w, rows=P):
        out = np.zeros((1, P, UNIT), np.float32)
        out[0, :w.shape[0], :w.shape[1]] = w
        return out

    def interleave(a, b):
        return np.stack([a, b], 1).reshape(-1, P, UNIT)

    def k_major(w):
        out = np.zeros((P, DT, P), np.float32)
        out[:, :, :w.shape[1]] = w.reshape(DT, P, -1).transpose(1, 0, 2)
        return out.reshape(1, P, UNIT)

    g1 = i["o_g1"][0]
    wk8 = np.concatenate([
        w_in_units, compress(i["e_cmpk_w1"][0]), compress(i["e_cmpv_w1"][0]), units(i["e_w_out"][0]),
        interleave(units(i["e_ffn_gate"][0]), units(i["e_ffn_up"][0])),
        k_major(g1[:, 0:128]), k_major(g1[:, 128:160]), pad_unit(i["o_g2"][0][0:128]), pad_unit(i["o_g2"][0][128:160]),
        k_major(np.concatenate([i["o_w1"][0], i["o_a1"][0]], 1)),
        pad_unit(np.concatenate([i["o_w2"][0], i["o_a2"][0]], 0)),
        units(i["o_w_v"][0]), units(i["o_w_r"][0]), units(i["o_w_k"][0]), units(i["o_w_o"][0]),
        interleave(units(i["o_ffn_gate"][0]), units(i["o_ffn_up"][0]))], 0)
    wdn = np.concatenate([units(i["e_ffn_down"][0]), units(i["o_ffn_down"][0])], 0)

    tbl = np.zeros((P, NH), np.float32)
    tbl[0:32] = i["rel_bias"]
    tbl[32] = NEG
    vals = {
        "n0": columns(i["e_attn_norm"][0]), "n1": columns(i["e_ffn_norm"][0]), "n2": columns(i["o_attn_norm"][0]),
        "n3": columns(i["o_ffn_norm"][0]), "n4": columns(i["final_norm"]), "mu": columns(i["o_mu"][0]),
        "w0": columns(i["o_w0"][0]), "a0": columns(i["o_a0"][0]), "k_k": columns(i["o_k_k"][0]),
        "k_a": columns(i["o_k_a"][0]), "r_k": columns(i["o_r_k"][0].reshape(-1)), "lnw": columns(i["o_lnx_w"][0]),
        "lnb": columns(i["o_lnx_b"][0]),
        "conv": i["e_conv_w"][0].reshape(4, 12, P).transpose(2, 1, 0).reshape(P, 48),
        "gnorm": columns(i["e_gdn_norm"][0]), "alog": np.tile(i["e_a_log"][0], (P, 1)),
        "dtb": np.tile(i["e_dt_bias"][0], (P, 1)),
        "wsmall": small.reshape(DT, P, 32).transpose(1, 0, 2).reshape(P, 256),
        "cw2": np.stack([i[f"e_cmp{t}_w2"][0].reshape(2, P, ND) for t in "kv"]).transpose(2, 0, 1, 3).reshape(P, 256),
        "pe": np.stack([i[f"e_cmp{t}_pe"][0].reshape(16, P) for t in "kv"]).transpose(2, 0, 1).reshape(P, 32),
        "tbl": tbl}
    vpack = np.concatenate([vals[k].reshape(P, -1) for k in VCOLS], 1)
    assert vpack.shape[1] == NVEC
    xT = i["x"][0].T.reshape(DT, P, SEQ).transpose(1, 0, 2)

    nc = bacc.Bacc("TRN2", target_bir_lowering=False, num_devices=1)
    feeds = {"xT": xT, "cpack": cpack, "vpack": vpack, "onehot": onehot, "wk8": wk8, "wdn": wdn}
    feeds = {k: np.ascontiguousarray(a) for k, a in feeds.items()}
    aps = {k: nc.dram_tensor(k, a.shape, F32, kind="ExternalInput").ap() for k, a in feeds.items()}
    aps["scratch"] = nc.dram_tensor("scratch", (NH, BIAS_LEN), F32, kind="Internal").ap()
    aps["g_spill"] = nc.dram_tensor("g_spill", (P, DT, SEQ), F32, kind="Internal").ap()
    aps["outT"] = nc.dram_tensor("outT", (P, DT, SEQ), F32, kind="ExternalOutput").ap()
    build(nc, **aps)
    r = run_bass_kernel_spmd(nc, [feeds], core_ids=[0])
    return np.ascontiguousarray(r.results[0]["outT"].transpose(2, 1, 0)).reshape(1, SEQ, D_MODEL)
```

```python
import math
from contextlib import ExitStack

import concourse.bass as bass
from concourse import mybir

F32 = mybir.dt.float32
F32R = mybir.dt.float32r
ALU = mybir.AluOpType
ACT = mybir.ActivationFunctionType

P = 128
SEQ = 512
D_MODEL = 1024
DT = D_MODEL // P
D_FF = 2816
FT = D_FF // P
EPS = 1e-6
GH, GD = 4, 128
CHUNK = 128
NCHUNK = SEQ // CHUNK
NH, ND = 8, 64
CMP_LEN, CMP_STRIDE = 32, 16
NCMP = SEQ // CMP_STRIDE - CMP_LEN // CMP_STRIDE + 1
RD = 64
EPITCH = SEQ // RD * (RD + 1)
UNIT = DT * P
IN_UNITS = 26
PITCH = SEQ + 4
HD = 4
BIAS_LEN = 640
NEG = -1e30
DECAY = math.exp(-0.5)

COLS, n = {}, 0
for _name, _w in (("ident", P), ("le", P), ("gt", P), ("ones", P), ("blk", P), ("flip", P),
                  ("lvl", 7 * P), ("lvl64", 6 * RD), ("le64", RD), ("lt64", RD), ("gt64", RD),
                  ("id64", RD), ("eps", 4), ("tile_in", 15), ("head_in", 30)):
    COLS[_name] = (n, _w)
    n += _w
NCONST = n
VCOLS, n = {}, 0
for _name, _w in (("n0", 8), ("n1", 8), ("n2", 8), ("n3", 8), ("n4", 8), ("mu", 48), ("w0", 8),
                  ("a0", 8), ("k_k", 8), ("k_a", 8), ("r_k", 8), ("lnw", 8), ("lnb", 8),
                  ("conv", 48), ("gnorm", 1), ("alog", 4), ("dtb", 4), ("wsmall", 256),
                  ("cw2", 256), ("pe", 32), ("tbl", 8)):
    VCOLS[_name] = (n, _w)
    n += _w
NVEC = n
del n


class Turns:

    def __init__(self, n):
        self.n, self.pos, self.used = n, 0, [0] * n

    def at(self, j, it=0, per=0):
        s = (self.pos + j) % self.n
        return s, self.used[s] + it * (per // self.n) + j // self.n

    def advance(self, m):
        for j in range(m):
            self.used[(self.pos + j) % self.n] += 1
        self.pos = (self.pos + m) % self.n


def build(nc, xT, cpack, vpack, onehot, wk8, wdn, scratch, g_spill, outT):
    ctx = ExitStack()
    sems = {}

    carried_on = {
        "z_out": ("qt_done", 28), "xt_sub": ("x_step", 52), "x_sub": ("qk_done", 4), "xtm": ("vtok2_mm", 4),
        "m_mm": ("kk_mm", 4), "k_mm": ("qk_mm", 4), "rb_mm": ("ktok_mm", 4), "bt_mm": ("g_sum_mm", 1),
        "kt_mm": ("ks_mm", 4), "vt_mm": ("vnew_mm", 4), "g_mm": ("o_mm", 4), "q_mm": ("qt_mm", 28),
        "xmm": ("xx_mm", 28), "u_mm": ("st_mm", 4), "z_mm": ("decay_mm", 12), "y_mm": ("bias_mm", 8),
        "mean_mm": ("otok_turned", 4), "bonus_mm": ("score_mm", 96), "dev_mm": ("turned", 96), "ksum_mm": ("qk_sum", 9),
        "wa_mm": ("o_sum", 5), "lora_mm": ("vtok_mm", 2), "bda": ("decay_row", 4), "bdb": ("decay_low", 4),
        "tok_out": ("decay_up", 4), "g_out": ("ktok_done", 4), "bdq": ("vnew_done", 4), "bdxt": ("turn_copied", 96),
        "bdu": ("exp_done", 96), "bdz": ("hid_done", 4), "y_out": ("blocks_done", 10),
        "rk_done": ("m_done", 4), "centered": ("rhs_done", 4), "bonus": ("up_masked", 4), "y_read": ("rhs_step", 4),
        "gated": ("st_step", 4), "key_mod": ("mstep", 8), "dev_sq": ("qk_sq", 2), "dev_root": ("qk_root", 1),
        "k_out": ("o_sq", 1), "k_recip": ("g_pos", 1), "gn_recip": ("g_done", 1), "kn_done": ("st_zero", 2),
        "gn_done": ("rg_step", 12),
    }

    def seen(name):
        return carried_on[name][1]

    def sig(name):
        name = carried_on.get(name, (name,))[0]
        if name not in sems:
            sems[name] = ctx.enter_context(nc.semaphore(name))
        return sems[name]

    places, twins = {}, []

    def sb(name, cols):
        places[name] = -(-nc.sbuf_base // 32) * 32
        return ctx.enter_context(nc.sbuf_tensor(name, [P, cols], F32))

    def twin(name, start, cols, dtype=F32R):
        t = nc.alloc_sbuf_tensor_at(f"{name}_{start}_{cols}", [P, cols], dtype, offset=places[name] + 4 * start)
        if dtype == F32R:
            twins.append((name, start, cols, t[:, :].tensor))
        return t

    def rounded(a):
        end = a.offset + 1 + sum((n - 1) * step for step, n in a.ap[1:])
        for name, start, cols, t in twins:
            if a.tensor.name == name and start <= a.offset and end <= start + cols:
                return bass.AP(t, a.offset - start, [(cols, P), *a.ap[1:]])
        raise KeyError(a.tensor.name)

    with ctx:
        x = sb("x", DT * SEQ)[:, :].rearrange("p (m t) -> p m t", m=DT)
        h_t = sb("h", DT * PITCH)
        h = h_t[:, :].rearrange("p (m t) -> p m t", m=DT)
        ht = h[:, :, HD:HD + SEQ]
        wring = sb("wring", 4 * UNIT)[:, :].rearrange("p (s k) -> p s k", s=4)
        dring_t = sb("dring", 2 * D_FF)
        dring = dring_t[:, :].rearrange("p (s k) -> p s k", s=2)
        con = sb("con", NCONST)
        vec = sb("vec", NVEC)
        norm_t_flat = sb("norm_t", 2 * SEQ)[:, :]
        norm_t = norm_t_flat.rearrange("p (s t) -> p s t", s=2)
        ARENA = 31000
        arena = sb("arena", ARENA)
        bank = [ctx.enter_context(nc.psum_tensor(f"bank{i}", [P, 512], F32)) for i in range(8)]

        def c(name):
            o, w = COLS[name]
            return con[:, o:o + w]

        def v(name):
            o, w = VCOLS[name]
            return vec[:, o:o + w]

        class Carve:
            def __init__(self, base, t=arena, top=ARENA):
                self.at, self.t, self.top = base, t, top

            def __call__(self, cols, shape=None):
                a = self.t[:, self.at:self.at + cols]
                self.at += cols
                assert self.at <= self.top, self.at
                return a if shape is None else a.rearrange("p (a b) -> p a b", a=shape)

        L0 = Carve(0)
        proj = L0(IN_UNITS * SEQ, IN_UNITS)
        bias = L0(NH * SEQ, NH)
        otok = L0(4 * NH * ND, 4)
        tok = L0(P, 4)
        gates_flat = L0(96)
        gates = gates_flat.rearrange("p (q n) -> p q n", q=4)
        g_col, beta, nbeg, gtmp, gaux = (L0(16) for _ in range(5))
        eg, ea = L0(32), L0(4)
        mark = L0.at
        N = Carve(mark)
        BLK = 2 * NCMP + 1
        kst = [N(2 * SEQ)[:, 0:16 * BLK].rearrange("p (a b) -> p a b", b=BLK) for _ in range(2)]
        hid = N(4 * 62, 4)
        pebias = N(4)
        kcT = N(32)
        vcT = N(P)
        vtok = N(2 * SEQ, 8)
        q_st = N(SEQ)
        probs = [N(SEQ) for _ in range(2)]
        probsT = [N(SEQ) for _ in range(2)]
        nmx = [N(2) for _ in range(2)]
        sums, rg = N(24), N(24)
        oacc = [N(SEQ) for _ in range(3)]
        conv = [N(SEQ) for _ in range(2)]
        bias_st = N(2 * SEQ, 2)
        B = Carve(mark + 4 * SEQ)
        oh = B(BIAS_LEN)
        brow = B(BIAS_LEN)
        shifted = B(NH * SEQ, NH)
        G = Carve(mark)
        (k_st, qst, v_st, gbc, leg, gtg, egr, dlow, dup, mlow, qk, xi, xit, qt_, ktok, vb, rr, vn,
         st) = (G(SEQ, GH) for _ in range(19))
        tile_out = norm_t_flat[0:8, :]
        gtg_flat, leg_flat = (a.rearrange("p a b -> p (a b)") for a in (gtg, leg))
        rn0 = bias
        F = Carve(0)
        hid_lo, hid_hi, sil = F(FT * SEQ, FT), F(FT * SEQ, FT), F(2 * SEQ, 2)
        hid_t = twin("arena", 0, FT * SEQ, F32)[:, :].rearrange("p (m t) -> p m t", m=FT)
        twin("arena", 0, FT * SEQ)
        twin("arena", FT * SEQ, FT * SEQ)
        hid_lo_r, hid_hi_r = rounded(hid_lo), rounded(hid_hi)
        F = Carve(6 * DT * SEQ + 64)
        rhs_hi = F(DT * SEQ, DT)
        ffn_wh = [F(UNIT) for _ in range(2)]
        dhi = Carve(6 * DT * SEQ + 64)(2 * D_FF, 2)
        in_hi, in_wh = bias, [otok[:, 2 * i:2 * i + 2, :].rearrange("p a b -> p (a b)") for i in range(2)]
        in_lo = dring_t[:, 0:DT * SEQ].rearrange("p (m t) -> p m t", m=DT)
        R = Carve(0)
        g_a = R(DT * SEQ, DT)
        e_flat = R(DT * EPITCH)
        e_a = e_flat.rearrange("p (m t) -> p m t", m=DT)
        e_c = e_flat.rearrange("p (m c t) -> p m c t", m=DT, c=SEQ // RD)
        a_a, v_a, r_a, k_a_ = (R(DT * SEQ, DT) for _ in range(4))
        assert R.at == 6 * DT * SEQ + DT * (EPITCH - SEQ)
        mixb = R(DT * SEQ, DT)
        left = R.at
        L = Carve(left)
        padmask, hid_g1, hid_g2, hid_wa = L(EPITCH), L(SEQ), L(SEQ), L(SEQ)
        D = Carve(0, dring_t, 2 * D_FF)
        mixa = D(DT * SEQ, DT)
        key_t = dring_t[:, DT * EPITCH:DT * EPITCH + 2 * SEQ].rearrange("p (s t) -> p s t", s=2)
        kk_a = mixa
        ei_flat = dring_t[:, 0:DT * EPITCH]
        ei_a = ei_flat.rearrange("p (m t) -> p m t", m=DT)
        ei_c = ei_flat.rearrange("p (m c t) -> p m c t", m=DT, c=SEQ // RD)
        G_ = Carve(0)
        bdU, bdX, bdQ = (G_(UNIT, DT) for _ in range(3))
        ry_c = G_(SEQ, DT)
        E_ = Carve(DT * SEQ)
        bdA, bdB, bdK, bdM = (E_(UNIT, DT) for _ in range(4))
        M_ = Carve(left - DT * SEQ)
        bdAK, bdBt, bdKt, bdVt = (M_(UNIT, DT) for _ in range(4))
        H_ = Carve(0, h_t, DT * PITCH)
        bdV, bdZ = (H_(UNIT, DT) for _ in range(2))
        rb_c, rk_c, vt_c, x_c = (H_(SEQ, DT) for _ in range(4))
        xt_c, q_c, u_c = (D(SEQ, DT) for _ in range(3))
        C_ = Carve(left)
        ar_c = C_(UNIT, DT)
        z_c, g_c = C_(SEQ, DT), C_(SEQ, DT)
        p_c = Carve(left + EPITCH + 3 * SEQ)(64, DT)
        b_c = norm_t[:, 0, :].rearrange("p (m t) -> p m t", m=DT)
        bdXT = bdQ
        rsd = e_flat[:, 0:SEQ]
        v_hi, r_hi = r_a, g_a
        rwkv_wh = [norm_t_flat, arena[:, left + EPITCH:left + EPITCH + UNIT]]
        twin("wring", 0, 4 * UNIT)
        twin("dring", 0, 2 * D_FF)
        twin("h", 0, DT * PITCH)
        twin("norm_t", 0, 2 * SEQ)
        twin("arena", 5 * DT * SEQ + 64, DT * SEQ)
        twin("arena", 6 * DT * SEQ + 64, ARENA - (6 * DT * SEQ + 64))
        kn = g_a
        head_out = con[0:16, COLS["flip"][0]:COLS["flip"][0] + D_MODEL]
        key_rows, dev_rows = hid_wa[0:16, :], rsd[0:16, :]

        def eps(i):
            o = COLS["eps"][0] + i
            return con[:, o:o + 1]

        def width(u):
            qt = u // 3 % 4
            return P * (qt + 1) if u % 3 < 2 else P // CMP_STRIDE * qt + 7

        PB = (0, 1, 6, 7)
        rings = {e: (Turns(4), Turns(2), Turns(4)) for e in ("sp", "pe", "act", "dve")}

        def k8_product(pe, it, per, j, rhs, gate=None):
            ring, _, banks = rings["pe"]
            s, u = ring.at(j, it, per)
            b, w = banks.at(j, it, per)
            b = PB[b]
            pe.wait_ge(sig(f"w_full{s}"), (u + 1) * 16)
            pe.wait_ge(sig(f"bank_free{b}"), w + 1)
            for k in range(DT):
                if gate:
                    pe.wait_ge(sig(gate[0]), gate[1] + k + 1)
                mm = nc.tensor.matmul(bank[b][:, :], wring[:, s, k * P:(k + 1) * P], rhs[:, k, :],
                                      start=k == 0, stop=k == DT - 1)
            mm.then_inc(sig(f"unit_done{s}"), 1)

        split = {e: [0, 0, 0] for e in rings}

        def split_high(sem, dst, src):
            nc.scalar.activation(dst, src, ACT.Copy).then_inc(sig(sem), 1)

        def split_low(sem, a, high, dst):
            nc.vector.tensor_tensor(dst, a, high, ALU.subtract).then_inc(sig(sem), 1)

        def weights_high(act, it, per, j, wh):
            s, u = rings["act"][0].at(j, it, per)
            act.wait_ge(sig(f"w_full{s}"), (u + 1) * 16)
            split_high("w_hi", rounded(wh[s % 2]), wring[:, s, :])

        def weights_low(dve, it, per, j, wh):
            s, _ = rings["dve"][0].at(j, it, per)
            dve.wait_ge(sig("w_hi"), split["dve"][0] + it * per + j + 1)
            split_low("w_lo", wring[:, s, :], rounded(wh[s % 2]), rounded(wring[:, s, :]))

        def unit_through(eng, who, it, per, j):
            s, u = rings[who][0].at(j, it, per)
            eng.wait_ge(sig(f"unit_done{s}"), u + 1)

        def pass_units(who, n, banks=True):
            rings[who][0].advance(n)
            if banks:
                rings[who][2].advance(n)
            split[who][0] += n

        def split_product(pe, it, per, j, hi, lo, wh, order=range(DT)):
            ring, _, banks = rings["pe"]
            s, _ = ring.at(j, it, per)
            b, w = banks.at(j, it, per)
            b = PB[b]
            pe.wait_ge(sig("w_lo"), split["pe"][0] + it * per + j + 1)
            pe.wait_ge(sig(f"bank_free{b}"), w + 1)
            for i, k in enumerate(order):
                pe.wait_ge(sig("rhs_lo"), split["pe"][1] + i + 1)
                w_k = slice(k * P, (k + 1) * P)
                for n, (a, m) in enumerate(((wh[s % 2], hi), (wring[:, s, :], hi), (wh[s % 2], lo))):
                    mm = nc.tensor.matmul(bank[b][:, :], rounded(a[:, w_k]), rounded(m[:, k, :]),
                                          start=i == 0 and n == 0, stop=i == DT - 1 and n == 2)
            mm.then_inc(sig(f"unit_done{s}"), 1)

        PIECES = ((0, 8), (8, 16), (16, FT))

        def down_high(act, m):
            s, u = rings["act"][1].at(m)
            act.wait_ge(sig(f"d_full{s}"), (u + 1) * 16)
            for a, b in PIECES:
                split_high("d_hi", rounded(dhi[:, s, P * a:P * b]), dring[:, s, P * a:P * b])

        def down_low(dve, m):
            s, _ = rings["dve"][1].at(m)
            for i, (a, b) in enumerate(PIECES):
                dve.wait_ge(sig("d_hi"), split["dve"][2] + 3 * m + i + 1)
                w = dring[:, s, P * a:P * b]
                split_low("d_lo", w, rounded(dhi[:, s, P * a:P * b]), rounded(w))

        def k8_result(eng, who, it, per, j):
            ring, _, banks = rings[who]
            s, u = ring.at(j, it, per)
            eng.wait_ge(sig(f"unit_done{s}"), u + 1)
            return PB[banks.at(j, it, per)[0]]

        def k8_result_bank(who):
            banks = rings[who][2]
            b = PB[banks.at(0)[0]]
            banks.advance(1)
            return b

        def down_product(pe, it, per, j, gate):
            _, ring, banks = rings["pe"]
            s, _ = ring.at(j, it, per)
            b, w = banks.at(j, it, per)
            pe.wait_ge(sig(f"bank_free{PB[b]}"), w + 1)
            starts = [a for a, _ in PIECES]
            for k in range(FT):
                if k in starts:
                    pe.wait_ge(sig("d_lo"), split["pe"][2] + 3 * (it * per + j) + starts.index(k) + 1)
                pe.wait_ge(sig("ff_lo"), gate + k + 1)
                for n, (a, m) in enumerate(((dhi, hid_hi), (dring, hid_hi), (dhi, hid_lo))):
                    mm = nc.tensor.matmul(bank[PB[b]][:, :], rounded(a[:, s, k * P:(k + 1) * P]), rounded(m[:, k, :]),
                                          start=k == 0 and n == 0, stop=k == FT - 1 and n == 2)
            mm.then_inc(sig(f"down_done{s}"), 1)

        def skip(who, units, downs=0):
            ring, dr, banks = rings[who]
            ring.advance(units)
            dr.advance(downs)
            banks.advance(units + downs)


        block = ctx.enter_context(nc.Block())

        @block.sync
        def _(sp):
            sp.dma_start(x[:, :, :], xT).then_inc(sig("x_loaded"), 16)
            sp.dma_start(con[:, :], cpack).then_inc(sig("con_loaded"), 16)
            sp.dma_start(vec[:, :], vpack).then_inc(sig("vec_loaded"), 16)
            sp.dma_start(oh[0:33, :], onehot).then_inc(sig("onehot_loaded"), 16)
            ring, downs, _ = rings["sp"]
            loaded = [0, 0]

            def load_units(count):
                first = loaded[0]

                def body(it, per, m):
                    for j in range(m):
                        s, u = ring.at(j, it, per)
                        sp.wait_ge(sig(f"unit_done{s}"), u)
                        sp.dma_start(wring[:, s, :], wk8[bass.ds(it * per + first + j, 1), :, :]
                                     .rearrange("a p k -> p (a k)")).then_inc(sig(f"w_full{s}"), 16)

                if count // 4 > 1:
                    with sp.Fori(0, count // 4) as it:
                        body(it, 4, 4)
                    ring.advance(count // 4 * 4)
                    first += count // 4 * 4
                    count, done = count % 4, count // 4 * 4
                else:
                    done = 0
                body(0, 0, count)
                ring.advance(count)
                loaded[0] = first + count

            for j in range(4):
                sp.dma_start(wring[:, j, :], wk8[j, :, :]).then_inc(sig(f"w_full{j}"), 16)
            ring.advance(4)
            loaded[0] = 4
            def load_down(m):
                s, u = downs.at(0)
                if u:
                    sp.wait_ge(sig(f"down_done{s}"), u)
                sp.dma_start(dring[:, s, :], wdn[m, :, :]).then_inc(sig(f"d_full{s}"), 16)
                downs.advance(1)

            load_units(IN_UNITS + 8 + 8 + 40 - 4)
            load_down(0)
            load_down(1)
            load_units(4 + 4)
            for m in range(2, DT):
                load_down(m)
            load_units(2 + 32 + 40)
            sp.wait_ge(sig("y_read"), seen("y_read") + 8)
            load_down(8)
            load_down(9)
            load_units(4)
            for m in range(DT + 2, 2 * DT):
                load_down(m)
            for i in range(2):
                sp.wait_ge(sig("h_done"), 32 + 4 * i + 4)
                sp.dma_start(outT[:, 4 * i:4 * i + 4, :], ht[:, 4 * i:4 * i + 4, :]).then_inc(sig("stored"), 16)
            sp.wait_ge(sig("stored"), 32)

        @block.gpsimd
        def _(pool):
            pool.wait_ge(sig("bias_row"), 2)
            pool.dma_start(scratch, brow[0:NH, :]).then_inc(sig("row_stored"), 16)
            pool.wait_ge(sig("row_stored"), 16)
            pool.dma_start(shifted[:, :, :], bass.AP(scratch.tensor, 0, [[1, P], [BIAS_LEN, NH], [1, SEQ]])
                           ).then_inc(sig("shifted_loaded"), 16)
            pool.wait_ge(sig("g_done"), 1)
            def every_head(a):
                return a.unsqueeze(1).broadcast_to([P, GH, P])
            with pool.Fori(0, NCHUNK) as n:
                pool.wait_ge(sig("chunk_done"), n + 1)
                g_n = g_col[:, bass.ds(4 * n, 4)].unsqueeze(2).broadcast_to([P, GH, P])
                for dst, src in ((gbc, c("ones")), (gtg, c("gt")), (leg, c("le"))):
                    nc.gpsimd.tensor_tensor(dst, every_head(src), g_n, ALU.mult).then_inc(sig("g_spread"), 1)
                pool.wait_ge(sig("qk_mm"), n + 1)
                pool.wait_ge(sig("decay_row"), n + 1)
                nc.gpsimd.tensor_tensor(qst, qst, egr, ALU.mult).then_inc(sig("q_decayed"), 1)
                pool.wait_ge(sig("ktok_done"), n + 1)
                nc.gpsimd.tensor_tensor(ktok, ktok, eg[:, bass.ds(16 + 4 * n, 4)].unsqueeze(2)
                                        .broadcast_to([P, GH, P]), ALU.mult).then_inc(sig("k_decayed"), 1)

            pool.wait_ge(sig("lora_out"), DT)
            pool.dma_start(g_spill, g_a[:, :, :]).then_inc(sig("g_stored"), 16)
            pool.wait_ge(sig("g_stored"), 16)
            pool.wait_ge(sig("k_out"), seen("k_out") + 2 * DT)
            for a in (bdAK, bdBt, bdKt, bdVt, bdV, bdZ, z_c):
                nc.gpsimd.memset(a, 0.0).then_inc(sig("bd_zero"), 1)
            pool.wait_ge(sig("scan_ready"), 1)
            for a in (bdU, bdX, bdQ, bdK):
                nc.gpsimd.memset(a, 0.0).then_inc(sig("bd_zero"), 1)

            def chunk(n):
                for lv in range(5):
                    for g in range(2):
                        pool.wait_ge(sig("x_sub"), seen("x_sub") + n * 10 + 2 * lv + g + 1)
                        pool.sem_inc(sig("carrier"), 1)
                        for e in range(2):
                            nc.gpsimd.tensor_copy(bdX[RD * e:RD * e + RD, 4 * g:4 * g + 4, RD * e:RD * e + RD],
                                                  x_c[RD * e:RD * e + RD, 4 * g:4 * g + 4, :]).then_inc(sig("bdx"), 1)

            with pool.Fori(0, SEQ // RD - 1) as n:
                chunk(n)
            chunk(SEQ // RD - 1)
            pool.wait_ge(sig("y_out"), seen("y_out") + SEQ // RD)
            pool.dma_start(g_a[:, :, :], g_spill).then_inc(sig("g_loaded"), 16)


        @block.scalar
        def _(act):
            for b in PB:
                act.sem_inc(sig(f"bank_free{b}"), 1)
            act.sem_inc(sig("silu_done"), 2)
            act.sem_inc(sig("o_copied"), 1)
            act.wait_ge(sig("x_loaded"), 16)
            act.wait_ge(sig("con_loaded"), 16)

            def norm(r):
                nc.scalar.activation(ht[:, 0:4, :], x[:, 0:4, :], ACT.Square).then_inc(sig("sq_a"), 1)
                act.wait_ge(sig("sum_done"), r + 1)
                nc.scalar.activation(norm_t[:, 0, :], bank[2][:, :], ACT.Sqrt, bias=eps(0),
                                     scale=1.0 / D_MODEL).then_inc(sig("rms_done"), 1)

            def rhs_highs(src, dst, sem, base, order=range(DT)):
                for i, k in enumerate(order):
                    if sem:
                        act.wait_ge(sig(sem), base + i + 1)
                    split_high("rhs_hi", rounded(dst[:, k, :]), src[:, k, :])

            norm(0)
            weights_high(act, 0, 0, 0, in_wh)
            weights_high(act, 0, 0, 1, in_wh)
            rhs_highs(ht, in_hi, "h_done", 0)
            with act.Fori(0, 3) as it:
                def silu(j):
                    act.wait_ge(sig("conv_done"), it * 4 + j + 1)
                    nc.scalar.activation(proj[:, bass.ds(it * 4 + j, 1), :].rearrange("p a t -> p (a t)"),
                                         conv[j % 2], ACT.Silu).then_inc(sig("silu_done"), 1)

                for j in range(4):
                    unit_through(act, "act", it, 4, j)
                    weights_high(act, it, 4, j + 2, in_wh)
                    if j:
                        silu(j - 1)
                silu(3)
            pass_units("act", 12)
            for i in range(12, IN_UNITS):
                b = k8_result(act, "act", 0, 0, 0)
                if i + 2 < IN_UNITS:
                    weights_high(act, 0, 0, 2, in_wh)
                pass_units("act", 1)
                fn, scale = (ACT.Silu, 1.0) if i < 16 else (ACT.Copy, ND ** -0.5 if i < 20 else 1.0)
                nc.scalar.activation(proj[:, i, :], bank[b][:, :], fn, scale=scale
                                     ).then_inc(sig("proj_done"), 1)
                act.wait_ge(sig("proj_done"), i - 11)
                act.sem_inc(sig(f"bank_free{b}"), 1)
            act.wait_ge(sig("small_done"), 1)
            nc.scalar.activation(tok[:, :, :], bank[2][:, 0:P].rearrange("p (a b) -> p a b", a=4),
                                 ACT.Copy).then_inc(sig("tok_done"), 1)
            act.wait_ge(sig("vec_loaded"), 16)
            for i in range(2):
                for g in range(2):
                    for d in range(2):
                        first = proj[64 * g:64 * g + 64, 20 + i, d:d + 1]
                        src = bass.AP(first.tensor, first.offset, [first.ap[0], (2, 16), (CMP_STRIDE, NCMP)])
                        nc.scalar.activation(kst[i][64 * d:64 * d + 64, :, NCMP * g:NCMP * g + NCMP], src, ACT.Copy
                                             ).then_inc(sig("blocks_done"), 1)
                nc.scalar.activation(kst[i][:, :, BLK - 1], v("pe")[:, 16 * i:16 * i + 16], ACT.Copy
                                     ).then_inc(sig("blocks_done"), 1)
            for i in range(NH):
                act.wait_ge(sig("bias_mm"), i + 1)
                nc.scalar.activation(bias[:, i, :], bank[4 + i % 4][:, :], ACT.Copy).then_inc(sig("bias_done"), 1)
            rings["act"][0].advance(8)
            ring = rings["act"][0]
            for s in range(4):
                act.wait_ge(sig(f"unit_done{s}"), ring.used[s])
            nc.scalar.activation(pebias, bank[2][:, 2 * NCMP:256:64], ACT.Copy).then_inc(sig("pebias_done"), 1)
            act.wait_ge(sig("pebias_done"), 1)
            for i in range(4):
                nc.scalar.activation(hid[:, i, :], bank[2][:, 64 * i:64 * i + 62], ACT.Silu,
                                     bias=pebias[:, i:i + 1]).then_inc(sig("hid_done"), 1)
            for i in range(2):
                act.wait_ge(sig("vtok_mm"), i + 1)
                nc.scalar.activation(vtok[:, 4 * i:4 * i + 4, :], bank[6 + i][:, :].rearrange("p (a b) -> p a b", a=4),
                                     ACT.Copy).then_inc(sig("vtok_done"), 1)
            act.wait_ge(sig("tok_done"), 1)
            nc.scalar.activation(gates[:, :, :], tok[:, :, 8:32], ACT.Sigmoid).then_inc(sig("gates_done"), 1)
            nc.scalar.activation(beta.rearrange("p (a b) -> p a b", a=4), tok[:, :, 0:4], ACT.Sigmoid
                                 ).then_inc(sig("gates_done"), 1)
            with act.Fori(0, 4) as j:
                def exp_(u):
                    act.wait_ge(sig("scored"), j * 24 + u + 3)
                    w = width(u)
                    nc.scalar.activation(probs[u % 2][:, 0:w], probs[u % 2][:, 0:w], ACT.Exp,
                                         bias=nmx[u % 2][:, 1:2], accum_out=sums[:, u:u + 1]
                                         ).then_inc(sig("exp_done"), 1)

                def evac(u):
                    act.wait_ge(sig("turned"), j * 24 + u + 1)
                    w, r = (P, width(u)) if u % 3 == 2 else (width(u), P)
                    nc.scalar.activation(probsT[u % 2][0:r, 0:w], bank[4][0:r, 0:w], ACT.Copy
                                         ).then_inc(sig("turn_copied"), 1)

                exp_(0)
                for u in range(24):
                    if u < 23:
                        exp_(u + 1)
                    evac(u)
            for i in range(4):
                act.wait_ge(sig("otok_turned"), i + 1)
                nc.scalar.activation(ht[:, 4 + i, :], bank[2 + i][:, :], ACT.Copy).then_inc(sig("mix_nsa"), 1)

            act.wait_ge(sig("g_arg"), 1)
            nc.scalar.activation(gaux, gtmp, ACT.Abs).then_inc(sig("g_step"), 1)
            act.wait_ge(sig("g_step"), 1)
            nc.scalar.activation(gaux, gaux, ACT.Exp, scale=-1.0).then_inc(sig("g_step"), 1)
            nc.scalar.activation(ea, v("alog"), ACT.Exp).then_inc(sig("g_step"), 1)
            act.wait_ge(sig("g_step"), 3)
            nc.scalar.activation(gaux, gaux, ACT.Ln, bias=c("ones")[:, 0:1]).then_inc(sig("g_step"), 1)
            act.wait_ge(sig("pair_done"), 5)
            nc.scalar.activation(rn0[:, 0:4, :], proj[:, 0:4, :], ACT.Square).then_inc(sig("qk_sq"), 1)
            nc.scalar.activation(rn0[:, 4:8, :], proj[:, 4:8, :], ACT.Square).then_inc(sig("qk_sq"), 1)
            act.wait_ge(sig("g_sum_mm"), 1)
            nc.scalar.activation(eg, bank[2][:, 0:32], ACT.Exp).then_inc(sig("eg_done"), 1)
            act.wait_ge(sig("qk_sum"), 1)
            nc.scalar.activation(rn0[0:8, 0, :], bank[4][0:8, :], ACT.Sqrt, bias=eps(0)[0:8, :]
                                 ).then_inc(sig("qk_root"), 1)
            with act.Fori(0, NCHUNK) as n:
                act.wait_ge(sig("decay_mm"), 3 * n + 1)
                nc.scalar.activation(egr, bank[2][:, :].rearrange("p (a b) -> p a b", a=GH), ACT.Exp
                                     ).then_inc(sig("decay_row"), 1)
                act.wait_ge(sig("decay_mm"), 3 * n + 2)
                nc.scalar.activation(dlow, bank[3][:, :].rearrange("p (a b) -> p a b", a=GH), ACT.Exp
                                     ).then_inc(sig("decay_low"), 1)
                act.wait_ge(sig("decay_mm"), 3 * n + 3)
                nc.scalar.activation(dup, bank[4][:, :].rearrange("p (a b) -> p a b", a=GH), ACT.Exp
                                     ).then_inc(sig("decay_up"), 1)
                act.wait_ge(sig("ktok_mm"), n + 1)
                nc.scalar.activation(ktok, bank[7][:, :].rearrange("p (a b) -> p a b", a=GH), ACT.Copy
                                     ).then_inc(sig("ktok_done"), 1)
                act.wait_ge(sig("vnew_mm"), n + 1)
                nc.scalar.activation(vn, bank[7][:, :].rearrange("p (a b) -> p a b", a=GH), ACT.Copy
                                     ).then_inc(sig("vnew_done"), 1)
                act.wait_ge(sig("o_mm"), n + 1)
                nc.scalar.activation(ht[:, 0:4, bass.ds(CHUNK * n, CHUNK)],
                                     bank[2][:, :].rearrange("p (a b) -> p a b", a=GH), ACT.Copy
                                     ).then_inc(sig("o_copied"), 1)
            act.wait_ge(sig("o_copied"), NCHUNK + 1)
            nc.scalar.activation(rn0[:, 0:4, :], ht[:, 0:4, :], ACT.Square).then_inc(sig("o_sq"), 1)
            act.wait_ge(sig("o_sum"), 1)
            nc.scalar.activation(rn0[0:4, 4, :], bank[4][0:4, :], ACT.Sqrt, bias=eps(0)[0:4, :], scale=1.0 / GD
                                 ).then_inc(sig("o_root"), 1)

            def split_units(n):
                for j in range(n):
                    unit_through(act, "act", 0, 0, j)
                    weights_high(act, 0, 0, j + 2, ffn_wh)
                pass_units("act", n)

            def gate_ups(f):
                def turn(it, per, last):
                    for j in range(4):
                        unit_through(act, "act", it, per, j)
                        if not last or j < 2:
                            weights_high(act, it, per, j + 2, ffn_wh)
                        first = f * FT + (FT - 2 if last else 0)
                        if j % 2 == 0:
                            b = PB[rings["act"][2].at(j, it, per)[0]]
                            act.wait_ge(sig("ff_done"), first + it * 2 + j // 2 + 1)
                            nc.scalar.activation(sil[:, j // 2, :], bank[b][:, :], ACT.Silu).then_inc(sig("sil_done"), 1)
                        else:
                            act.wait_ge(sig("ff_done"), first + it * 2 + j // 2 + 3)
                            act.sem_inc(sig("carrier"), 1)
                            p = it * 2 + j // 2
                            if last:
                                src, dst = hid_t[:, FT - 2 + j // 2, :], hid_hi_r[:, FT - 2 + j // 2, :]
                            else:
                                src, dst = (a[:, bass.ds(p, 1), :].rearrange("p a t -> p (a t)") for a in (hid_t, hid_hi_r))
                            split_high("ff_hi", dst, src)

                with act.Fori(0, FT // 2 - 1) as it:
                    turn(it, 4, False)
                pass_units("act", 2 * FT - 4)
                turn(0, 0, True)
                pass_units("act", 4)

            def downs_high():
                unit_through(act, "act", 0, 0, -1)
                for m in range(2):
                    down_high(act, m)
                for m in range(DT - 2):
                    s, u = rings["act"][1].at(m)
                    act.wait_ge(sig(f"down_done{s}"), u + 1)
                    down_high(act, m + 2)
                skip("act", 0, DT)

            act.wait_ge(sig("chunk_done"), NCHUNK + 1)
            weights_high(act, 0, 0, 0, ffn_wh)
            weights_high(act, 0, 0, 1, ffn_wh)
            rhs_highs(ht, rhs_hi, None, 0, range(4, 8))
            rhs_highs(ht, rhs_hi, "mix_gdn", 0, range(4))
            split_units(DT)
            act.wait_ge(sig("x_added"), DT)
            norm(1)
            rhs_highs(ht, rhs_hi, "h_done", DT)
            gate_ups(0)
            downs_high()
            act.wait_ge(sig("x_added"), 2 * DT)
            norm(2)

            def lora_results(fn, dst, bias=None):
                for m in range(DT):
                    b = k8_result_bank("act")
                    act.wait_ge(sig("lora_mm"), seen("lora_mm") + lora[0] + 1)
                    lora[0] += 1
                    nc.scalar.activation(dst[:, m, :], bank[b][:, :], fn,
                                         **({"bias": bias[:, m:m + 1]} if bias is not None else {})
                                         ).then_inc(sig("lora_out"), 1)
                    act.wait_ge(sig("lora_out"), lora[0])
                    act.sem_inc(sig(f"bank_free{b}"), 1)

            lora = [0]
            for i, (dst, rows) in enumerate(((hid_g1, P), (hid_g2, 32))):
                b = k8_result(act, "act", 0, 0, 0)
                skip("act", 1)
                nc.scalar.activation(dst[0:rows, :], bank[b][0:rows, :], ACT.Sigmoid).then_inc(sig("hid_g"), 1)
                act.wait_ge(sig("hid_g"), i + 1)
                act.sem_inc(sig(f"bank_free{b}"), 1)
            lora_results(ACT.Copy, g_a)
            rings["act"][0].advance(4)
            for i, fn in enumerate((ACT.Tanh, ACT.Copy)):
                b = k8_result_bank("act")
                act.wait_ge(sig("wa_mm"), seen("wa_mm") + i + 1)
                nc.scalar.activation(hid_wa[64 * i:64 * i + 64, :], bank[b][64 * i:64 * i + 64, :], fn
                                     ).then_inc(sig("hid_wa"), 1)
                act.wait_ge(sig("hid_wa"), i + 1)
                act.sem_inc(sig(f"bank_free{b}"), 1)
                if i == 0:
                    lora_results(ACT.Sigmoid, k_a_, v("w0"))
                    act.wait_ge(sig("pads"), 1)
                    nc.scalar.activation(e_c[:, :, :, 1:], k_a_.rearrange("p m (c t) -> p m c t", t=RD), ACT.Exp,
                                         scale=-DECAY).then_inc(sig("decay_exp"), 1)
            lora_results(ACT.Sigmoid, a_a, v("a0"))
            weights_high(act, 0, 0, 0, rwkv_wh)
            weights_high(act, 0, 0, 1, rwkv_wh)
            rhs_highs(mixb, v_hi, "mixed", 3 * DT)
            act.wait_ge(sig("g_stored"), 16)
            for m in range(DT):
                b = k8_result(act, "act", 0, 0, 0)
                weights_high(act, 0, 0, 2, rwkv_wh)
                pass_units("act", 1)
                nc.scalar.activation(v_a[:, m, :], bank[b][:, :], ACT.Copy).then_inc(sig("v_out"), 1)
                act.wait_ge(sig("v_out"), m + 1)
                act.sem_inc(sig(f"bank_free{b}"), 1)
                for k in (2 * m, 2 * m + 1):
                    if k < DT:
                        act.wait_ge(sig("mixed"), 4 * DT + k + 1)
                        split_high("rhs_hi", rounded(r_hi[:, k, :]), mixa[:, k, :])
            for m in range(DT):
                unit_through(act, "act", 0, 0, 0)
                weights_high(act, 0, 0, 2, rwkv_wh)
                pass_units("act", 1)
                for k in (2 * m, 2 * m + 1):
                    if k < DT:
                        act.wait_ge(sig("mixed"), 5 * DT + k + 1)
                        split_high("rhs_hi", rounded(ht[:, k, :]), mixb[:, k, :])
            act.wait_ge(sig("r_out"), 8)
            act.wait_ge(sig("pads"), 2)
            nc.scalar.activation(ei_c[:, :, :, 1:], k_a_.rearrange("p m (c t) -> p m c t", t=RD), ACT.Exp,
                                 scale=DECAY).then_inc(sig("decay_exp"), 1)
            act.wait_ge(sig("decay_exp"), 2)
            for m in range(DT):
                b = k8_result(act, "act", 0, 0, 0)
                if m + 2 < DT:
                    weights_high(act, 0, 0, 2, rwkv_wh)
                pass_units("act", 1)
                nc.scalar.activation(k_a_[:, m, :], bank[b][:, :], ACT.Copy).then_inc(sig("k_out"), 1)
                nc.scalar.activation(kn[:, m, :], bank[b][:, :], ACT.Square, scale=v("k_k")[:, m:m + 1]
                                     ).then_inc(sig("k_out"), 1)
                act.wait_ge(sig("k_out"), seen("k_out") + 2 * m + 2)
                act.sem_inc(sig(f"bank_free{b}"), 1)
            act.wait_ge(sig("ksum_mm"), seen("ksum_mm") + DT)
            nc.scalar.activation(key_rows, bank[2][0:16, :], ACT.Sqrt, bias=eps(1)[0:16, :]
                                 ).then_inc(sig("k_root"), 1)
            act.wait_ge(sig("bd_zero"), 14)
            def half(dst, src, e, s, fn=ACT.Copy):
                nc.scalar.activation(dst[RD * e:RD * e + RD, :, RD * e:RD * e + RD], src, fn).then_inc(sig(s), 1)

            def stage(n, i):
                e = i % 2
                src = (kk_a, a_a)[i // 2][RD * e:RD * e + RD, :, bass.ds(RD * n, RD)]
                half((bdA, bdB)[i // 2], src, e, ("bda", "bdb")[i // 2])

            def chunk(n, more):
                for i, (dst, s) in enumerate(((bdBt, "bt_mm"), (bdKt, "kt_mm"), (bdVt, "vt_mm"))):
                    act.wait_ge(sig(s), seen(s) + n + 1)
                    src = bank[4 + i][:, :].rearrange("p (m t) -> p m t", m=DT)
                    for e in range(2):
                        half(dst, src[RD * e:RD * e + RD, :, :], e, "tok_out")
                nc.scalar.activation(vt_c, bank[6][:, :].rearrange("p (m t) -> p m t", m=DT), ACT.Copy
                                     ).then_inc(sig("tok_out"), 1)
                for lv in range(5):
                    for g in range(2):
                        act.wait_ge(sig("q_out"), n * 12 + 2 * lv + g + 1)
                        for e in range(2):
                            nc.scalar.activation(bdQ[RD * e:RD * e + RD, 4 * g:4 * g + 4, RD * e:RD * e + RD],
                                                 q_c[RD * e:RD * e + RD, 4 * g:4 * g + 4, :], ACT.Copy
                                                 ).then_inc(sig("bdq"), 1)
                    if more and lv in (1, 2):
                        stage(n + 1, lv + 1)
                act.wait_ge(sig("g_mm"), seen("g_mm") + n + 1)
                nc.scalar.activation(g_c, bank[1][:, :].rearrange("p (m t) -> p m t", m=DT), ACT.Copy, scale=-1.0
                                     ).then_inc(sig("g_out"), 1)
                if more:
                    stage(n + 1, 0)
                    stage(n + 1, 1)
                act.wait_ge(sig("xt_sub"), seen("xt_sub") + n * 12 + 12)
                for e in range(2):
                    half(bdXT, xt_c[RD * e:RD * e + RD, :, :], e, "bdxt")
                act.wait_ge(sig("u_out"), n + 1)
                for e in range(2):
                    half(bdU, u_c[RD * e:RD * e + RD, :, :], e, "bdu")
                act.wait_ge(sig("y_mm"), seen("y_mm") + n + 1)
                act.sem_inc(sig("carrier"), 1)
                nc.scalar.activation(kk_a[:, :, bass.ds(RD * n, RD)], bank[3][:, :].rearrange("p (m t) -> p m t", m=DT),
                                     ACT.Copy).then_inc(sig("y_out"), 1)
                act.wait_ge(sig("z_out"), seen("z_out") + 2 * n + 2)
                for e in range(2):
                    half(bdZ, z_c[RD * e:RD * e + RD, :, :], e, "bdz")

            for i in range(4):
                stage(0, i)
            with act.Fori(0, SEQ // RD - 1) as n:
                chunk(n, True)
            chunk(SEQ // RD - 1, False)
            act.wait_ge(sig("bdz"), seen("bdz") + 2 * SEQ // RD)
            weights_high(act, 0, 0, 0, ffn_wh)
            weights_high(act, 0, 0, 1, ffn_wh)
            for m in range(DT):
                act.wait_ge(sig("centered"), seen("centered") + m + 1)
                nc.scalar.activation(ht[:, m, :], mixb[:, m, :], ACT.Square).then_inc(sig("dev_sq"), 1)
            act.wait_ge(sig("dev_mm"), seen("dev_mm") + DT)
            nc.scalar.activation(dev_rows, bank[4][0:16, :], ACT.Sqrt, bias=eps(2)[0:16, :], scale=1.0 / RD
                                 ).then_inc(sig("dev_root"), 1)
            rhs_highs(k_a_, rhs_hi, "gated", seen("gated"))
            split_units(DT)
            act.wait_ge(sig("x_added"), 3 * DT)
            norm(3)
            rhs_highs(ht, rhs_hi, "h_done", 3 * DT)
            gate_ups(1)
            downs_high()
            act.wait_ge(sig("x_added"), 4 * DT)
            norm(4)


        @block.vector
        def _(dve):
            nc.vector.sem_inc(sig("scored"), 2)
            nc.vector.sem_inc(sig("pv_read"), 1)
            nc.vector.sem_inc(sig("pair_done"), 1)
            nc.vector.sem_inc(sig("chunk_done"), 1)
            nc.vector.sem_inc(sig("ff_done"), 2)
            dve.wait_ge(sig("x_loaded"), 16)
            dve.wait_ge(sig("con_loaded"), 16)

            def norm(r):
                nc.vector.tensor_tensor(ht[:, 4:8, :], x[:, 4:8, :], x[:, 4:8, :], ALU.mult
                                        ).then_inc(sig("sq_d"), 1)
                dve.wait_ge(sig("rms_done"), r + 1)
                nc.vector.reciprocal(norm_t[:, 1, :], norm_t[:, 0, :]).then_inc(sig("rrms_done"), 1)
                dve.wait_ge(sig("rrms_done"), r + 1)
                for k in range(DT):
                    nc.vector.scalar_tensor_tensor(ht[:, k, :], x[:, k, :], v(f"n{r}")[:, k:k + 1],
                                                   norm_t[:, 1, :], ALU.mult, ALU.mult
                                                   ).then_inc(sig("h_done"), 1)

            dve.wait_ge(sig("vec_loaded"), 16)
            def rhs_lows(a, high, base, order=range(DT), dst=None):
                for i, k in enumerate(order):
                    dve.wait_ge(sig("rhs_hi"), base + i + 1)
                    split_low("rhs_lo", a[:, k, :], rounded(high[:, k, :]), rounded((a if dst is None else dst)[:, k, :]))

            norm(0)
            weights_low(dve, 0, 0, 0, in_wh)
            rhs_lows(ht, in_hi, 0, dst=in_lo)
            weights_low(dve, 0, 0, 1, in_wh)
            split["dve"][1] = DT
            dve.wait_ge(sig("row_mm"), 1)
            nc.vector.tensor_copy(brow[0:NH, 0:512], bank[3][0:NH, :]).then_inc(sig("bias_row"), 1)
            nc.vector.tensor_copy(brow[0:NH, 512:BIAS_LEN], bank[4][0:NH, 0:128]).then_inc(sig("bias_row"), 1)
            with dve.Fori(0, 3) as it:
                for j in range(4):
                    b = k8_result(dve, "dve", it, 4, j)
                    weights_low(dve, it, 4, j + 2, in_wh)
                    dve.wait_ge(sig("silu_done"), it * 4 + j + 1)
                    taps = v("conv").rearrange("p (i w) -> p i w", w=4)
                    tap = lambda w: taps[:, bass.ds(it * 4 + j, 1), w]
                    nc.vector.tensor_scalar(conv[j % 2], bank[b][:, :], tap(3), None, ALU.mult
                                            ).then_inc(sig("tap"), 1)
                    for d in (1, 2, 3):
                        dve.wait_ge(sig("tap"), (it * 4 + j) * 3 + d)
                        ins = nc.vector.scalar_tensor_tensor(conv[j % 2][:, d:SEQ], bank[b][:, 0:SEQ - d],
                                                             tap(3 - d), conv[j % 2][:, d:SEQ],
                                                             ALU.mult, ALU.add)
                        ins.then_inc(sig("tap" if d < 3 else "conv_done"), 1)
                    dve.wait_ge(sig("conv_done"), it * 4 + j + 1)
                    dve.sem_inc(sig(f"bank_free{b}"), 1)
            pass_units("dve", 12)
            for j in range(2, IN_UNITS - 12):
                weights_low(dve, 0, 0, j, in_wh)
            pass_units("dve", IN_UNITS - 12)
            rings["dve"][0].advance(8)
            dve.wait_ge(sig("cmp_mm"), 1)
            nc.vector.tensor_copy(kcT[:, 0:NCMP], bank[4][:, 0:NCMP]).then_inc(sig("cmp_done"), 1)
            nc.vector.tensor_copy(vcT[0:NCMP, :], bank[5][0:NCMP, 0:P]).then_inc(sig("cmp_done"), 1)
            dve.wait_ge(sig("gates_done"), 2)
            dve.wait_ge(sig("proj_done"), IN_UNITS - 12)
            dve.wait_ge(sig("bias_done"), NH)
            with dve.Fori(0, 4) as j:
                nc.vector.tensor_copy(q_st, proj[:, bass.ds(16 + j, 1), :].rearrange("p a t -> p (a t)")
                                      ).then_inc(sig("staged"), 1)
                for s in range(2):
                    nc.vector.tensor_copy(bias_st[:, s, :], bias[:, bass.ds(4 * s + j, 1), :]
                                          .rearrange("p a t -> p (a t)")).then_inc(sig("staged"), 1)
                dve.wait_ge(sig("staged"), 3 * j + 3)
                for u in range(24):
                    s, qt, br = u // 12, u // 3 % 4, u % 3
                    w = width(u)
                    dve.wait_ge(sig("score_mm"), j * 24 + u + 1)
                    if br < 2:
                        bb = bias_st[:, s, SEQ - P - P * qt:]
                    else:
                        bb = bias_st[:, s, 415 - P * qt:415 - P * qt + 16 * (w - 1) + 1:16]
                    dve.sem_inc(sig("carrier"), 1)
                    nc.vector.tensor_tensor_reduce(
                        out=probs[u % 2][:, 0:w], in0=bank[2 + u % 2][:, 0:w], in1=bb, scale=1.0,
                        scalar=NEG, op0=ALU.add, op1=ALU.max, accum_out=nmx[u % 2][:, 0:1]
                    ).then_inc(sig("max_done"), 1)
                    dve.wait_ge(sig("max_done"), j * 24 + u + 1)
                    nc.vector.tensor_scalar(nmx[u % 2][:, 1:2], nmx[u % 2][:, 0:1], 0.1 * NEG, -1.0,
                                            ALU.max, ALU.mult).then_inc(sig("scored"), 1)
                dve.wait_ge(sig("exp_done"), j * 24 + 24)
                nc.vector.tensor_scalar(rg, sums, 1e-30, None, ALU.max).then_inc(sig("rg_step"), 1)
                dve.wait_ge(sig("rg_step"), 3 * j + 1)
                nc.vector.reciprocal(rg, rg).then_inc(sig("rg_step"), 1)
                dve.wait_ge(sig("rg_step"), 3 * j + 2)
                gv = gates_flat.rearrange("p (q s h b) -> p s q h b", q=4, s=2, h=4)[:, :, :, bass.ds(j, 1), :]
                nc.vector.tensor_tensor(rg.rearrange("p (s q b) -> p s q b", s=2, q=4),
                                        rg.rearrange("p (s q b) -> p s q b", s=2, q=4),
                                        gv.rearrange("p s q h b -> p s q (h b)"), ALU.mult
                                        ).then_inc(sig("rg_step"), 1)
                dve.wait_ge(sig("rg_step"), 3 * j + 3)
                dve.wait_ge(sig("pv_mm"), j + 1)
                for br in range(3):
                    scale = rg.rearrange("p (a b) -> p a b", b=3)[:, :, br:br + 1].broadcast_to([P, 8, ND])
                    nc.vector.tensor_tensor(oacc[br].rearrange("p (a d) -> p a d", a=8),
                                            bank[5 + br][:, :].rearrange("p (a d) -> p a d", a=8), scale,
                                            ALU.mult).then_inc(sig("branch"), 1)
                dve.wait_ge(sig("branch"), 4 * j + 3)
                dve.sem_inc(sig("pv_read"), 1)
                nc.vector.tensor_tensor(oacc[0], oacc[0], oacc[1], ALU.add).then_inc(sig("branch"), 1)
                dve.wait_ge(sig("branch"), 4 * j + 4)
                ov = otok.rearrange("p q (s h d) -> p s q h d", s=2, h=4)[:, :, :, bass.ds(j, 1), :]
                nc.vector.tensor_tensor(ov.rearrange("p s q h d -> p s q (h d)"),
                                        oacc[0].rearrange("p (s q d) -> p s q d", s=2, q=4),
                                        oacc[2].rearrange("p (s q d) -> p s q d", s=2, q=4), ALU.add
                                        ).then_inc(sig("pair_done"), 1)

            nc.vector.tensor_tensor(gtmp.rearrange("p (a b) -> p a b", a=4), tok[:, :, 4:8],
                                    v("dtb").unsqueeze(1).broadcast_to([P, 4, 4]), ALU.add
                                    ).then_inc(sig("g_arg"), 1)
            dve.wait_ge(sig("g_step"), 4)
            dve.wait_ge(sig("g_arg"), 1)
            nc.vector.scalar_tensor_tensor(g_col, gtmp, 0.0, gaux, ALU.max, ALU.add).then_inc(sig("g_pos"), 1)
            dve.wait_ge(sig("g_pos"), 1)
            nc.vector.scalar_tensor_tensor(g_col.rearrange("p (a b) -> p a b", a=4),
                                           g_col.rearrange("p (a b) -> p a b", a=4), -1.0,
                                           ea.unsqueeze(1).broadcast_to([P, 4, 4]), ALU.mult, ALU.mult
                                           ).then_inc(sig("g_done"), 1)
            nc.vector.memset(st, 0.0).then_inc(sig("st_zero"), 1)
            nc.vector.tensor_copy(tile_out.rearrange("p (a b) -> p a b", b=P), c("ident")[0:8, 0:8].unsqueeze(2)
                                  .broadcast_to([8, 8, P])).then_inc(sig("st_zero"), 1)
            dve.wait_ge(sig("eg_done"), 1)
            nc.vector.scalar_tensor_tensor(nbeg, beta, -1.0, eg[:, 0:16], ALU.mult, ALU.mult
                                           ).then_inc(sig("nbeg_done"), 1)
            dve.wait_ge(sig("qk_root"), 1)
            nc.vector.reciprocal(rn0[0:8, 0, :], rn0[0:8, 0, :]).then_inc(sig("qk_recip"), 1)
            for i in range(8):
                dve.wait_ge(sig("qk_sum"), i + 2)
                nc.vector.scalar_tensor_tensor(proj[:, i, :], proj[:, i, :], GD ** -0.5 if i < 4 else 1.0,
                                               bank[4 + i % 4][:, :], ALU.mult, ALU.mult).then_inc(sig("qk_normed"), 1)

            def heads(b):
                return bank[b][:, :].rearrange("p (a b) -> p a b", a=GH)

            def every_head(a):
                return a.unsqueeze(1).broadcast_to([P, GH, P])

            def per_token(a, n):
                return a[:, bass.ds(4 * n, 4)].unsqueeze(2).broadcast_to([P, GH, P])

            dve.wait_ge(sig("qk_normed"), 8)
            with dve.Fori(0, NCHUNK) as n:
                for dst, a in ((k_st, 4), (qst, 0), (v_st, 8)):
                    nc.vector.tensor_copy(dst, proj[:, a:a + 4, bass.ds(CHUNK * n, CHUNK)]
                                          ).then_inc(sig("chunk_staged"), 1)
                dve.wait_ge(sig("decay_low"), n + 1)
                nc.vector.tensor_tensor(dlow, dlow, every_head(c("gt")), ALU.mult).then_inc(sig("mstep"), 1)
                dve.wait_ge(sig("mstep"), 2 * n + 1)
                nc.vector.tensor_tensor(dlow, dlow, per_token(beta, n), ALU.mult).then_inc(sig("mstep"), 1)
                dve.wait_ge(sig("mstep"), 2 * n + 2)
                dve.wait_ge(sig("kk_mm"), n + 1)
                nc.vector.tensor_tensor(mlow, heads(5), dlow, ALU.mult).then_inc(sig("m_done"), 1)
                nc.vector.tensor_copy(xi, every_head(c("ident"))).then_inc(sig("x_init"), 1)
                nc.vector.tensor_copy(xit, every_head(c("ident"))).then_inc(sig("x_init"), 1)
                dve.wait_ge(sig("decay_up"), n + 1)
                nc.vector.tensor_tensor(dup, dup, every_head(c("le")), ALU.mult).then_inc(sig("up_masked"), 1)
                dve.wait_ge(sig("up_masked"), n + 1)
                dve.wait_ge(sig("qk_mm"), n + 1)
                nc.vector.tensor_tensor(qk, heads(6), dup, ALU.mult).then_inc(sig("qk_done"), 1)
                dve.wait_ge(sig("vtok2_mm"), n + 1)
                nc.vector.tensor_tensor(vb, heads(2), per_token(beta, n), ALU.mult).then_inc(sig("vb_done"), 1)
                dve.wait_ge(sig("ks_mm"), n + 1)
                nc.vector.tensor_tensor(rr, heads(6), per_token(nbeg, n), ALU.mult).then_inc(sig("rhs_step"), 1)
                dve.wait_ge(sig("rhs_step"), n + 1)
                dve.wait_ge(sig("vb_done"), n + 1)
                nc.vector.tensor_tensor(rr, rr, vb, ALU.add).then_inc(sig("rhs_done"), 1)
                for lv in range(7):
                    dve.wait_ge(sig("qt_mm"), n * 7 + lv + 1)
                    nc.vector.tensor_tensor(qt_, heads(3), every_head(c("lvl")[:, P * lv:P * lv + P]), ALU.mult
                                            ).then_inc(sig("qt_done"), 1)
                    dve.wait_ge(sig("xx_mm"), n * 7 + lv + 1)
                    if lv < 6:
                        nc.vector.tensor_tensor(xi, xi, heads(4), ALU.subtract).then_inc(sig("x_step"), 1)
                    nc.vector.tensor_tensor(xit, xit, heads(5), ALU.subtract).then_inc(sig("x_step"), 1)
                dve.wait_ge(sig("st_mm"), n + 1)
                nc.vector.tensor_tensor(st, st, egr[:, :, P - 1:P].broadcast_to([P, GH, P]), ALU.mult
                                        ).then_inc(sig("st_step"), 1)
                dve.wait_ge(sig("st_step"), n + 1)
                nc.vector.tensor_tensor(st, st, heads(3), ALU.add).then_inc(sig("chunk_done"), 1)
            dve.wait_ge(sig("o_root"), 1)
            nc.vector.reciprocal(rn0[0:4, 4, :], rn0[0:4, 4, :]).then_inc(sig("o_step"), 1)
            for i in range(4):
                dve.wait_ge(sig("o_sum"), i + 2)
                nc.vector.scalar_tensor_tensor(ht[:, i, :], ht[:, i, :], v("gnorm"), bank[(5, 6, 7, 3)[i]][:, :],
                                               ALU.mult, ALU.mult).then_inc(sig("o_step"), 1)
                dve.wait_ge(sig("o_step"), i + 2)
                nc.vector.tensor_tensor(ht[:, i, :], ht[:, i, :], proj[:, 12 + i, :], ALU.mult
                                        ).then_inc(sig("mix_gdn"), 1)

            def add_results(total):
                with dve.Fori(0, DT // 4) as it:
                    for j in range(4):
                        b = k8_result(dve, "dve", it, 4, j)
                        weights_low(dve, it, 4, j + 2, ffn_wh)
                        xm = x[:, bass.ds(it * 4 + j, 1), :].rearrange("p a t -> p (a t)")
                        nc.vector.tensor_tensor(xm, xm, bank[b][:, :], ALU.add).then_inc(sig("x_added"), 1)
                        dve.wait_ge(sig("x_added"), total - DT + 1 + it * 4 + j)
                        dve.sem_inc(sig(f"bank_free{b}"), 1)
                pass_units("dve", DT)

            def gate_ups(f):
                def turn(it, per, last):
                    for j in range(4):
                        first = f * FT + (FT - 2 if last else 0) + it * 2 + j // 2
                        b = k8_result(dve, "dve", it, per, j)
                        if not last or j < 2:
                            weights_low(dve, it, per, j + 2, ffn_wh)
                        if j % 2 == 0:
                            bg = b
                            continue
                        if last:
                            tile, high, low = (a[:, FT - 2 + j // 2, :] for a in (hid_t, hid_hi_r, hid_lo_r))
                        else:
                            tile, high, low = (a[:, bass.ds(it * 2 + j // 2, 1), :].rearrange("p a t -> p (a t)")
                                               for a in (hid_t, hid_hi_r, hid_lo_r))
                        dve.wait_ge(sig("sil_done"), first + 1)
                        nc.vector.tensor_tensor(tile, sil[:, j // 2, :], bank[b][:, :], ALU.mult
                                                ).then_inc(sig("ff_done"), 1)
                        dve.wait_ge(sig("ff_hi"), first + 1)
                        dve.sem_inc(sig(f"bank_free{bg}"), 1)
                        dve.sem_inc(sig(f"bank_free{b}"), 1)
                        split_low("ff_lo", tile, high, low)

                with dve.Fori(0, FT // 2 - 1) as it:
                    turn(it, 4, False)
                pass_units("dve", 2 * FT - 4)
                turn(0, 0, True)
                pass_units("dve", 4)

            def add_down(total):
                for m in range(2):
                    down_low(dve, m)
                for m in range(DT):
                    s, u = rings["dve"][1].at(m)
                    dve.wait_ge(sig(f"down_done{s}"), u + 1)
                    b = PB[rings["dve"][2].at(m)[0]]
                    nc.vector.tensor_tensor(x[:, m, :], x[:, m, :], bank[b][:, :], ALU.add).then_inc(sig("x_added"), 1)
                    dve.wait_ge(sig("x_added"), total - DT + 1 + m)
                    dve.sem_inc(sig(f"bank_free{b}"), 1)
                    if m + 2 < DT:
                        down_low(dve, m + 2)
                skip("dve", 0, DT)
                split["dve"][2] += 3 * DT

            weights_low(dve, 0, 0, 0, ffn_wh)
            weights_low(dve, 0, 0, 1, ffn_wh)
            rhs_lows(ht, rhs_hi, DT, (4, 5, 6, 7, 0, 1, 2, 3))
            add_results(DT)
            norm(1)
            rhs_lows(ht, rhs_hi, 2 * DT)
            gate_ups(0)
            add_down(2 * DT)
            nc.vector.tensor_copy(head_out.rearrange("p (a b) -> p a b", b=RD), c("ident")[0:16, 0:16].unsqueeze(2)
                                  .broadcast_to([16, 16, RD])).then_inc(sig("pads_h"), 1)
            nc.vector.memset(h[:, :, HD - 1:HD], 0.0).then_inc(sig("pads_h"), 1)
            nc.vector.memset(padmask, 0.0).then_inc(sig("pads_h"), 1)
            dve.wait_ge(sig("pads_h"), 3)
            nc.vector.memset(padmask.rearrange("p (c t) -> p c t", t=RD + 1)[:, :, 0:1], 1.0).then_inc(sig("pads_h"), 1)
            nc.vector.memset(e_c[:, :, :, 0:1].rearrange("p m c t -> p (m c) t"), 0.0).then_inc(sig("pads"), 1)
            norm(2)
            dve.wait_ge(sig("h_done"), 3 * DT)

            mixes = [0]

            def mix(i, dst, tiles=range(DT)):
                if tiles[0] == 0:
                    mixes[0] += 1
                    if mixes[0] > 2:
                        dve.wait_ge(sig("mix_used"), mixes[0] - 2)
                for k in tiles:
                    nc.vector.tensor_tensor(dst[:, k, :], h[:, k, HD - 1:HD - 1 + SEQ], ht[:, k, :], ALU.subtract
                                            ).then_inc(sig("mix_diff"), 1)
                    dve.wait_ge(sig("mix_diff"), (mixes[0] - 1) * DT + k + 1)
                    nc.vector.scalar_tensor_tensor(dst[:, k, :], dst[:, k, :], v("mu")[:, DT * i + k:DT * i + k + 1],
                                                   ht[:, k, :], ALU.mult, ALU.add).then_inc(sig("mixed"), 1)

            mix(5, mixa)
            mix(1, mixb)
            mix(4, mixa)
            dve.wait_ge(sig("decay_exp"), 1)
            dve.wait_ge(sig("pads_h"), 4)
            for m in range(DT):
                nc.vector.tensor_tensor_scan(e_a[:, m, :], e_a[:, m, :], padmask, 0.0, ALU.mult, ALU.add
                                             ).then_inc(sig("decay_scan"), 1)
            mix(3, mixb)
            skip("dve", 2)
            rings["dve"][2].advance(8 + 1 + 8 + 1 + 8)
            rings["dve"][0].advance(4)
            weights_low(dve, 0, 0, 0, rwkv_wh)
            rhs_lows(mixb, v_hi, 3 * DT)
            weights_low(dve, 0, 0, 1, rwkv_wh)

            def next_mix(i, dst, high, base, m):
                if m < DT // 2:
                    mix(i, dst, (2 * m, 2 * m + 1))
                    rhs_lows(dst, high, base + 2 * m, (2 * m, 2 * m + 1))

            for m in range(DT):
                next_mix(0, mixa, r_hi, 4 * DT, m)
                weights_low(dve, 0, 0, 2, rwkv_wh)
                pass_units("dve", 1)
            dve.wait_ge(sig("decay_scan"), DT)
            for m in range(DT):
                b = k8_result(dve, "dve", 0, 0, 0)
                next_mix(2, mixb, ht, 5 * DT, m)
                weights_low(dve, 0, 0, 2, rwkv_wh)
                pass_units("dve", 1)
                nc.vector.tensor_tensor(r_a[:, m, :].rearrange("p (c t) -> p c t", t=RD),
                                        bank[b][:, :].rearrange("p (c t) -> p c t", t=RD),
                                        e_c[:, m, :, 1:], ALU.mult).then_inc(sig("r_out"), 1)
                dve.wait_ge(sig("r_out"), m + 1)
                dve.sem_inc(sig(f"bank_free{b}"), 1)
            nc.vector.memset(ei_c[:, :, :, 0:1].rearrange("p m c t -> p (m c) t"), 0.0).then_inc(sig("pads"), 1)
            dve.wait_ge(sig("decay_exp"), 2)
            for m in range(DT):
                nc.vector.tensor_tensor_scan(ei_a[:, m, :], ei_a[:, m, :], padmask, 0.0, ALU.mult, ALU.add
                                             ).then_inc(sig("decay_scan"), 1)
                if m % 4 == 3:
                    weights_low(dve, 0, 0, 2 + m // 4, rwkv_wh)
            dve.wait_ge(sig("decay_scan"), 2 * DT)
            nc.vector.tensor_copy(p_c, e_c[:, :, :, RD:RD + 1].rearrange("p m c t -> p m (c t)")
                                  ).then_inc(sig("pc_done"), 1)
            steps = [0]

            def step(ins):
                ins.then_inc(sig("key_step"), 1)
                steps[0] += 1
                dve.wait_ge(sig("key_step"), steps[0])

            def chunked(a, m):
                return a[:, m, :].rearrange("p (c t) -> p c t", t=RD)

            for m in range(DT):
                if 4 <= m + 3 < DT:
                    weights_low(dve, 0, 0, m + 3, rwkv_wh)
                dve.wait_ge(sig("ksum_mm"), seen("ksum_mm") + m + 1)
                nc.vector.tensor_scalar(kn[:, m, :], k_a_[:, m, :], v("k_k")[:, m:m + 1], None, ALU.mult
                                        ).then_inc(sig("key_mod"), 1)
                step(nc.vector.tensor_scalar(key_t[:, m % 2, :], a_a[:, m, :], -1.0, v("k_a")[:, m:m + 1],
                                             ALU.add, ALU.mult))
                dve.wait_ge(sig("key_mod"), seen("key_mod") + m + 1)
                step(nc.vector.scalar_tensor_tensor(k_a_[:, m, :], key_t[:, m % 2, :], 1.0, k_a_[:, m, :],
                                                    ALU.add, ALU.mult))
                step(nc.vector.tensor_tensor(chunked(k_a_, m), chunked(k_a_, m), ei_c[:, m, :, 1:], ALU.mult))
                step(nc.vector.tensor_tensor(chunked(a_a, m), chunked(a_a, m), ei_c[:, m, :, 1:], ALU.mult))
            pass_units("dve", DT)
            dve.wait_ge(sig("k_root"), 1)
            nc.vector.reciprocal(key_rows, key_rows).then_inc(sig("k_recip"), 1)
            for m in range(DT):
                dve.wait_ge(sig("ksum_mm"), seen("ksum_mm") + DT + m + 1)
                nc.vector.tensor_tensor(kn[:, m, :], kn[:, m, :], bank[2 + m % 4][:, :], ALU.mult
                                        ).then_inc(sig("kn_done"), 1)
                dve.wait_ge(sig("kn_done"), seen("kn_done") + m + 1)
                nc.vector.tensor_tensor(a_a[:, m, :], a_a[:, m, :], kn[:, m, :], ALU.mult).then_inc(sig("key_step"), 1)
                step(nc.vector.tensor_tensor(chunked(kk_a, m), chunked(kn, m), e_c[:, m, :, 0:RD], ALU.mult))
                steps[0] += 1
            dve.wait_ge(sig("key_step"), steps[0])
            dve.sem_inc(sig("scan_ready"), 1)
            for a in (bdA, bdB, bdM):
                nc.vector.memset(a, 0.0).then_inc(sig("bd_zero"), 1)
            dve.wait_ge(sig("bd_zero"), 14)

            def tiles(b):
                return bank[b][:, :].rearrange("p (m t) -> p m t", m=DT)

            def all_tiles(name, e=None, n=DT):
                a = c(name) if e is None else c(name)[RD * e:RD * e + RD, :]
                return a.unsqueeze(1).broadcast_to([P if e is None else RD, n, RD])

            def stage(n, i):
                now, e = bass.ds(RD * n, RD), (i - 3) % 2
                lo = slice(RD * e, RD * e + RD)
                dst, src = ((b_c, a_a[:, :, now]), (ar_c[:, :, 0:RD], kk_a[:, :, now]), (ar_c[:, :, RD:], r_a[:, :, now]),
                            (bdK[lo, :, lo], k_a_[lo, :, now]), (bdK[lo, :, lo], k_a_[lo, :, now]),
                            (bdV[lo, :, lo], v_a[lo, :, now]), (bdV[lo, :, lo], v_a[lo, :, now]))[i]
                nc.vector.tensor_copy(dst, src).then_inc(sig("rhs_staged"), 1)

            def chunk(n, more):
                dve.wait_ge(sig("m_mm"), seen("m_mm") + n + 1)
                for e in range(2):
                    nc.vector.tensor_tensor(bdM[RD * e:RD * e + RD, :, RD * e:RD * e + RD],
                                            tiles(0)[RD * e:RD * e + RD, :, :], all_tiles("gt64", e), ALU.mult
                                            ).then_inc(sig("m_out"), 1)
                for dst in (x_c, xt_c):
                    nc.vector.tensor_copy(dst, all_tiles("id64")).then_inc(sig("m_out"), 1)
                for e in range(2):
                    nc.vector.tensor_copy(bdX[RD * e:RD * e + RD, :, RD * e:RD * e + RD], all_tiles("id64", e)
                                          ).then_inc(sig("m_out"), 1)
                dve.wait_ge(sig("k_mm"), seen("k_mm") + n + 1)
                for g in range(2):
                    kb = bank[1 + g][:, :].rearrange("p (m t) -> p m t", m=4)
                    for e in range(2):
                        nc.vector.tensor_tensor(bdAK[RD * e:RD * e + RD, 4 * g:4 * g + 4, RD * e:RD * e + RD],
                                                kb[RD * e:RD * e + RD, :, 0:RD], all_tiles("lt64", e, 4), ALU.mult
                                                ).then_inc(sig("ak_out"), 1)
                    nc.vector.tensor_tensor(rk_c[:, 4 * g:4 * g + 4, :], kb[:, :, RD:], all_tiles("le64", None, 4),
                                            ALU.mult).then_inc(sig("ak_out"), 1)
                dve.wait_ge(sig("rb_mm"), seen("rb_mm") + n + 1)
                nc.vector.tensor_tensor(rb_c, tiles(3), all_tiles("le64"), ALU.mult).then_inc(sig("rb_out"), 1)
                nc.vector.tensor_copy(ry_c, ar_c[:, :, RD:]).then_inc(sig("rb_out"), 1)
                ahead = list(range(7)) if more else []
                for lv in range(6):
                    for g in range(2):
                        dve.wait_ge(sig("q_mm"), seen("q_mm") + n * 12 + 2 * lv + g + 1)
                        qb = bank[(7, 0)[g]][:, 0:256].rearrange("p (m t) -> p m t", m=4)
                        lm = c("lvl64")[:, RD * lv:RD * lv + RD].unsqueeze(1).broadcast_to([P, 4, RD])
                        nc.vector.tensor_tensor(q_c[:, 4 * g:4 * g + 4, :], qb, lm, ALU.mult).then_inc(sig("q_out"), 1)
                        if lv > 1 and ahead:
                            stage(n + 1, ahead.pop(0))
                    for g in range(2):
                        for a, s, sub, b, k in ((xt_c, "xtm", "xt_sub", 4, 12), (x_c, "xmm", "x_sub", 2, 10)):
                            if lv == 5 and a is x_c:
                                continue
                            dve.wait_ge(sig(s), seen(s) + n * k + 2 * lv + g + 1)
                            nc.vector.tensor_tensor(a[:, 4 * g:4 * g + 4, :], a[:, 4 * g:4 * g + 4, :],
                                                    bank[b + g][:, 0:256].rearrange("p (m t) -> p m t", m=4),
                                                    ALU.subtract).then_inc(sig(sub), 1)
                dve.wait_ge(sig("u_mm"), seen("u_mm") + n + 1)
                nc.vector.tensor_copy(u_c, tiles(7)).then_inc(sig("u_out"), 1)
                dve.wait_ge(sig("z_mm"), seen("z_mm") + n + 1)
                nc.vector.tensor_tensor(z_c, z_c, tiles(6), ALU.add).then_inc(sig("z_out"), 1)
                dve.wait_ge(sig("z_out"), seen("z_out") + 2 * n + 1)
                nc.vector.tensor_tensor(z_c, z_c, p_c[:, :, bass.ds(n, 1)].broadcast_to([P, DT, RD]), ALU.mult
                                        ).then_inc(sig("z_out"), 1)

            for i in range(7):
                stage(0, i)
            with dve.Fori(0, SEQ // RD - 1) as n:
                chunk(n, True)
            chunk(SEQ // RD - 1, False)
            dve.wait_ge(sig("y_out"), seen("y_out") + SEQ // RD)
            for m in range(DT):
                nc.vector.scalar_tensor_tensor(r_a[:, m, :], r_a[:, m, :], v("r_k")[:, m:m + 1], k_a_[:, m, :],
                                               ALU.mult, ALU.mult).then_inc(sig("rk_done"), 1)
            for m in range(DT):
                dve.wait_ge(sig("mean_mm"), seen("mean_mm") + m + 1)
                nc.vector.scalar_tensor_tensor(mixb[:, m, :], bank[2 + m % 2][:, :], -1.0 / RD, kk_a[:, m, :],
                                               ALU.mult, ALU.add).then_inc(sig("centered"), 1)
            dve.wait_ge(sig("centered"), seen("centered") + DT)
            dve.sem_inc(sig("y_read"), 8)
            for m in range(DT):
                dve.wait_ge(sig("bonus_mm"), seen("bonus_mm") + m + 1)
                nc.vector.tensor_tensor(v_a[:, m, :], bank[(0, 1)[m % 2]][:, :], v_a[:, m, :], ALU.mult
                                        ).then_inc(sig("bonus"), 1)
            dve.wait_ge(sig("dev_root"), seen("dev_root") + 1)
            nc.vector.reciprocal(dev_rows, dev_rows).then_inc(sig("gn_recip"), 1)
            for m in range(DT):
                dve.wait_ge(sig("dev_mm"), seen("dev_mm") + DT + m + 1)
                nc.vector.tensor_tensor(mixb[:, m, :], mixb[:, m, :], bank[2 + m % 4][:, :], ALU.mult
                                        ).then_inc(sig("gn_done"), 1)
                dve.wait_ge(sig("gn_done"), seen("gn_done") + m + 1)
                step(nc.vector.tensor_scalar(mixb[:, m, :], mixb[:, m, :], v("lnw")[:, m:m + 1], v("lnb")[:, m:m + 1],
                                             ALU.mult, ALU.add))
                dve.wait_ge(sig("bonus"), seen("bonus") + m + 1)
                step(nc.vector.tensor_tensor(mixb[:, m, :], mixb[:, m, :], v_a[:, m, :], ALU.add))
                dve.wait_ge(sig("g_loaded"), 16)
                nc.vector.tensor_tensor(k_a_[:, m, :], mixb[:, m, :], g_a[:, m, :], ALU.mult).then_inc(sig("gated"), 1)
                if m == 1:
                    weights_low(dve, 0, 0, 0, ffn_wh)
                    weights_low(dve, 0, 0, 1, ffn_wh)
                if m:
                    rhs_lows(k_a_, rhs_hi, 6 * DT + m - 1, (m - 1,))
            rhs_lows(k_a_, rhs_hi, 7 * DT - 1, (DT - 1,))
            add_results(3 * DT)
            norm(3)
            rhs_lows(ht, rhs_hi, 7 * DT)
            gate_ups(1)
            add_down(4 * DT)
            norm(4)

        @block.tensor
        def _(pe):
            pe.wait_ge(sig("con_loaded"), 16)

            def norm_sum(r):
                for k in range(DT):
                    pe.wait_ge(sig("sq_a" if k < 4 else "sq_d"), r + 1)
                    mm = nc.tensor.matmul(bank[2][:, :], c("ones"), ht[:, k, :], start=k == 0, stop=k == DT - 1)
                mm.then_inc(sig("sum_done"), 1)

            norm_sum(0)
            pe.wait_ge(sig("vec_loaded"), 16)
            pe.wait_ge(sig("onehot_loaded"), 16)
            nc.tensor.matmul(bank[3][0:NH, :], v("tbl")[0:33, :], oh[0:33, 0:512], start=True, stop=True)
            nc.tensor.matmul(bank[4][0:NH, 0:128], v("tbl")[0:33, :], oh[0:33, 512:BIAS_LEN],
                             start=True, stop=True).then_inc(sig("row_mm"), 1)
            for _ in range(2):
                with pe.Fori(0, 3) as it:
                    for j in range(4):
                        split_product(pe, it, 4, j, in_hi, in_lo, in_wh)
                pass_units("pe", 12)
            for j in range(2):
                split_product(pe, 0, 0, j, in_hi, in_lo, in_wh)
            pass_units("pe", 2)
            split["pe"][1] += DT
            ws = v("wsmall").rearrange("p (k n) -> p k n", k=DT)
            for t in range(4):
                for k in range(DT):
                    mm = nc.tensor.matmul(bank[2][:, 32 * t:32 * t + 32], ht[:, k, P * t:P * t + P], ws[:, k, :],
                                          start=k == 0, stop=k == DT - 1)
            mm.then_inc(sig("small_done"), 1)
            pe.wait_ge(sig("shifted_loaded"), 16)
            pe.wait_ge(sig("proj_done"), IN_UNITS - 12)
            for i in range(NH):
                if i >= 4:
                    pe.wait_ge(sig("bias_done"), i - 3)
                nc.tensor.matmul(bank[4 + i % 4][:, :], c("flip"), shifted[:, i, :], start=True, stop=True
                                 ).then_inc(sig("bias_mm"), 1)
            pe.wait_ge(sig("blocks_done"), 10)
            pe.wait_ge(sig("tok_done"), 1)
            ring = rings["pe"][0]
            for i in range(8):
                s, u = ring.at(0)
                pe.wait_ge(sig(f"w_full{s}"), 16 * (u + 1))
                for m in range(8):
                    tap = 8 * (i % 2) + m
                    w = wring[:, s, P * m:P * m + P]
                    mm = nc.tensor.matmul(bank[2][:, 64 * (i // 2):64 * (i // 2) + BLK], w, kst[i // 4][:, tap, :],
                                          start=tap == 0, stop=tap == 15)
                mm.then_inc(sig(f"unit_done{s}"), 1)
                ring.advance(1)
            pe.wait_ge(sig("bias_done"), NH)
            pe.wait_ge(sig("hid_done"), 4)
            cw = v("cw2").rearrange("p (i k n) -> p i k n", i=2, k=2)
            for g in range(2):
                for k in range(2):
                    nc.tensor.matmul(bank[4][64 * g:64 * g + 64, 0:NCMP], cw[:, 0, k, :],
                                     hid[:, k, NCMP * g:NCMP * g + NCMP], start=k == 0, stop=k == 1)
            for g in range(2):
                for k in range(2):
                    mm = nc.tensor.matmul(bank[5][0:NCMP, 64 * g:64 * g + 64],
                                          hid[:, 2 + k, NCMP * g:NCMP * g + NCMP], cw[:, 1, k, :],
                                          start=k == 0, stop=k == 1)
            mm.then_inc(sig("cmp_mm"), 1)
            pe.wait_ge(sig("proj_done"), IN_UNITS - 12)
            for i in range(2):
                for t in range(4):
                    mm = nc.tensor.transpose(bank[6 + i][:, P * t:P * t + P], proj[:, 23 + 2 * i, P * t:P * t + P],
                                             c("ident"))
                mm.then_inc(sig("vtok_mm"), 1)
            pe.wait_ge(sig("cmp_done"), 2)
            pe.wait_ge(sig("vtok_done"), 2)
            with pe.Fori(0, 4) as j:
                pe.wait_ge(sig("staged"), 3 * j + 3)

                def score(u):
                    s, qt, br = u // 12, u // 3 % 4, u % 3
                    keys = (proj[:, 22, :], proj[:, 24, :], kcT)[br]
                    pe.wait_ge(sig("scored"), j * 24 + u + 1)
                    nc.tensor.matmul(bank[2 + u % 2][:, 0:width(u)], q_st[64 * s:64 * s + 64, P * qt:P * qt + P],
                                     keys[64 * s:64 * s + 64, 0:width(u)], start=True, stop=True
                                     ).then_inc(sig("score_mm"), 1)

                def turn(u):
                    pe.wait_ge(sig("exp_done"), j * 24 + u + 1)
                    w = width(u)
                    for b in range(-(-w // P)):
                        n = min(P, w - P * b)
                        mm = nc.tensor.transpose(bank[4][0:n, P * b:P * b + P], probs[u % 2][:, P * b:P * b + n],
                                                 c("ident"))
                    mm.then_inc(sig("turned"), 1)

                def weigh(u):
                    s, qt, br = u // 12, u // 3 % 4, u % 3
                    w = width(u)
                    pe.wait_ge(sig("turn_copied"), j * 24 + u + 1)
                    nb = -(-w // P)
                    for b in range(nb):
                        n = min(P, w - P * b)
                        vals = vtok[:, 4 * br + b, 64 * s:64 * s + 64] if br < 2 else vcT[0:n, 64 * s:64 * s + 64]
                        o = (4 * s + qt) * ND
                        mm = nc.tensor.matmul(bank[5 + br][:, o:o + ND], probsT[u % 2][0:n, P * b:P * b + P], vals,
                                              start=b == 0, stop=b == nb - 1)
                    if u == 23:
                        mm.then_inc(sig("pv_mm"), 1)

                score(0)
                score(1)
                pe.wait_ge(sig("pv_read"), j + 1)
                for u in range(24):
                    turn(u)
                    if u < 22:
                        score(u + 2)
                    weigh(u)
            pe.wait_ge(sig("pair_done"), 5)
            for i in range(4):
                for t in range(4):
                    mm = nc.tensor.transpose(bank[2 + i][:, P * t:P * t + P], otok[:, t, P * i:P * i + P], c("ident"))
                mm.then_inc(sig("otok_turned"), 1)

            pe.wait_ge(sig("g_done"), 1)
            nc.tensor.matmul(bank[2][:, 0:16], c("le"), g_col, start=True, stop=True)
            nc.tensor.matmul(bank[2][:, 16:32], c("gt"), g_col, start=True, stop=True).then_inc(sig("g_sum_mm"), 1)
            pe.wait_ge(sig("mix_nsa"), 4)
            def row_sums(b, sq, i, n):
                return nc.tensor.matmul(bank[b][0:n, :], c("tile_in")[:, 7 - i:7 - i + n], sq,
                                        start=i == 0, stop=i == n - 1)

            def spread_row(b, rows, i, n):
                return nc.tensor.matmul(bank[b][:, :], tile_out[0:n, P * i:P * i + P], rows,
                                        start=True, stop=True)

            for i in range(8):
                pe.wait_ge(sig("qk_sq"), 1 + i // 4)
                mm = row_sums(4, rn0[:, i, :], i, 8)
            mm.then_inc(sig("qk_sum"), 1)
            pe.wait_ge(sig("qk_recip"), 1)
            pe.wait_ge(sig("st_zero"), 2)
            for i in range(8):
                if i >= 4:
                    pe.wait_ge(sig("qk_normed"), i - 3)
                spread_row(4 + i % 4, rn0[0:8, 0, :], i, 8).then_inc(sig("qk_sum"), 1)
            pe.wait_ge(sig("qk_normed"), 8)
            pe.wait_ge(sig("eg_done"), 1)
            pe.wait_ge(sig("st_zero"), 2)
            with pe.Fori(0, NCHUNK) as n:
                def four(b, lhs, rhs, s, first=True, last=True):
                    for i in range(GH):
                        mm = nc.tensor.matmul(bank[b][:, P * i:P * i + P], lhs(i), rhs(i), start=first, stop=last)
                    mm.then_inc(sig(s), 1)

                pe.wait_ge(sig("chunk_staged"), 3 * n + 3)
                four(5, lambda i: k_st[:, i, :], lambda i: k_st[:, i, :], "kk_mm")
                four(6, lambda i: k_st[:, i, :], lambda i: qst[:, i, :], "qk_mm")
                for i in range(GH):
                    mm = nc.tensor.transpose(bank[7][:, P * i:P * i + P], k_st[:, i, :], c("ident"))
                mm.then_inc(sig("ktok_mm"), 1)
                pe.wait_ge(sig("g_spread"), 3 * n + 3)
                pe.wait_ge(sig("o_copied"), n + 1)
                four(2, lambda i: gbc[:, i, :], lambda i: c("le"), "decay_mm")
                nc.tensor.matmul(bank[3][:, :], c("le"), gtg_flat, start=True, stop=True).then_inc(sig("decay_mm"), 1)
                nc.tensor.matmul(bank[4][:, :], c("gt"), leg_flat, start=True, stop=True).then_inc(sig("decay_mm"), 1)
                pe.wait_ge(sig("decay_row"), n + 1)
                for i in range(GH):
                    mm = nc.tensor.transpose(bank[2][:, P * i:P * i + P], v_st[:, i, :], c("ident"))
                mm.then_inc(sig("vtok2_mm"), 1)
                pe.wait_ge(sig("qk_done"), n + 1)
                four(6, lambda i: k_st[:, i, :], lambda i: st[:, i, :], "ks_mm")
                pe.wait_ge(sig("m_done"), n + 1)
                pe.wait_ge(sig("x_init"), 2 * n + 2)
                pe.wait_ge(sig("decay_low"), n + 1)
                pe.wait_ge(sig("decay_up"), n + 1)
                for lv in range(7):
                    if lv:
                        pe.wait_ge(sig("x_step"), n * 13 + 2 * lv)
                    four(3, lambda i: mlow[:, i, :], lambda i: xit[:, i, :], "qt_mm")
                    pe.wait_ge(sig("qt_done"), n * 7 + lv + 1)
                    if lv < 6:
                        for i in range(GH):
                            nc.tensor.matmul(bank[4][:, P * i:P * i + P], qt_[:, i, :], xi[:, i, :], start=True, stop=True)
                    four(5, lambda i: xi[:, i, :], lambda i: qt_[:, i, :], "xx_mm")
                pe.wait_ge(sig("x_step"), n * 13 + 13)
                pe.wait_ge(sig("rhs_done"), n + 1)
                pe.wait_ge(sig("ktok_done"), n + 1)
                four(7, lambda i: xit[:, i, :], lambda i: rr[:, i, :], "vnew_mm")
                pe.wait_ge(sig("q_decayed"), n + 1)
                pe.wait_ge(sig("vnew_done"), n + 1)
                pe.wait_ge(sig("vb_done"), n + 1)
                for i in range(GH):
                    nc.tensor.matmul(bank[2][:, P * i:P * i + P], st[:, i, :], qst[:, i, :], start=True, stop=False)
                    mm = nc.tensor.matmul(bank[2][:, P * i:P * i + P], vn[:, i, :], qk[:, i, :], start=False, stop=True)
                mm.then_inc(sig("o_mm"), 1)
                pe.wait_ge(sig("k_decayed"), n + 1)
                four(3, lambda i: ktok[:, i, :], lambda i: vn[:, i, :], "st_mm")
            pe.wait_ge(sig("o_sq"), 1)
            for i in range(4):
                mm = row_sums(4, rn0[:, i, :], i, 4)
            mm.then_inc(sig("o_sum"), 1)
            pe.wait_ge(sig("o_step"), 1)
            pe.wait_ge(sig("chunk_done"), NCHUNK + 1)
            for i in range(4):
                spread_row((5, 6, 7, 3)[i], rn0[0:4, 4, :], i, 4).then_inc(sig("o_sum"), 1)
            with pe.Fori(0, DT // 4) as it:
                for j in range(4):
                    split_product(pe, it, 4, j, rhs_hi, ht, ffn_wh, (4, 5, 6, 7, 0, 1, 2, 3))
            pass_units("pe", DT)
            split["pe"][1] += DT

            def gate_ups():
                with pe.Fori(0, FT // 2) as it:
                    for j in range(4):
                        split_product(pe, it, 4, j, rhs_hi, ht, ffn_wh)
                pass_units("pe", 2 * FT)
                split["pe"][1] += DT

            def downs(gate):
                with pe.Fori(0, 2) as it:
                    for j in range(4):
                        down_product(pe, it, 4, j, gate)
                skip("pe", 0, DT)
                split["pe"][2] += 3 * DT

            norm_sum(1)
            gate_ups()
            downs(0)
            norm_sum(2)

            ring, _, banks = rings["pe"]

            def free_bank():
                b, w = banks.at(0)
                pe.wait_ge(sig(f"bank_free{PB[b]}"), w + 1)
                banks.advance(1)
                return PB[b]

            done = {}

            def bump(s):
                done[s] = done.get(s, 0) + 1
                return sig(s)

            def lora_out(parts):
                for m in range(DT):
                    b = free_bank()
                    for i, (w, rhs) in enumerate(parts):
                        mm = nc.tensor.matmul(bank[b][:, :], w[:, P * m:P * m + P], rhs, start=i == 0,
                                              stop=i == len(parts) - 1)
                    mm.then_inc(bump("lora_mm"), 1)

            for _ in range(2):
                k8_product(pe, 0, 0, 0, mixa, ("mixed", 0))
                skip("pe", 1)
            pe.wait_ge(sig("mixed"), DT)
            (s2, c2), (s3, c3) = ring.at(0), ring.at(1)
            pe.wait_ge(sig(f"w_full{s2}"), 16 * (c2 + 1))
            pe.wait_ge(sig(f"w_full{s3}"), 16 * (c3 + 1))
            pe.wait_ge(sig("hid_g"), 2)
            lora_out(((wring[:, s2, :], hid_g1), (wring[0:32, s3, :], hid_g2[0:32, :])))
            pe.wait_ge(sig("lora_mm"), seen("lora_mm") + DT)
            pe.sem_inc(sig(f"unit_done{s2}"), 1)
            pe.sem_inc(sig(f"unit_done{s3}"), 1)
            pe.sem_inc(sig("mix_used"), 1)
            ring.advance(2)
            (s4, c4), (s5, c5) = ring.at(0), ring.at(1)
            pe.wait_ge(sig(f"w_full{s4}"), 16 * (c4 + 1))
            pe.wait_ge(sig(f"w_full{s5}"), 16 * (c5 + 1))
            for i, mx in enumerate((mixb, mixa)):
                b = free_bank()
                for k in range(DT):
                    pe.wait_ge(sig("mixed"), DT * (i + 1) + k + 1)
                    mm = nc.tensor.matmul(bank[b][64 * i:64 * i + 64, :], wring[:, s4, P * k + 64 * i:P * k + 64 * i + 64],
                                          mx[:, k, :], start=k == 0, stop=k == DT - 1)
                mm.then_inc(sig("wa_mm"), 1)
                pe.wait_ge(sig("hid_wa"), i + 1)
                pe.sem_inc(sig("mix_used"), 1)
                lora_out(((wring[64 * i:64 * i + 64, s5, :], hid_wa[64 * i:64 * i + 64, :]),))
            pe.wait_ge(sig("lora_mm"), seen("lora_mm") + 3 * DT)
            pe.sem_inc(sig(f"unit_done{s4}"), 1)
            pe.sem_inc(sig(f"unit_done{s5}"), 1)
            ring.advance(2)
            for high, mx in ((v_hi, mixb), (r_hi, mixa)):
                with pe.Fori(0, 2) as it:
                    for j in range(4):
                        split_product(pe, it, 4, j, high, mx, rwkv_wh)
                pass_units("pe", DT)
                split["pe"][1] += DT
                s, u = ring.at(3)
                pe.wait_ge(sig(f"unit_done{s}"), u)
                pe.sem_inc(sig("mix_used"), 1)
            def head_sums(b, sq, m):
                return nc.tensor.matmul(bank[b][0:16, :], c("head_in")[:, 14 - 2 * m:30 - 2 * m], sq[:, m, :],
                                        start=m == 0, stop=m == DT - 1)

            def spread_heads(b, rows, m):
                return nc.tensor.matmul(bank[b][:, :], head_out[:, P * m:P * m + P], rows, start=True, stop=True)

            for m in range(DT):
                split_product(pe, 0, 0, 0, ht, mixb, rwkv_wh)
                pass_units("pe", 1)
                if m:
                    pe.wait_ge(sig("k_out"), seen("k_out") + 2 * m)
                    head_sums(2, kn, m - 1).then_inc(sig("ksum_mm"), 1)
            split["pe"][1] += DT
            pe.wait_ge(sig("k_out"), seen("k_out") + 2 * DT)
            head_sums(2, kn, DT - 1).then_inc(sig("ksum_mm"), 1)
            pe.wait_ge(sig("k_recip"), seen("k_recip") + 1)
            for m in range(DT):
                if m > 3:
                    pe.wait_ge(sig("kn_done"), seen("kn_done") + m - 3)
                spread_heads(2 + m % 4, key_rows, m).then_inc(sig("ksum_mm"), 1)

            pe.wait_ge(sig("pc_done"), 1)
            pe.wait_ge(sig("kn_done"), seen("kn_done") + DT)
            def tiles(b, parts, s=None, lo=0, hi=DT, w=RD, start=None, stop=None):
                for m in range(lo, hi):
                    o = (m - lo) * w
                    for i, (lhs, rhs) in enumerate(parts):
                        if start is None:
                            mm = nc.tensor.matmul(bank[b][:, o:o + w], lhs[:, m, :], rhs(m), start=i == 0,
                                                  stop=i == len(parts) - 1)
                        else:
                            mm = nc.tensor.matmul(bank[b][:, o:o + w], lhs[:, m, :], rhs(m),
                                                  start=start and m == lo and i == 0, stop=stop,
                                                  skip_group_check=True)
                if s:
                    mm.then_inc(sig(s), 1)

            def stacked(a):
                return lambda m: a[:, m, :]

            def chunk(n):
                pe.wait_ge(sig("bda"), seen("bda") + 2 * n + 2)
                pe.wait_ge(sig("rhs_staged"), 7 * n + 7)
                tiles(0, ((bdA, stacked(b_c)),), "m_mm")
                tiles(1, ((bdK, stacked(ar_c)),), None, 0, 4, P)
                tiles(2, ((bdK, stacked(ar_c)),), "k_mm", 4, 8, P)
                pe.wait_ge(sig("bdb"), seen("bdb") + 2 * n + 2)
                tiles(4, ((bdB, lambda m: c("id64")),), "bt_mm")
                tiles(5, ((bdK, lambda m: c("id64")),), "kt_mm")
                pe.wait_ge(sig("y_out"), seen("y_out") + n)
                tiles(3, ((bdB, lambda m: ar_c[:, m, RD:]),), "rb_mm")
                pe.wait_ge(sig("z_out"), seen("z_out") + 2 * n)
                tiles(6, ((bdV, lambda m: c("id64")),), "vt_mm")
                pe.wait_ge(sig("m_out"), 6 * n + 6)
                pe.wait_ge(sig("ak_out"), 6 * n + 6)
                pe.wait_ge(sig("rb_out"), 2 * n + 2)
                pe.wait_ge(sig("tok_out"), seen("tok_out") + 7 * n + 4)
                for lv in range(6):
                    if lv == 5:
                        pe.wait_ge(sig("tok_out"), seen("tok_out") + 7 * n + 7)
                        tiles(1, ((bdA, stacked(z_c)), (bdAK, stacked(vt_c))), "g_mm")
                    for g in range(2):
                        if lv:
                            pe.wait_ge(sig("xt_sub"), seen("xt_sub") + n * 12 + 2 * (lv - 1) + g + 1)
                        tiles((7, 0)[g], ((bdM, stacked(xt_c)),), "q_mm", 4 * g, 4 * g + 4)
                    for g in range(2):
                        pe.wait_ge(sig("q_out"), n * 12 + 2 * lv + g + 1)
                        if lv:
                            pe.wait_ge(sig("bdx"), n * 20 + 4 * (lv - 1) + 2 * g + 2)
                        tiles(4 + g, ((bdX, stacked(q_c)),), "xtm", 4 * g, 4 * g + 4)
                        if lv < 5:
                            pe.wait_ge(sig("bdq"), seen("bdq") + n * 20 + 4 * lv + 2 * g + 2)
                            tiles(2 + g, ((bdQ, stacked(x_c)),), "xmm", 4 * g, 4 * g + 4)
                pe.wait_ge(sig("x_sub"), seen("x_sub") + n * 10 + 10)
                pe.wait_ge(sig("bdz"), seen("bdz") + 2 * n)
                tiles(6, ((bdKt, stacked(vt_c)),), None, start=True, stop=False)
                tiles(3, ((bdZ, stacked(ry_c)), (bdVt, stacked(rk_c))), None, start=True, stop=False)
                pe.wait_ge(sig("bdxt"), seen("bdxt") + 2 * n + 2)
                pe.wait_ge(sig("g_out"), seen("g_out") + n + 1)
                tiles(7, ((bdXT, stacked(g_c)),), "u_mm")
                pe.wait_ge(sig("u_out"), n + 1)
                tiles(6, ((bdBt, stacked(u_c)),), "z_mm", start=False, stop=True)
                pe.wait_ge(sig("bdu"), seen("bdu") + 2 * n + 2)
                tiles(3, ((bdU, stacked(rb_c)),), "y_mm", start=False, stop=True)

            pe.wait_ge(sig("bd_zero"), 14)
            with pe.Fori(0, SEQ // RD - 1) as n:
                chunk(n)
            chunk(SEQ // RD - 1)
            pe.wait_ge(sig("y_out"), seen("y_out") + SEQ // RD)
            for m in range(DT):
                if m > 1:
                    pe.wait_ge(sig("centered"), seen("centered") + m - 1)
                nc.tensor.matmul(bank[2 + m % 2][:, :], c("blk"), kk_a[:, m, :], start=True, stop=True
                                 ).then_inc(sig("mean_mm"), 1)
            for m in range(DT):
                pe.wait_ge(sig("dev_sq"), seen("dev_sq") + m + 1)
                head_sums(4, ht, m).then_inc(sig("dev_mm"), 1)
                pe.wait_ge(sig("rk_done"), seen("rk_done") + m + 1)
                if m > 1:
                    pe.wait_ge(sig("bonus"), seen("bonus") + m - 1)
                nc.tensor.matmul(bank[(0, 1)[m % 2]][:, :], c("blk"), r_a[:, m, :], start=True, stop=True
                                 ).then_inc(sig("bonus_mm"), 1)
            pe.wait_ge(sig("gn_recip"), seen("gn_recip") + 1)
            for m in range(DT):
                if m > 3:
                    pe.wait_ge(sig("gn_done"), seen("gn_done") + m - 3)
                spread_heads(2 + m % 4, dev_rows, m).then_inc(sig("dev_mm"), 1)
            with pe.Fori(0, DT // 4) as it:
                for j in range(4):
                    split_product(pe, it, 4, j, rhs_hi, k_a_, ffn_wh)
            pass_units("pe", DT)
            split["pe"][1] += DT
            norm_sum(3)
            gate_ups()
            downs(FT)
            norm_sum(4)


def constants():
    import numpy as np
    p, q = np.arange(P)[:, None], np.arange(P)[None, :]
    r = np.arange(RD)[None, :]
    a = np.zeros((P, NCONST), np.float32)

    def put(name, value):
        o, w = COLS[name]
        a[:, o:o + w] = value

    put("ident", p == q)
    put("flip", p + q == P - 1)
    put("le", p <= q)
    put("gt", p > q)
    put("ones", 1.0)
    put("blk", p // RD == q // RD)
    put("lvl", np.concatenate([(p // b % 2 == 0) & (q // b == p // b + 1) for b in (1, 2, 4, 8, 16, 32, 64)], 1))
    pr = p % RD
    put("lvl64", np.concatenate([(pr // b % 2 == 0) & (r // b == pr // b + 1) for b in (1, 2, 4, 8, 16, 32)], 1))
    put("le64", pr <= r)
    put("lt64", pr < r)
    put("gt64", pr > r)
    put("id64", pr == r)
    put("tile_in", np.arange(15)[None, :] == 7)
    put("head_in", np.arange(30)[None, :] == 14 + p // RD)
    put("eps", np.array([[EPS, 1e-12, 64e-5, GD * EPS]], np.float32))
    dist = 511 - np.arange(BIAS_LEN)
    n = np.maximum(dist, 0)
    large = 16 + (np.log(np.maximum(n, 1).astype(np.float32) / np.float32(16)) / np.float32(np.log(128 / 16))
                  * np.float32(16)).astype(np.int32)
    bucket = np.where(n < 16, n, np.minimum(large, 31))
    onehot = np.zeros((33, BIAS_LEN), np.float32)
    onehot[bucket, np.arange(BIAS_LEN)] = dist >= 0
    onehot[32] = dist < 0
    return a, onehot


def kernel(**inputs):
    import numpy as np
    import concourse.bacc as bacc
    from concourse.bass_utils import run_bass_kernel_spmd

    i = {k: np.asarray(v) for k, v in inputs.items()}

    def columns(a):
        return np.ascontiguousarray(a.reshape(-1, P).T)

    def units(w):
        k, n = w.shape
        return w.reshape(k // P, P, n // P, P).transpose(2, 1, 0, 3).reshape(n // P, P, k)

    cpack, onehot = constants()
    w_in = i["e_w_in"][0]
    cut = np.cumsum([0] + [512] * 4 + [4] * 2 + [512] + [128] * 6 + [24])
    part = [w_in[:, a:b] for a, b in zip(cut[:-1], cut[1:])]
    nq = part[6].reshape(D_MODEL, 2, 4, ND).transpose(0, 2, 1, 3).reshape(D_MODEL, 512)
    w_in_units = units(np.concatenate(part[0:4] + [nq] + part[7:13], 1))
    gate = part[13].reshape(D_MODEL, NH, 3)[:, :, [1, 2, 0]].reshape(D_MODEL, 24)
    small = np.concatenate([part[4], part[5], gate], 1)

    def compress(w):
        w = w.reshape(2, 8, P, 2, P)
        return w.transpose(3, 0, 2, 1, 4).reshape(4, P, UNIT)

    def pad_unit(w, rows=P):
        out = np.zeros((1, P, UNIT), np.float32)
        out[0, :w.shape[0], :w.shape[1]] = w
        return out

    def interleave(a, b):
        return np.stack([a, b], 1).reshape(-1, P, UNIT)

    def k_major(w):
        out = np.zeros((P, DT, P), np.float32)
        out[:, :, :w.shape[1]] = w.reshape(DT, P, -1).transpose(1, 0, 2)
        return out.reshape(1, P, UNIT)

    g1 = i["o_g1"][0]
    wk8 = np.concatenate([
        w_in_units, compress(i["e_cmpk_w1"][0]), compress(i["e_cmpv_w1"][0]), units(i["e_w_out"][0]),
        interleave(units(i["e_ffn_gate"][0]), units(i["e_ffn_up"][0])),
        k_major(g1[:, 0:128]), k_major(g1[:, 128:160]), pad_unit(i["o_g2"][0][0:128]), pad_unit(i["o_g2"][0][128:160]),
        k_major(np.concatenate([i["o_w1"][0], i["o_a1"][0]], 1)),
        pad_unit(np.concatenate([i["o_w2"][0], i["o_a2"][0]], 0)),
        units(i["o_w_v"][0]), units(i["o_w_r"][0]), units(i["o_w_k"][0]), units(i["o_w_o"][0]),
        interleave(units(i["o_ffn_gate"][0]), units(i["o_ffn_up"][0]))], 0)
    wdn = np.concatenate([units(i["e_ffn_down"][0]), units(i["o_ffn_down"][0])], 0)

    tbl = np.zeros((P, NH), np.float32)
    tbl[0:32] = i["rel_bias"]
    tbl[32] = NEG
    vals = {
        "n0": columns(i["e_attn_norm"][0]), "n1": columns(i["e_ffn_norm"][0]), "n2": columns(i["o_attn_norm"][0]),
        "n3": columns(i["o_ffn_norm"][0]), "n4": columns(i["final_norm"]), "mu": columns(i["o_mu"][0]),
        "w0": columns(i["o_w0"][0]), "a0": columns(i["o_a0"][0]), "k_k": columns(i["o_k_k"][0]),
        "k_a": columns(i["o_k_a"][0]), "r_k": columns(i["o_r_k"][0].reshape(-1)), "lnw": columns(i["o_lnx_w"][0]),
        "lnb": columns(i["o_lnx_b"][0]),
        "conv": i["e_conv_w"][0].reshape(4, 12, P).transpose(2, 1, 0).reshape(P, 48),
        "gnorm": columns(i["e_gdn_norm"][0]), "alog": np.tile(i["e_a_log"][0], (P, 1)),
        "dtb": np.tile(i["e_dt_bias"][0], (P, 1)),
        "wsmall": small.reshape(DT, P, 32).transpose(1, 0, 2).reshape(P, 256),
        "cw2": np.stack([i[f"e_cmp{t}_w2"][0].reshape(2, P, ND) for t in "kv"]).transpose(2, 0, 1, 3).reshape(P, 256),
        "pe": np.stack([i[f"e_cmp{t}_pe"][0].reshape(16, P) for t in "kv"]).transpose(2, 0, 1).reshape(P, 32),
        "tbl": tbl}
    vpack = np.concatenate([vals[k].reshape(P, -1) for k in VCOLS], 1)
    assert vpack.shape[1] == NVEC
    xT = i["x"][0].T.reshape(DT, P, SEQ).transpose(1, 0, 2)

    nc = bacc.Bacc("TRN2", target_bir_lowering=False, num_devices=1)
    feeds = {"xT": xT, "cpack": cpack, "vpack": vpack, "onehot": onehot, "wk8": wk8, "wdn": wdn}
    feeds = {k: np.ascontiguousarray(a) for k, a in feeds.items()}
    aps = {k: nc.dram_tensor(k, a.shape, F32, kind="ExternalInput").ap() for k, a in feeds.items()}
    aps["scratch"] = nc.dram_tensor("scratch", (NH, BIAS_LEN), F32, kind="Internal").ap()
    aps["g_spill"] = nc.dram_tensor("g_spill", (P, DT, SEQ), F32, kind="Internal").ap()
    aps["outT"] = nc.dram_tensor("outT", (P, DT, SEQ), F32, kind="ExternalOutput").ap()
    build(nc, **aps)
    r = run_bass_kernel_spmd(nc, [feeds], core_ids=[0])
    return np.ascontiguousarray(r.results[0]["outT"].transpose(2, 1, 0)).reshape(1, SEQ, D_MODEL)
```
